# Optimizing a Trainium2 kernel written in Bass

```python
import jax, jax.numpy as jnp
from jax import lax
import numpy as np
import math
import jax
import jax.numpy as jnp

D_MODEL = 1024
BATCH = 1
SEQ = 512
DEPTH = 1

CHUNK = 64
Q_BLOCK = 128
CONV_DIM = D_MODEL // 2
CONV_WIDTH = 3
N_HEADS = 8
NOPE_DIM = 64
ROPE_DIM = 32
V_DIM = 64
Q_LORA = 384
KV_LORA = 256
ROPE_THETA = 10000.0
D_FF = 2816
PLE_DIM = 256
EPS = 1e-6

QK_DIM = NOPE_DIM + ROPE_DIM
SPLIT_SIZES = (CONV_DIM, CONV_DIM, CONV_DIM, Q_LORA, KV_LORA, ROPE_DIM, D_MODEL, D_MODEL)
N_IN = CONV_DIM * 3 + Q_LORA + KV_LORA + ROPE_DIM + 2 * D_MODEL


def _rmsnorm(x, g):
    xf = x.astype(jnp.float32)
    y = xf * lax.rsqrt(jnp.mean(xf * xf, axis=-1, keepdims=True) + EPS)
    return (y * g.astype(jnp.float32)).astype(x.dtype)

def _causal_dwconv3(x, w):
    s = x.shape[1]
    xp = jnp.pad(x, ((0, 0), (CONV_WIDTH - 1, 0), (0, 0)))
    return xp[:, 0:s] * w[0] + xp[:, 1:s + 1] * w[1] + xp[:, 2:s + 2] * w[2]

def _rope(x, positions):
    half = ROPE_DIM // 2
    inv = 1.0 / (ROPE_THETA ** (jnp.arange(half, dtype=jnp.float32) * (2.0 / ROPE_DIM)))
    ang = positions.astype(jnp.float32)[..., None] * inv
    cos = jnp.cos(ang)[:, :, None, :]
    sin = jnp.sin(ang)[:, :, None, :]
    xf = x.astype(jnp.float32)
    x1, x2 = xf[..., :half], xf[..., half:]
    return jnp.concatenate([x1 * cos - x2 * sin, x2 * cos + x1 * sin], axis=-1).astype(x.dtype)

def _chunk_causal_attention(q, k, v):
    bsz, s, h, dqk = q.shape
    nblk = s // Q_BLOCK
    scale = dqk ** -0.5
    k_chunk = jnp.arange(s) // CHUNK
    qb = q.reshape(bsz, nblk, Q_BLOCK, h, dqk).transpose(1, 0, 2, 3, 4)
    kf = k.astype(jnp.float32)
    vf = v.astype(jnp.float32)
    neg = jnp.finfo(jnp.float32).min

    def one_block(args):
        qi, bi = args
        q_chunk = (bi * Q_BLOCK + jnp.arange(Q_BLOCK)) // CHUNK
        mask = k_chunk[None, :] <= q_chunk[:, None]
        sc = jnp.einsum('bqhd,bkhd->bhqk', qi.astype(jnp.float32), kf) * scale
        sc = jnp.where(mask[None, None], sc, neg)
        pr = jax.nn.softmax(sc, axis=-1)
        return jnp.einsum('bhqk,bkhd->bqhd', pr, vf)

    out = lax.map(one_block, (qb, jnp.arange(nblk)))
    return out.transpose(1, 0, 2, 3, 4).reshape(bsz, s, h, v.shape[-1]).astype(v.dtype)

def first_inputs(seed: int = 0) -> dict:
    key = jax.random.key(seed)
    ks = jax.random.split(key, 32)
    L = DEPTH
    f32 = jnp.float32

    def w(k, shape, fan_in):
        return jax.random.normal(k, shape, f32) * (fan_in ** -0.5)

    def gain(k, shape):
        return 1.0 + 0.05 * jax.random.normal(k, shape, f32)

    x = jax.random.normal(ks[0], (BATCH, SEQ, D_MODEL), f32)
    p = jax.random.normal(ks[1], (DEPTH, BATCH, SEQ, PLE_DIM), f32)
    offset = jax.random.randint(ks[2], (BATCH, 1), 0, 4096, dtype=jnp.int32)
    positions = offset + jnp.arange(SEQ, dtype=jnp.int32)[None, :]
    return {
        "x": x,
        "p": p,
        "positions": positions,
        "g_mix_pre": gain(ks[3], (L, D_MODEL)),
        "w_in": w(ks[4], (L, D_MODEL, N_IN), D_MODEL),
        "conv_a_w": w(ks[5], (L, CONV_WIDTH, CONV_DIM), CONV_WIDTH),
        "w_a_out": w(ks[6], (L, CONV_DIM, D_MODEL), CONV_DIM),
        "g_q_lat": gain(ks[7], (L, Q_LORA)),
        "w_q_up": w(ks[8], (L, Q_LORA, N_HEADS * QK_DIM), Q_LORA),
        "g_kv_lat": gain(ks[9], (L, KV_LORA)),
        "w_kv_up": w(ks[10], (L, KV_LORA, N_HEADS * (NOPE_DIM + V_DIM)), KV_LORA),
        "w_b_out": w(ks[11], (L, N_HEADS * V_DIM, D_MODEL), N_HEADS * V_DIM),
        "w_o": w(ks[12], (L, D_MODEL, D_MODEL), D_MODEL),
        "g_mix_post": gain(ks[13], (L, D_MODEL)),
        "g_ffn_pre": gain(ks[14], (L, D_MODEL)),
        "w_ffn_up": w(ks[15], (L, D_MODEL, 2 * D_FF), D_MODEL),
        "conv_ffn_w": w(ks[16], (L, CONV_WIDTH, 2 * D_FF), CONV_WIDTH),
        "b_ffn_conv": 0.01 * jax.random.normal(ks[17], (L, 2 * D_FF), f32),
        "w_ffn_down": w(ks[18], (L, D_FF, D_MODEL), D_FF),
        "g_ffn_post": gain(ks[19], (L, D_MODEL)),
        "w_ple_proj": w(ks[20], (L, PLE_DIM, D_MODEL), PLE_DIM),
        "w_ple_gate": w(ks[21], (L, D_MODEL, D_MODEL), D_MODEL),
        "g_ple_post": gain(ks[22], (L, D_MODEL)),
    }

def first_block(x, p, positions, g_mix_pre, w_in, conv_a_w, w_a_out, g_q_lat, w_q_up,
              g_kv_lat, w_kv_up, w_b_out, w_o, g_mix_post, g_ffn_pre, w_ffn_up,
              conv_ffn_w, b_ffn_conv, w_ffn_down, g_ffn_post, w_ple_proj, w_ple_gate,
              g_ple_post):
    bsz, s, _ = x.shape
    split_pts = list(np.cumsum(SPLIT_SIZES)[:-1])
    h = x
    for i in range(DEPTH):
        u = _rmsnorm(h, g_mix_pre[i])
        z = u @ w_in[i]
        a_b, a_c, a_x, q_lat, kv_lat, k_rope, gate_a, gate_b = jnp.split(z, split_pts, axis=-1)

        ya = a_b * _causal_dwconv3(a_c * a_x, conv_a_w[i])
        ya = ya @ w_a_out[i]

        q = (_rmsnorm(q_lat, g_q_lat[i]) @ w_q_up[i]).reshape(bsz, s, N_HEADS, QK_DIM)
        kv = (_rmsnorm(kv_lat, g_kv_lat[i]) @ w_kv_up[i]).reshape(bsz, s, N_HEADS, NOPE_DIM + V_DIM)
        q_nope, q_pe = q[..., :NOPE_DIM], q[..., NOPE_DIM:]
        k_nope, v = kv[..., :NOPE_DIM], kv[..., NOPE_DIM:]
        q_pe = _rope(q_pe, positions)
        k_pe = _rope(k_rope[:, :, None, :], positions)
        q_full = jnp.concatenate([q_nope, q_pe], axis=-1)
        k_full = jnp.concatenate(
            [k_nope, jnp.broadcast_to(k_pe, (bsz, s, N_HEADS, ROPE_DIM))], axis=-1)
        ob = _chunk_causal_attention(q_full, k_full, v).reshape(bsz, s, N_HEADS * V_DIM)
        yb = ob @ w_b_out[i]

        mixed = jax.nn.sigmoid(gate_a) * ya + jax.nn.sigmoid(gate_b) * yb
        h = h + _rmsnorm(mixed @ w_o[i], g_mix_post[i])

        u2 = _rmsnorm(h, g_ffn_pre[i])
        up = _causal_dwconv3(u2 @ w_ffn_up[i], conv_ffn_w[i]) + b_ffn_conv[i]
        f_gate, f_val = up[..., :D_FF], up[..., D_FF:]
        f = (jax.nn.gelu(f_gate, approximate=True) * f_val) @ w_ffn_down[i]
        h = h + _rmsnorm(f, g_ffn_post[i])

        e = p[i] @ w_ple_proj[i]
        g = jax.nn.sigmoid(h @ w_ple_gate[i])
        h = h + _rmsnorm(e * g, g_ple_post[i])
    return h


DEPTH_2 = 2

N_A_LAYERS = DEPTH_2 // 2
N_B_LAYERS = DEPTH_2 - N_A_LAYERS
MEM_LEN = 256
MEM_HEADS = 4
MEM_HEAD_DIM = 64
MEM_W = MEM_HEADS * MEM_HEAD_DIM
MIX_W = D_MODEL
MAIN_W = MIX_W - MEM_W
GLA_HEADS = 4
GLA_DV = MAIN_W // GLA_HEADS
GLA_DK = GLA_DV // 2
GLA_RANK = 16
GLA_GATE_NORM = 16.0
GLA_CHUNK = 16
NSA_HEADS = 12
NSA_GROUPS = 4
NSA_HEAD_DIM = MAIN_W // NSA_HEADS
NSA_REP = NSA_HEADS // NSA_GROUPS
CMP_BLOCK = 32
CMP_STRIDE = 16
CMP_HIDDEN = 128
SEL_BLOCK = 64
SEL_TOPK = 16
WINDOW = 512
Q_BLOCK_2 = 64
REL_BUCKETS = 32
REL_MAX_DIST = 128
FFN_DIM = 2816
GLA_SIZES = (GLA_HEADS * GLA_DK, GLA_HEADS * GLA_DK, GLA_HEADS * GLA_DV, GLA_HEADS * GLA_DV, GLA_RANK, MEM_W)
GLA_IN = sum(GLA_SIZES)
NSA_SIZES = (NSA_HEADS * NSA_HEAD_DIM, NSA_HEADS * 3, MEM_W)
NSA_IN = sum(NSA_SIZES)
SHARED_KV_W = 6 * NSA_GROUPS * NSA_HEAD_DIM


def rmsnorm(x, g):
    xf = x.astype(jnp.float32)
    y = xf * lax.rsqrt(jnp.mean(xf * xf, axis=-1, keepdims=True) + EPS)
    return (y * g.astype(jnp.float32)).astype(x.dtype)

def split_cols(x, sizes):
    out = []
    start = 0
    for n in sizes:
        out.append(x[..., start:start + n])
        start += n
    return out

def rel_bucket(dist):
    dist = jnp.maximum(dist, 0)
    max_exact = REL_BUCKETS // 2
    large = max_exact + (jnp.log(jnp.maximum(dist, 1).astype(jnp.float32) / max_exact)
                         / math.log(REL_MAX_DIST / max_exact) * (REL_BUCKETS - max_exact)).astype(jnp.int32)
    large = jnp.minimum(large, REL_BUCKETS - 1)
    return jnp.where(dist < max_exact, dist, large)

def masked_softmax(s, mask):
    s = jnp.where(mask, s.astype(jnp.float32), -1e30)
    m = jnp.max(s, axis=-1, keepdims=True)
    p = jnp.where(mask, jnp.exp(s - m), 0.0)
    return p / jnp.maximum(jnp.sum(p, axis=-1, keepdims=True), 1e-30)

def gla_mixer(q, k, v, log_a, g_out, out_norm):
    dtype = v.dtype
    B, S = q.shape[0], q.shape[1]
    C = GLA_CHUNK
    N = S // C

    def chunked(t):
        return t.reshape(B, N, C, GLA_HEADS, t.shape[-1]).transpose(0, 3, 1, 2, 4).astype(jnp.float32)

    qc = chunked(q) * GLA_DK ** -0.5
    kc = chunked(k)
    vc = chunked(v)
    b = lax.cumsum(chunked(log_a), axis=3)
    causal = jnp.tril(jnp.ones((C, C), dtype=bool))
    diff = b[..., :, None, :] - b[..., None, :, :]
    decay = jnp.exp(jnp.where(causal[:, :, None], diff, -jnp.inf))
    attn = jnp.einsum('bhnid,bhnjd,bhnijd->bhnij', qc, kc, decay)
    o_intra = jnp.einsum('bhnij,bhnjv->bhniv', attn, vc)
    b_last = b[..., -1:, :]
    q_in = qc * jnp.exp(b)
    k_out = kc * jnp.exp(b_last - b)
    a_last = jnp.exp(b_last[..., 0, :])

    def step(state, inp):
        qi, ki, vi, ai = inp
        o = jnp.einsum('bhcd,bhdv->bhcv', qi, state)
        state = ai[..., None] * state + jnp.einsum('bhcd,bhcv->bhdv', ki, vi)
        return state, o

    xs = (jnp.moveaxis(q_in, 2, 0), jnp.moveaxis(k_out, 2, 0), jnp.moveaxis(vc, 2, 0), jnp.moveaxis(a_last, 2, 0))
    state0 = jnp.zeros((B, GLA_HEADS, GLA_DK, GLA_DV), jnp.float32)
    _, o_inter = lax.scan(step, state0, xs)
    o = o_intra + jnp.moveaxis(o_inter, 0, 2)
    o = o.transpose(0, 2, 3, 1, 4).reshape(B, S, GLA_HEADS, GLA_DV)
    o = rmsnorm(o, out_norm) * jax.nn.silu(g_out.astype(jnp.float32))
    return o.reshape(B, S, GLA_HEADS * GLA_DV).astype(dtype)

def mem_attention(q, mem_kv):
    B, S = q.shape[0], q.shape[1]
    M = mem_kv.shape[1]
    k, v = split_cols(mem_kv, (MEM_W, MEM_W))
    qh = q.reshape(B, S, MEM_HEADS, MEM_HEAD_DIM)
    kh = k.reshape(B, M, MEM_HEADS, MEM_HEAD_DIM)
    vh = v.reshape(B, M, MEM_HEADS, MEM_HEAD_DIM)
    s = jnp.einsum('bshd,bmhd->bhsm', qh, kh).astype(jnp.float32) * MEM_HEAD_DIM ** -0.5
    p = jax.nn.softmax(s, axis=-1)
    o = jnp.einsum('bhsm,bmhd->bshd', p, vh.astype(jnp.float32))
    return o.reshape(B, S, MEM_W).astype(q.dtype)

def shared_kv(h, kv_norm, w_kv, cmp_pos, cmp_w1, cmp_b1, cmp_w2, cmp_b2):
    B, S = h.shape[0], h.shape[1]
    G, Dh = NSA_GROUPS, NSA_HEAD_DIM
    kv = (rmsnorm(h, kv_norm) @ w_kv).reshape(B, S, 6, G, Dh).transpose(2, 0, 3, 1, 4)
    NC = (S - CMP_BLOCK) // CMP_STRIDE + 1
    win = jnp.arange(NC)[:, None] * CMP_STRIDE + jnp.arange(CMP_BLOCK)[None, :]

    def compress(t, j):
        blocks = t[:, :, win] + cmp_pos[j]
        flat = blocks.reshape(B, G, NC, CMP_BLOCK * Dh)
        return jax.nn.silu(flat @ cmp_w1[j] + cmp_b1[j]) @ cmp_w2[j] + cmp_b2[j]

    kc = compress(kv[0], 0)
    vc = compress(kv[1], 1)
    return (kc, vc, kv[2], kv[3], kv[4], kv[5])

def nsa_mixer(q, gates, shared, rel_bias):
    kc, vc, ks, vs, kw, vw = shared
    B, S = q.shape[0], q.shape[1]
    G, R, Dh = NSA_GROUPS, NSA_REP, NSA_HEAD_DIM
    NC = kc.shape[2]
    NSB = S // SEL_BLOCK
    n_sel = min(SEL_TOPK, NSB)
    qg = (q * Dh ** -0.5).reshape(B, S, G, R, Dh).transpose(0, 2, 3, 1, 4)
    gg = gates.reshape(B, S, G, R, 3).transpose(0, 2, 3, 1, 4)
    kb = ks.reshape(B, G, NSB, SEL_BLOCK, Dh)
    vb = vs.reshape(B, G, NSB, SEL_BLOCK, Dh)
    kw_p = jnp.pad(kw, ((0, 0), (0, 0), (WINDOW, 0), (0, 0)))
    vw_p = jnp.pad(vw, ((0, 0), (0, 0), (WINDOW, 0), (0, 0)))
    cmp_start = jnp.arange(NC) * CMP_STRIDE
    cmp_end = cmp_start + CMP_BLOCK - 1
    sel_idx = jnp.arange(NSB)
    sel_start = sel_idx * SEL_BLOCK
    overlap = ((cmp_start[:, None] < sel_start[None, :] + SEL_BLOCK)
               & (cmp_end[:, None] >= sel_start[None, :])).astype(jnp.float32)
    tbl = rel_bias.astype(jnp.float32).reshape(REL_BUCKETS, G, R)
    g_idx = jnp.arange(G)[None, :, None, None]

    def common_bias(dist):
        return tbl[rel_bucket(dist)].transpose(2, 3, 0, 1)

    def group_bias(dist):
        return jnp.moveaxis(tbl[rel_bucket(dist), g_idx], -1, 2)

    def block(c):
        t0 = c * Q_BLOCK_2
        t = t0 + jnp.arange(Q_BLOCK_2)
        qb = lax.dynamic_slice_in_dim(qg, t0, Q_BLOCK_2, axis=3)
        gb = lax.dynamic_slice_in_dim(gg, t0, Q_BLOCK_2, axis=3)
        d_c = t[:, None] - cmp_end[None, :]
        s_c = jnp.einsum('bgrqd,bgkd->bgrqk', qb, kc).astype(jnp.float32) + common_bias(d_c)
        p_c = masked_softmax(s_c, d_c >= 0)
        o_c = jnp.einsum('bgrqk,bgkd->bgrqd', p_c, vc.astype(jnp.float32))
        imp = jnp.einsum('bgrqk,kj->bgqj', p_c, overlap)
        cur = (t // SEL_BLOCK)[:, None]
        jj = sel_idx[None, :]
        forced = (jj == 0) | (jj == cur) | (jj == cur - 1)
        score = jnp.where(forced, 1e4, jnp.where(jj <= cur, imp, -1.0))
        _, idx = lax.top_k(score, n_sel)
        gather = jax.vmap(jax.vmap(lambda blk, ix: blk[ix]))
        k_sel = gather(kb, idx).reshape(B, G, Q_BLOCK_2, n_sel * SEL_BLOCK, Dh)
        v_sel = gather(vb, idx).reshape(B, G, Q_BLOCK_2, n_sel * SEL_BLOCK, Dh)
        pos = (idx[..., None] * SEL_BLOCK + jnp.arange(SEL_BLOCK)).reshape(B, G, Q_BLOCK_2, n_sel * SEL_BLOCK)
        d_s = t[None, None, :, None] - pos
        s_s = jnp.einsum('bgrqd,bgqkd->bgrqk', qb, k_sel).astype(jnp.float32) + group_bias(d_s)
        p_s = masked_softmax(s_s, (d_s >= 0)[:, :, None])
        o_s = jnp.einsum('bgrqk,bgqkd->bgrqd', p_s, v_sel.astype(jnp.float32))
        kwb = lax.dynamic_slice_in_dim(kw_p, t0, WINDOW + Q_BLOCK_2, axis=2)
        vwb = lax.dynamic_slice_in_dim(vw_p, t0, WINDOW + Q_BLOCK_2, axis=2)
        s_pos = t0 - WINDOW + jnp.arange(WINDOW + Q_BLOCK_2)
        d_w = t[:, None] - s_pos[None, :]
        mask_w = (d_w >= 0) & (d_w < WINDOW) & (s_pos[None, :] >= 0)
        s_w = jnp.einsum('bgrqd,bgkd->bgrqk', qb, kwb).astype(jnp.float32) + common_bias(d_w)
        p_w = masked_softmax(s_w, mask_w)
        o_w = jnp.einsum('bgrqk,bgkd->bgrqd', p_w, vwb.astype(jnp.float32))
        o = gb[..., 0:1] * o_c + gb[..., 1:2] * o_s + gb[..., 2:3] * o_w
        return o.astype(q.dtype)

    out = lax.map(block, jnp.arange(S // Q_BLOCK_2))
    return out.transpose(1, 0, 4, 2, 3, 5).reshape(B, S, NSA_HEADS * Dh)

def conv_ffn(x, w_up, conv_w, conv_b, w_down):
    S = x.shape[1]
    u = x @ w_up
    u_pad = jnp.pad(u, ((0, 0), (CONV_WIDTH - 1, 0), (0, 0)))
    hc = conv_b
    for j in range(CONV_WIDTH):
        hc = hc + conv_w[j] * u_pad[:, j:j + S]
    a, b = split_cols(hc, (FFN_DIM, FFN_DIM))
    return (jax.nn.silu(a) * b) @ w_down

def second_inputs(seed: int = 0) -> dict:
    key = jax.random.key(seed)
    ks = jax.random.split(key, 26)
    f32 = jnp.float32

    def nrm(k, shape, scale):
        return jax.random.normal(k, shape, f32) * scale

    def gain(k, shape):
        return 1.0 + 0.02 * jax.random.normal(k, shape, f32)

    res = (2.0 * DEPTH_2) ** -0.5
    return {
        'x': nrm(ks[0], (BATCH, SEQ, D_MODEL), 1.0),
        'mem': nrm(ks[1], (BATCH, MEM_LEN, D_MODEL), 1.0),
        'norm_mix': gain(ks[2], (DEPTH_2, D_MODEL)),
        'norm_mem': gain(ks[3], (DEPTH_2, D_MODEL)),
        'w_mem_kv': nrm(ks[4], (DEPTH_2, D_MODEL, 2 * MEM_W), D_MODEL ** -0.5),
        'w_out': nrm(ks[5], (DEPTH_2, MIX_W, D_MODEL), MIX_W ** -0.5 * res),
        'norm_ffn': gain(ks[6], (DEPTH_2, D_MODEL)),
        'w_up': nrm(ks[7], (DEPTH_2, D_MODEL, 2 * FFN_DIM), D_MODEL ** -0.5),
        'conv_w': nrm(ks[8], (DEPTH_2, CONV_WIDTH, 2 * FFN_DIM), CONV_WIDTH ** -0.5),
        'conv_b': nrm(ks[9], (DEPTH_2, 2 * FFN_DIM), 0.01),
        'w_down': nrm(ks[10], (DEPTH_2, FFN_DIM, D_MODEL), FFN_DIM ** -0.5 * res),
        'gla_w_in': nrm(ks[11], (N_A_LAYERS, D_MODEL, GLA_IN), D_MODEL ** -0.5),
        'gla_w_gate_up': nrm(ks[12], (N_A_LAYERS, GLA_RANK, GLA_HEADS * GLA_DK), GLA_RANK ** -0.5),
        'gla_b_gate': nrm(ks[13], (N_A_LAYERS, GLA_HEADS * GLA_DK), 0.01),
        'gla_out_norm': gain(ks[14], (N_A_LAYERS, GLA_DV)),
        'nsa_w_in': nrm(ks[15], (N_B_LAYERS, D_MODEL, NSA_IN), D_MODEL ** -0.5),
        'kv_norm': gain(ks[16], (D_MODEL,)),
        'w_kv_shared': nrm(ks[17], (D_MODEL, SHARED_KV_W), D_MODEL ** -0.5),
        'cmp_pos': nrm(ks[18], (2, CMP_BLOCK, NSA_HEAD_DIM), 0.1),
        'cmp_w1': nrm(ks[19], (2, CMP_BLOCK * NSA_HEAD_DIM, CMP_HIDDEN), (CMP_BLOCK * NSA_HEAD_DIM) ** -0.5),
        'cmp_b1': nrm(ks[20], (2, CMP_HIDDEN), 0.01),
        'cmp_w2': nrm(ks[21], (2, CMP_HIDDEN, NSA_HEAD_DIM), CMP_HIDDEN ** -0.5),
        'cmp_b2': nrm(ks[22], (2, NSA_HEAD_DIM), 0.01),
        'rel_bias': nrm(ks[23], (REL_BUCKETS, NSA_HEADS), 0.5),
        'final_norm': gain(ks[24], (D_MODEL,)),
    }

def second_block(x, mem, norm_mix, norm_mem, w_mem_kv, w_out, norm_ffn, w_up, conv_w, conv_b, w_down,
              gla_w_in, gla_w_gate_up, gla_b_gate, gla_out_norm, nsa_w_in, kv_norm, w_kv_shared,
              cmp_pos, cmp_w1, cmp_b1, cmp_w2, cmp_b2, rel_bias, final_norm):
    B, S = x.shape[0], x.shape[1]
    h = x
    shared = None
    for i in range(DEPTH_2):
        if i == N_A_LAYERS:
            shared = shared_kv(h, kv_norm, w_kv_shared, cmp_pos, cmp_w1, cmp_b1, cmp_w2, cmp_b2)
        xn = rmsnorm(h, norm_mix[i])
        mem_kv = rmsnorm(mem, norm_mem[i]) @ w_mem_kv[i]
        if i < N_A_LAYERS:
            q, k, v, g, lr, mq = split_cols(xn @ gla_w_in[i], GLA_SIZES)
            log_a = jax.nn.log_sigmoid((lr @ gla_w_gate_up[i] + gla_b_gate[i]).astype(jnp.float32)) / GLA_GATE_NORM
            main = gla_mixer(q.reshape(B, S, GLA_HEADS, GLA_DK), k.reshape(B, S, GLA_HEADS, GLA_DK),
                             v.reshape(B, S, GLA_HEADS, GLA_DV), log_a.reshape(B, S, GLA_HEADS, GLA_DK),
                             g.reshape(B, S, GLA_HEADS, GLA_DV), gla_out_norm[i])
        else:
            q, gl, mq = split_cols(xn @ nsa_w_in[i - N_A_LAYERS], NSA_SIZES)
            gates = jax.nn.sigmoid(gl.astype(jnp.float32)).reshape(B, S, NSA_HEADS, 3)
            main = nsa_mixer(q.reshape(B, S, NSA_HEADS, NSA_HEAD_DIM), gates, shared, rel_bias)
        mo = mem_attention(mq, mem_kv)
        h = h + jnp.concatenate([main.astype(xn.dtype), mo.astype(xn.dtype)], axis=-1) @ w_out[i]
        h = h + conv_ffn(rmsnorm(h, norm_ffn[i]), w_up[i], conv_w[i], conv_b[i], w_down[i])
    return rmsnorm(h, final_norm)


def setup_inputs(seed=0):
    out = dict(first_inputs(seed))
    for name, value in second_inputs(seed + 1).items():
        if name != "x":
            out[name + "_2"] = value
    return out


def reference(
    x, p, positions, g_mix_pre, w_in, conv_a_w, w_a_out, g_q_lat, w_q_up, g_kv_lat, w_kv_up,
    w_b_out, w_o, g_mix_post, g_ffn_pre, w_ffn_up, conv_ffn_w, b_ffn_conv, w_ffn_down,
    g_ffn_post, w_ple_proj, w_ple_gate, g_ple_post, mem_2, norm_mix_2, norm_mem_2, w_mem_kv_2,
    w_out_2, norm_ffn_2, w_up_2, conv_w_2, conv_b_2, w_down_2, gla_w_in_2, gla_w_gate_up_2,
    gla_b_gate_2, gla_out_norm_2, nsa_w_in_2, kv_norm_2, w_kv_shared_2, cmp_pos_2, cmp_w1_2,
    cmp_b1_2, cmp_w2_2, cmp_b2_2, rel_bias_2, final_norm_2,
):
    x = first_block(
        x, p, positions, g_mix_pre, w_in, conv_a_w, w_a_out, g_q_lat, w_q_up, g_kv_lat, w_kv_up,
        w_b_out, w_o, g_mix_post, g_ffn_pre, w_ffn_up, conv_ffn_w, b_ffn_conv, w_ffn_down,
        g_ffn_post, w_ple_proj, w_ple_gate, g_ple_post,
    )
    return second_block(
        x, mem_2, norm_mix_2, norm_mem_2, w_mem_kv_2, w_out_2, norm_ffn_2, w_up_2, conv_w_2,
        conv_b_2, w_down_2, gla_w_in_2, gla_w_gate_up_2, gla_b_gate_2, gla_out_norm_2,
        nsa_w_in_2, kv_norm_2, w_kv_shared_2, cmp_pos_2, cmp_w1_2, cmp_b1_2, cmp_w2_2, cmp_b2_2,
        rel_bias_2, final_norm_2,
    )


_drawn_inputs = setup_inputs


def setup_inputs(seed=0):
    import zlib

    import numpy as np

    out = dict(_drawn_inputs(seed))
    spreads = {}
    factors = {'g_q_lat': 8.0,
     'g_kv_lat': 7.558,
     'b_ffn_conv': 7.341,
     'mem_2': 2.972,
     'norm_mix_2': 8.0,
     'norm_mem_2': 8.0,
     'w_mem_kv_2': 2.954,
     'norm_ffn_2': 8.0,
     'conv_b_2': 8.0,
     'gla_w_gate_up_2': 4.158,
     'gla_b_gate_2': 37.217,
     'gla_out_norm_2': 8.0,
     'kv_norm_2': 24.841,
     'cmp_pos_2': 32.265,
     'cmp_b1_2': 176.815,
     'cmp_b2_2': 200.0,
     'rel_bias_2': 12.988,
     'final_norm_2': 22.89}
    for name, (base, spread) in spreads.items():
        noise = np.random.default_rng([zlib.crc32(name.encode()), seed]).standard_normal(out[name].shape)
        drawn = base * np.exp(spread * noise) if base else spread * noise
        out[name] = jnp.asarray(drawn.astype(out[name].dtype))
    for name, factor in factors.items():
        out[name] = (out[name] * factor).astype(out[name].dtype)
    return out
```

```python
from contextlib import ExitStack

import numpy as np

import concourse.bass as bass
from concourse import mybir

P = 128
S = 512
TT = S // P
D = 1024
KD = D // P
EPS = 1e-6
NEG = -1e30
CONV = 512
KC_ = CONV // P
Q_LORA, KV_LORA = 384, 256
HA, NOPE, ROPE, VD = 8, 64, 32, 64
QK = NOPE + ROPE
ROPE_THETA = 10000.0
F_DIM = 2816
KF_ = F_DIM // P
PLE = 256
MEM = 256
MH, MDH = 4, 64
GH, GDK, GDV, GR = 4, 96, 192, 16
NH, NG, NDH = 12, 4, 64
REP = NH // NG
CMP_B, CMP_S, CMP_H = 32, 16, 128
NCMP = (S - CMP_B) // CMP_S + 1
LP = CMP_B // 2
BUCKETS, MAX_DIST = 32, 128
RING = 4
UNIT = 1024
LEVELS = 7
TW = 640

ALU = mybir.AluOpType
ACT = mybir.ActivationFunctionType
F32 = mybir.dt.float32
F32R = mybir.dt.float32r
I32 = mybir.dt.int32
AX = mybir.AxisListType.X

NSA_ORDER = [(REP * (2 * t + g) + r) for t in range(NG // 2) for r in range(REP) for g in range(2)]



def _pack(blocks):
    units, at = [], UNIT
    for b in blocks:
        if at + b.shape[1] > UNIT:
            units.append(np.zeros((P, UNIT), np.float32))
            at = 0
        units[-1][:b.shape[0], at:at + b.shape[1]] = b
        at += b.shape[1]
    return units


def _cols(w, first, n=P):
    out = []
    for k in range(-(-w.shape[0] // P)):
        b = np.zeros((P, P), np.float32)
        rows = w[k * P:(k + 1) * P, first:first + n]
        b[:rows.shape[0], :rows.shape[1]] = rows
        out.append(b)
    return out


def _moving(w, first, n):
    return [w[k * P:(k + 1) * P, first:first + n] for k in range(w.shape[0] // P)]


def weight_units(a):
    u = []

    def tiles(w, firsts, n=P):
        u.extend(_pack([b for f in firsts for b in _cols(w, f, n)]))

    def ffn(up, down):
        tiles(up, [f + h for f in range(0, F_DIM, P) for h in (0, F_DIM)])
        for f in range(0, D, P):
            u.extend(_pack(_cols(down, f)))

    def memory(w):
        tiles(w, [0, P])
        u.extend(_pack(_moving(w, MH * MDH, MH * MDH)))

    w = a["w_in"][0]
    c = CONV
    tiles(w, [x + i * P for i in range(KC_) for x in (c, 2 * c, 0)])
    at = 3 * CONV
    tiles(w, range(at, at + Q_LORA + KV_LORA, P))
    at += Q_LORA + KV_LORA
    r = w[:, at:at + ROPE]
    h = ROPE // 2
    turned = np.concatenate([r[:, h:], r[:, :h]], 1)
    tiles(np.concatenate([np.zeros((D, NOPE), np.float32), r, turned], 1), [0])
    at += ROPE
    tiles(w, range(at, at + 2 * D, P))
    q = a["w_q_up"][0].reshape(Q_LORA, HA, QK)
    q = np.concatenate([q, q[:, :, NOPE + h:], q[:, :, NOPE:NOPE + h]], 2).reshape(Q_LORA, HA * P)
    tiles(q, range(0, HA * P, P))
    kv = a["w_kv_up"][0].reshape(KV_LORA, HA, NOPE + VD)
    tiles(kv[:, :, :NOPE].reshape(KV_LORA, -1), range(0, HA * NOPE, P))
    u.extend(_pack(_moving(kv[:, :, NOPE:].reshape(KV_LORA, -1), 0, HA * VD)))
    tiles(a["w_a_out"][0], range(0, D, P))
    tiles(a["w_b_out"][0], range(0, D, P))
    tiles(a["w_o"][0], range(0, D, P))
    ffn(a["w_ffn_up"][0], a["w_ffn_down"][0])
    tiles(a["w_ple_proj"][0], range(0, D, P))
    tiles(a["w_ple_gate"][0], range(0, D, P))

    memory(a["w_mem_kv_2"][0])
    w = a["gla_w_in_2"][0]
    nk, nv = GH * GDK, GH * GDV
    tiles(w, [2 * nk + 2 * nv], GR)
    tiles(w, range(0, 2 * nk, GDK), GDK)
    tiles(w, [2 * nk + 2 * nv + GR + i * P for i in range(2)])
    for first in range(2 * nk, 2 * nk + 2 * nv, 256):
        u.extend(_pack(_moving(w, first, 256)))
    tiles(a["w_out_2"][0], range(0, D, P))
    ffn(a["w_up_2"][0], a["w_down_2"][0])

    w = a["w_kv_shared_2"]
    nk = NG * NDH
    tiles(w, [j * nk + i * P for j in (0, 1, 2, 4) for i in range(2)])
    for j in (3, 5):
        u.extend(_pack(_moving(w, j * nk, nk)))
    for j in range(2):
        tiles(a["cmp_w1_2"][j], [0])
    memory(a["w_mem_kv_2"][1])
    w = a["nsa_w_in_2"][0]
    nq = NH * NDH
    heads = [w[:, NDH * x:NDH * (x + 1)] for x in NSA_ORDER]
    tiles(np.concatenate(heads, 1), range(0, nq, P))
    tiles(w, [nq + 3 * NH + i * P for i in range(2)])
    tiles(w, [nq], 3 * NH)
    tiles(a["w_out_2"][1], range(0, D, P))
    ffn(a["w_up_2"][1], a["w_down_2"][1])
    return np.stack(u)


def _column_layout():
    at, where = 0, {}
    for name, n in [("mix_pre", 8), ("q_lat", 3), ("kv_lat", 2), ("mix_post", 8), ("ffn_pre", 8),
                    ("ffn_post", 8), ("ple_post", 8), ("conv_a", 3 * KC_), ("ffn0", 8 * KF_),
                    ("ffn1", 8 * KF_), ("ffn2", 8 * KF_), ("nmix0", 8), ("nmix1", 8), ("nmem0", 8),
                    ("nmem1", 8), ("nffn1", 8), ("nffn2", 8), ("nkv", 8), ("final", 8), ("cb1", 2),
                    ("cb2", 1), ("pos0", LP), ("pos1", LP), ("w2_0", NDH), ("w2_1", NDH),
                    ("eps", 1), ("inv", 1), ("quarter", 1), ("halfpi", 1), ("sign", 1), ("valid", 1)]:
        where[name] = at
        at += n
    return where, at


COL, N_COL = _column_layout()
ROW = {"bgate": 0, "onorm": GH * GDK, "cb2r": GH * GDK + GDV}
N_ROW = GH * GDK + GDV + NDH


def columns(a):
    out = np.zeros((P, N_COL), np.float32)

    def put(name, v, step=1, shift=0):
        m = np.asarray(v, np.float32).reshape(-1, P).T
        at = COL[name] + shift
        out[:, at:at + step * m.shape[1]:step] = m

    put("mix_pre", a["g_mix_pre"][0])
    put("q_lat", a["g_q_lat"][0])
    put("kv_lat", a["g_kv_lat"][0])
    put("mix_post", a["g_mix_post"][0])
    put("ffn_pre", a["g_ffn_pre"][0])
    put("ffn_post", a["g_ffn_post"][0])
    put("ple_post", a["g_ple_post"][0])
    for j in range(3):
        put("conv_a", a["conv_a_w"][0, j], 3, j)
    for name, w, b in (("ffn0", a["conv_ffn_w"][0], a["b_ffn_conv"][0]),
                       ("ffn1", a["conv_w_2"][0], a["conv_b_2"][0]),
                       ("ffn2", a["conv_w_2"][1], a["conv_b_2"][1])):
        for half in range(2):
            part = slice(half * F_DIM, (half + 1) * F_DIM)
            for j in range(3):
                put(name, w[j, part], 8, 4 * half + j)
            put(name, b[part], 8, 4 * half + 3)
    for i in range(2):
        put(f"nmix{i}", a["norm_mix_2"][i])
        put(f"nmem{i}", a["norm_mem_2"][i])
        put(f"nffn{i + 1}", a["norm_ffn_2"][i])
        out[:, COL["cb1"] + i] = a["cmp_b1_2"][i]
        at = COL[f"pos{i}"]
        out[:, at:at + LP] = a["cmp_pos_2"][i].reshape(LP, P).T
        at = COL[f"w2_{i}"]
        out[:, at:at + NDH] = a["cmp_w2_2"][i]
    put("nkv", a["kv_norm_2"])
    put("final", a["final_norm_2"])
    out[:NDH, COL["cb2"]] = a["cmp_b2_2"][0]
    out[NDH:, COL["cb2"]] = a["cmp_b2_2"][0]
    half = ROPE // 2
    inv = (1.0 / (np.float32(ROPE_THETA) ** (np.arange(half, dtype=np.float32)
                                              * np.float32(2.0 / ROPE)))).astype(np.float32)
    out[NOPE:, COL["inv"]] = np.tile(inv, 4)
    out[:, COL["eps"]] = EPS
    out[NOPE:NOPE + ROPE, COL["quarter"]] = 0.25
    out[NOPE:NOPE + ROPE, COL["halfpi"]] = np.pi / 2
    out[:, COL["sign"]] = 1.0
    out[NOPE + ROPE:NOPE + ROPE + half, COL["sign"]] = -1.0
    out[CMP_B - 1:, COL["valid"]] = 1.0
    return out


def rows(a):
    r = np.concatenate([a["gla_b_gate_2"][0], a["gla_out_norm_2"][0], a["cmp_b2_2"][1]])
    return np.ascontiguousarray(np.broadcast_to(r, (P, N_ROW)))


def bucket_table():
    out = np.zeros((BUCKETS + 1, TW), np.float32)
    exact = BUCKETS // 2
    for n in range(TW):
        d = S - 1 - n
        if d < 0:
            out[BUCKETS, n] = NEG
            continue
        large = exact + int(np.log(max(d, 1) / exact) / np.log(MAX_DIST / exact) * (BUCKETS - exact))
        out[d if d < exact else min(large, BUCKETS - 1), n] = 1.0
    return out


CONST = {"ident": 0, "ones": P}
N_CONST = 2 * P


def fixed():
    out = np.zeros((P, N_CONST), np.float32)
    out[:, :P] = np.eye(P)
    out[:, P:2 * P] = 1.0
    return out


def chunk_mask():
    out = np.zeros((P, S), np.float32)
    out[:64, S - 64:] = NEG
    return out


def decay_tables():
    t, i = np.arange(P)[:, None], np.arange(P)[None, :]
    sums, masks = [], [np.eye(P)]
    for lv in range(1, LEVELS + 1):
        b = 2 ** lv
        mid = i // b * b + b // 2 - 1
        late = i > mid
        sums.append(np.where(late, (t > mid) & (t <= i), (t > i) & (t <= mid)))
        j = np.arange(P)[:, None]
        masks.append((j // b == i // b) & (j % b < b // 2) & (i % b >= b // 2))
    sums += [t <= i, t > i]
    return (np.concatenate(sums, 1).astype(np.float32) / 16.0,
            np.concatenate(masks, 1).astype(np.float32))


N_SUMS, N_MASKS = LEVELS + 2, LEVELS + 1

U_FFN_UP, U_FFN_DOWN = 2 * KF_, 3 * KD
N_UNITS = (34 + 3 + 2 + 4 + 4 + 8 + U_FFN_UP + U_FFN_DOWN + 2 + 8
           + 4 + 11 + 12 + 8 + U_FFN_UP + U_FFN_DOWN
           + 8 + 4 + 4 + 4 + 9 + 8 + U_FFN_UP + U_FFN_DOWN)


class Count:

    def __init__(self, eng):
        self.eng, self.n, self.loop = eng, {}, None

    def did(self, ins, sem, wait=True):
        ins.then_inc(sem, 1)
        self.n[sem] = self.n.get(sem, 0) + 1
        if wait:
            self.eng.wait_ge(sem, self.at(sem))

    def tell(self, sem):
        self.eng.sem_inc(sem, 1)
        self.n[sem] = self.n.get(sem, 0) + 1

    def at(self, sem):
        n = self.n.get(sem, 0)
        if self.loop is None:
            return n
        i, start, per = self.loop
        return i * per[sem] + n if sem in per else n

    def enter(self, i, per):
        self.loop = (i, dict(self.n), per)

    def leave(self, turns):
        _, start, per = self.loop
        for sem, n in self.n.items():
            made = n - start.get(sem, 0)
            assert made == per.get(sem, 0), (sem.name, made)
            self.n[sem] = start.get(sem, 0) + turns * made
        self.loop = None


def build_program(nc, weights, x_t, p_t, mem_t, cols, rws, positions, rel, wgate, consts, chunk, buckets,
                  sums, masks, out):
    ctx = ExitStack()
    base = [17408]

    def fix(name, shape, dt=F32):
        t = nc.alloc_sbuf_tensor_at(name, shape, dt, offset=base[0])
        base[0] += -(-int(np.prod(shape[1:])) * 4 // 32) * 32
        return t

    wraw = fix("wraw", [P, RING, UNIT])
    whi = fix("whi", [P, RING, UNIT], F32R)
    wlo = fix("wlo", [P, RING, UNIT], F32R)
    h = fix("h", [P, KD, S])
    x_at = base[0]
    xhi = fix("xhi", [P, KD, S], F32R)
    xlo = fix("xlo", [P, KD, S], F32R)
    col = fix("col", [P, N_COL])
    row = fix("row", [P, N_ROW])
    const = fix("const", [P, N_CONST])
    rstd = fix("rstd", [P, S])
    u = fix("u", [P, 2, S + 2])
    rstd2 = nc.alloc_sbuf_tensor_at("rstd2", [P, S], F32, offset=base[0] - 4128)
    tmp = nc.alloc_sbuf_tensor_at("tmp", [P, S], F32, offset=base[0] - 2048)
    sqsum = fix("sqsum", [P, S])
    sq = fix("sq", [P, 2, S])
    rstd_t = fix("rstd_t", [P, 4])
    small = fix("small", [P, 16])
    decay = fix("decay", [P, GH * TT])
    osum = fix("osum", [P, GH * TT])
    oroot = fix("oroot", [P, GH * TT])
    arena = base[0]
    KB = 1024

    def put(name, shape, at, dt=F32):
        assert arena + at + int(np.prod(shape[1:])) * 4 <= 229344, (name, arena, at)
        return nc.alloc_sbuf_tensor_at(name, shape, dt, offset=arena + at)

    fhi = put("fhi", [P, KF_, S], 0, F32R)
    flo = put("flo", [P, KF_, S], 44 * KB, F32R)
    sg = put("sg", [P, 2 * KD, S], 0)
    lat = put("lat", [P, 5, S], 32 * KB)
    lathi = put("lathi", [P, 5, S], 42 * KB, F32R)
    latlo = put("latlo", [P, 5, S], 52 * KB, F32R)
    yhi = put("yhi", [P, KC_, S], 62 * KB, F32R)
    ylo = put("ylo", [P, KC_, S], 70 * KB, F32R)
    va = put("va", [P, TT, HA * VD], 78 * KB)
    cs = put("cs", [P, S], 86 * KB)
    kpe = put("kpe", [P, S], 84 * KB)
    chunkm = put("chunkm", [P, S], 88 * KB)
    prod = put("prod", [P, S + 2], 78 * KB)
    cv = put("cv", [P, S], 80 * KB + 64)
    pos_i = nc.alloc_sbuf_tensor_at("pos_i", [P, S], I32, offset=arena + 32 * KB)
    ang = put("ang", [P, 3, S], 34 * KB)
    relv = put("relv", [P, 16], 42 * KB)
    bk = put("bk", [P, TW], 42 * KB + 64)
    vr = put("vr", [P, TW], 45 * KB)
    s_a = put("s_a", [P, 2, S], 32 * KB)
    pt_a = put("pt_a", [P, 2, S], 36 * KB)
    qf = nc.alloc_sbuf_tensor_at("qf", [P, HA, S], F32, offset=x_at)
    kf = nc.alloc_sbuf_tensor_at("kf", [P, HA, S], F32, offset=x_at + 16 * KB)
    y_o = put("y_o", [P, KD, S], 32 * KB)
    y_d = nc.alloc_sbuf_tensor_at("y_d", [P, KD, S], F32, offset=x_at + 16 * KB)
    p_f = nc.alloc_sbuf_tensor_at("p_f", [P, 2, S], F32, offset=x_at)
    p_hi = nc.alloc_sbuf_tensor_at("p_hi", [P, 2, S], F32R, offset=x_at + 4 * KB)
    p_lo = nc.alloc_sbuf_tensor_at("p_lo", [P, 2, S], F32R, offset=x_at + 8 * KB)
    e = put("e", [P, KD, S], 0)
    gs = put("gs", [P, 2, S], 40 * KB)
    qg = put("qg", [P, GH, S], 0)
    kg = put("kg", [P, GH, S], 8 * KB)
    vg = put("vg", [P, TT, GH * GDV], 16 * KB)
    gg = put("gg", [P, TT, GH * GDV], 28 * KB)
    la = put("la", [P, TT, GH * GDK], 40 * KB)
    kout = put("kout", [P, TT, GH * GDK], 40 * KB)
    f = [put(f"f{i}", [P, GH, S], (46 + 8 * i) * KB) for i in range(2)]
    xg = put("xg", [P, TT, GH * GDK], 54 * KB)
    at_ = put("at_", [P, GH, S], 62 * KB)
    dm = put("dm", [P, N_SUMS, P], 70 * KB)
    mk = put("mk", [P, N_MASKS, P], 75 * KB)
    mq1 = put("mq1", [P, 2, S], 79 * KB)
    mk1 = put("mk1", [P, 2, MEM], 83 * KB)
    mv1 = put("mv1", [P, 2, MH * MDH], 85 * KB)
    st = put("st", [P, GH, GDV], 87 * KB)
    lr = put("lr", [P, S], 62 * KB)
    wg = put("wg", [P, GH * GDK], 64 * KB)
    glt = put("glt", [P, TT, GH * GDK], 46 * KB)
    o_g = put("o_g", [P, TT, GH * GDV], 46 * KB)
    s_1 = put("s_1", [P, 2, S], 0)
    pt_1 = put("pt_1", [P, 2, S], 4 * KB)
    mem1 = [put("mem1", [P, KD, MEM], 16 * KB), put("mem1hi", [P, KD, MEM], 24 * KB, F32R),
            put("mem1lo", [P, KD, MEM], 32 * KB, F32R)]
    qn = put("qn", [P, 6, S], 0)
    toep = put("toep", [P, NH, S], 12 * KB)
    kn = [put("ks", [P, 2, S], 36 * KB), put("kw", [P, 2, S], 40 * KB)]
    vn = [put("vs", [P, TT, NG * NDH], 44 * KB), put("vw", [P, TT, NG * NDH], 48 * KB)]
    kc = put("kc", [P, 2, 32], 52 * KB)
    vc = put("vc", [P, NG * NDH], 52 * KB + 256)
    gt = put("gt", [P, TT, 3 * NH], 52 * KB + 1280)
    mk2 = put("mk2", [P, 2, MEM], 54 * KB)
    mv2 = put("mv2", [P, 2, MH * MDH], 56 * KB)
    mq2 = put("mq2", [P, 2, S], 58 * KB)
    s_2 = put("s_2", [P, 2, S], 62 * KB)
    pt_2 = put("pt_2", [P, 2, S], 66 * KB)
    z = put("z", [P, NG, S], 58 * KB)
    zw = put("zw", [P, LP, NG * NCMP], 70 * KB)
    zhi = [put(f"zhi{j}", [P, LP, NG * NCMP], 16 * j * KB, F32R) for j in range(2)]
    zlo = [put(f"zlo{j}", [P, LP, NG * NCMP], (8 + 16 * j) * KB, F32R) for j in range(2)]
    hid = put("hid", [P, 2, P], 66 * KB)
    mem2 = [put("mem2", [P, KD, MEM], 58 * KB), put("mem2hi", [P, KD, MEM], 78 * KB, F32R),
            put("mem2lo", [P, KD, MEM], 70 * KB, F32R)]

    acc = ctx.enter_context(nc.psum_tensor("acc", [P, 4, S], F32))
    sc = ctx.enter_context(nc.psum_tensor("sc", [P, 2, S], F32))
    ptp = ctx.enter_context(nc.psum_tensor("ptp", [P, S], F32))
    pv = ctx.enter_context(nc.psum_tensor("pv", [P, S], F32))
    ebank = [sc[:, 0, :], sc[:, 1, :], ptp[:, :], pv[:, :]]
    distances = nc.dram_tensor("distances", [NH, P * TW], F32, kind="Internal").ap()

    ident, ones = const[:, 0:P], const[:, P:2 * P]

    def C(name, i=0, n=1, p=slice(None)):
        return col[p, COL[name] + i:COL[name] + i + n]

    def plain(ap):
        return ap.bitcast(F32)

    names = ("w_open w_split out_ready out_done w_used w_hi acc_free x_ready acc_ready ss_added rs_ready e_free "
             "o_free bc_ready sc_free sc_ready pn_ready t_copied t_ready pv_done in_rel in_bk in_const "
             "qkv_ready lr_ready in_wg in_sums la_ready e_ready g_ready kout_ready st_ready og_ready "
             "hid_ready gln_ready in_toep dve_step sq_ready src_ready u_ready c_ready a_ready v_ready "
             "s_ready p_ready vr_ready in_col in_pos angle_ready sine_ready dist_out gate_in sig_ready "
             "in_chunk in_p ple_sig gl_raw gl_ln in_masks f_ready gates_raw osq_ready oroot_ready "
             "gates_ready z_done hid_raw act_step in_row in_mem1 in_mem2").split()
    sem = {n: ctx.enter_context(nc.semaphore(n)) for n in names}
    loaded = [ctx.enter_context(nc.semaphore(f"w_loaded{j}")) for j in range(RING)]
    in_x = [ctx.enter_context(nc.semaphore(f"in_x{j}")) for j in range(4)]
    mark = {}

    def step(q, k, n, bias, v, dest, qt, first, last, scale=1.0, gate=None, valid=None, width=P):
        return dict(q=q, k=k, n=n, bias=bias, v=v, dest=dest, qt=qt, first=first, last=last,
                    scale=scale, gate=gate, valid=valid, width=width, blocks=len(v))

    def latent_steps():
        for hd in range(HA):
            for qt in range(TT):
                n = (qt + 1) * P
                yield step(qf[0:QK, hd, qt * P:(qt + 1) * P], kf[0:QK, hd, 0:n], n,
                           chunkm[:, S - n:S], [va[:, b, hd * VD:(hd + 1) * VD] for b in range(qt + 1)],
                           (yhi, ylo, hd // 2, hd % 2 * VD), qt, True, True, scale=QK ** -0.5)

    def memory_steps(mq, mkt, mv):
        for hd in range(MH):
            p = slice(hd % 2 * MDH, hd % 2 * MDH + MDH)
            for qt in range(TT):
                yield step(mq[p, hd // 2, qt * P:(qt + 1) * P], mkt[p, hd // 2, :], MEM, None,
                           [mv[:, b, hd * MDH:(hd + 1) * MDH] for b in range(MEM // P)],
                           (xhi, xlo, 6 + hd // 2, hd % 2 * MDH), qt, True, True)

    def branch_steps():
        for hd in range(NH):
            g, r = hd // REP, hd % REP
            p = slice(g % 2 * NDH, g % 2 * NDH + NDH)
            vcols = slice(g * NDH, (g + 1) * NDH)
            for qt in range(TT):
                q = qn[p, g // 2 * REP + r, qt * P:(qt + 1) * P]
                n = (qt + 1) * P
                dest = (xhi, xlo, hd // 2, hd % 2 * NDH)
                nc_ = min(NCMP, 7 + 8 * qt)
                first = S - P + CMP_B - 1 - P * qt
                yield step(q, kc[p, g // 2, 0:nc_], nc_,
                           toep[:, hd, first:first + CMP_S * (nc_ - 1) + 1:CMP_S], [vc[0:nc_, vcols]],
                           dest, qt, True, False, gate=gt[:, qt, 3 * hd:3 * hd + 1],
                           valid=C("valid") if qt == 0 else None, width=nc_)
                for b in range(2):
                    yield step(q, kn[b][p, g // 2, 0:n], n, toep[:, hd, S - n:S],
                               [vn[b][:, kb, vcols] for kb in range(qt + 1)], dest, qt, False, b == 1,
                               gate=gt[:, qt, 3 * hd + 1 + b:3 * hd + 2 + b])

    block = ctx.enter_context(nc.Block(no_gpsimd_drain=False))

    @block.sync
    def _(sp):
        for j in range(4):
            sp.dma_start(h[:, 2 * j:2 * j + 2, :], x_t[:, 2 * j:2 * j + 2, :]).then_inc(in_x[j], 16)

        def load(unit, j):
            sp.dma_start(wraw[:, j, :], weights[unit]).then_inc(loaded[j], 16)

        for j in range(RING):
            load(j, j)
        with sp.Fori(1, N_UNITS // RING) as i:
            for j in range(RING):
                sp.wait_ge(sem["w_split"], i * RING + (j - RING + 1))
                load(i * RING + j, j)
        for unit in range(N_UNITS // RING * RING, N_UNITS):
            sp.wait_ge(sem["w_split"], unit - RING + 1)
            load(unit, unit % RING)
        for k in range(KD):
            sp.wait_ge(sem["out_ready"], k + 1)
            sp.dma_start(out[:, k, :], h[:, k, :]).then_inc(sem["out_done"], 16)
        sp.wait_ge(sem["out_done"], 16 * KD)

    @block.gpsimd
    def _(pool):
        def split(unit, j, turn, used):
            pool.wait_ge(loaded[j], turn)
            if used is not None:
                pool.wait_ge(sem["w_used"], used)
            pool.sem_inc(sem["w_open"], 1)
            nc.gpsimd.tensor_copy(whi[:, j, :], wraw[:, j, :]).then_inc(sem["w_hi"], 1)
            pool.wait_ge(sem["w_hi"], unit + 1)
            nc.gpsimd.tensor_tensor(wlo[:, j, :], wraw[:, j, :], plain(whi[:, j, :]),
                                    ALU.subtract).then_inc(sem["w_split"], 1)

        for j in range(RING):
            split(j, j, 16, None)
        with pool.Fori(1, N_UNITS // RING) as i:
            for j in range(RING):
                split(i * RING + j, j, i * 16 + 16, i * RING + (j - RING + 1))
        for unit in range(N_UNITS // RING * RING, N_UNITS):
            split(unit, unit % RING, 16 * (unit // RING + 1), unit - RING + 1)

    @block.tensor
    def _(pe):
        t = 0
        un = 0
        xs = 0
        bc = 0
        ss = 0
        steps_done = heads_done = e_done = 0

        def bank(tile, n=S, p=P):
            return acc[0:p, tile % 4, 0:n]

        def open_tile(tile, turn=None):
            if turn is not None:
                pe.wait_ge(sem["acc_free"], turn)
            elif tile >= 4:
                pe.wait_ge(sem["acc_free"], tile - 3)

        def three(o, a_hi, a_lo, b_hi, b_lo, start, stop, begins=False, done=None):
            m = nc.tensor.matmul(o, a_hi, b_hi, start=start, stop=False)
            if begins:
                m.then_inc(sem["w_used"], 1)
            nc.tensor.matmul(o, a_lo, b_hi, start=False, stop=False)
            m = nc.tensor.matmul(o, a_hi, b_lo, start=False, stop=stop)
            if done is not None:
                m.then_inc(done, 1)

        def stationary(x_hi, x_lo, kts, tiles, n=S, fresh=0):
            nonlocal t, un
            piece = 0
            for m in range(tiles):
                open_tile(t)
                for k in range(kts):
                    if piece % 8 == 0:
                        pe.wait_ge(sem["w_split"], un + 1)
                    if m == 0 and k < fresh:
                        pe.wait_ge(sem["x_ready"], xs + k + 1)
                    slot, c = un % RING, piece % 8 * P
                    three(bank(t, n), whi[:, slot, c:c + P], wlo[:, slot, c:c + P], x_hi[:, k, 0:n],
                          x_lo[:, k, 0:n], k == 0, k == kts - 1, piece % 8 == 0 and un > 0,
                          sem["acc_ready"] if k == kts - 1 else None)
                    piece += 1
                    if piece % 8 == 0 or (m == tiles - 1 and k == kts - 1):
                        piece = -(-piece // 8) * 8
                        un += 1
                t += 1

        def stationary_loop(x_hi, x_lo, turns, groups=4, kts=KD):
            nonlocal t, un
            per = -(-kts // 8)
            assert groups % 4 == 0
            with pe.Fori(0, turns) as i:
                for m in range(groups):
                    open_tile(t + m, i * groups + (t + m - 3))
                    for k in range(kts):
                        unit = m * per + k // 8
                        if k % 8 == 0:
                            pe.wait_ge(sem["w_split"], i * (groups * per) + (un + unit + 1))
                        slot, c = (un + unit) % RING, k % 8 * P
                        three(bank(t + m), whi[:, slot, c:c + P], wlo[:, slot, c:c + P], x_hi[:, k, :],
                              x_lo[:, k, :], k == 0, k == kts - 1, k % 8 == 0,
                              sem["acc_ready"] if k == kts - 1 else None)
            t += turns * groups
            un += turns * groups * per

        def moving(x_hi, x_lo, kts, n, tiles=TT):
            nonlocal t, un
            for i in range(tiles):
                open_tile(t + i)
            per = UNIT // n
            for k in range(kts):
                if k % per == 0:
                    pe.wait_ge(sem["w_split"], un + 1)
                slot, c = un % RING, k % per * n
                for i in range(tiles):
                    a = slice(i * P, (i + 1) * P)
                    three(bank(t + i, n), x_hi[:, k, a], x_lo[:, k, a], whi[:, slot, c:c + n],
                          wlo[:, slot, c:c + n], k == 0, k == kts - 1, k % per == 0 and i == 0,
                          sem["acc_ready"] if k == kts - 1 else None)
                if k % per == per - 1 or k == kts - 1:
                    un += 1
            t += tiles

        def sum_features(n, cols_=S):
            nonlocal bc, ss
            ss += n
            pe.wait_ge(sem["ss_added"], ss)
            if bc:
                pe.wait_ge(sem["rs_ready"], bc)
            if e_done:
                pe.wait_ge(sem["e_free"], e_done)
            if heads_done:
                pe.wait_ge(sem["o_free"], heads_done)
            nc.tensor.matmul(pv[:, 0:cols_], ones, sqsum[:, 0:cols_], start=True, stop=True)\
                .then_inc(sem["bc_ready"], 1)
            bc += 1

        def sum_tokens():
            nonlocal bc
            pe.wait_ge(sem["rs_ready"], bc)
            for i in range(TT):
                m = nc.tensor.matmul(pv[:, i:i + 1], sqsum[:, i * P:(i + 1) * P], ones[:, 0:1],
                                     start=True, stop=True)
            m.then_inc(sem["bc_ready"], 1)
            bc += 1

        def attention(steps, s, pts):
            nonlocal steps_done, heads_done
            b0 = steps_done
            if e_done:
                pe.wait_ge(sem["e_free"], e_done)
            pe.wait_ge(sem["rs_ready"], bc)

            def scores(i):
                w = steps[i]
                if b0 + i >= 2:
                    pe.wait_ge(sem["sc_free"], b0 + i - 1)
                nc.tensor.matmul(sc[:, i % 2, 0:w["n"]], w["q"], w["k"], start=True, stop=True)\
                    .then_inc(sem["sc_ready"], 1)

            def turn(i):
                w = steps[i]
                pe.wait_ge(sem["pn_ready"], b0 + i + 1)
                if b0 + i >= 1:
                    pe.wait_ge(sem["t_copied"], b0 + i)
                for b in range(w["blocks"]):
                    m = nc.tensor.transpose(ptp[0:w["width"], b * P:(b + 1) * P],
                                            s[:, i % 2, b * P:b * P + w["width"]], ident)
                m.then_inc(sem["t_ready"], 1)

            def values(i):
                nonlocal heads_done
                w = steps[i]
                pe.wait_ge(sem["t_copied"], b0 + i + 1)
                if w["qt"] == 0 and w["first"] and heads_done:
                    pe.wait_ge(sem["o_free"], heads_done)
                for b, v in enumerate(w["v"]):
                    m = nc.tensor.matmul(pv[0:64, w["qt"] * P:(w["qt"] + 1) * P], v,
                                         pts[0:w["width"], i % 2, b * P:(b + 1) * P],
                                         start=w["first"] and b == 0,
                                         stop=w["last"] and b == w["blocks"] - 1)
                m.then_inc(sem["pv_done"], 1)
                if w["last"] and w["qt"] == TT - 1:
                    heads_done += 1

            for i in range(len(steps) + 2):
                if i < len(steps):
                    scores(i)
                if 1 <= i <= len(steps):
                    turn(i - 1)
                if i >= 2:
                    values(i - 2)
            steps_done += len(steps)

        def feed_forward():
            nonlocal xs
            stationary(xhi, xlo, KD, 2, fresh=KD)
            xs += KD
            sum_features(KD)
            stationary(xhi, xlo, KD, 2)
            stationary_loop(xhi, xlo, (U_FFN_UP - 4) // 4)
            up = t
            xs += KF_
            pe.wait_ge(sem["x_ready"], xs)
            stationary_loop(fhi, flo, 2, kts=KF_)
            return up

        pe.wait_ge(sem["in_rel"], 16)
        pe.wait_ge(sem["in_bk"], 16)
        for n0, n1 in ((0, S), (S, TW)):
            open_tile(t)
            nc.tensor.matmul(bank(t, n1 - n0, NH), relv[0:BUCKETS + 1, 0:NH], bk[0:BUCKETS + 1, n0:n1],
                             start=True, stop=True).then_inc(sem["acc_ready"], 1)
            t += 1

        pe.wait_ge(sem["in_const"], 16)
        stationary(xhi, xlo, KD, 2, fresh=KD)
        xs += KD
        sum_features(KD)
        stationary(xhi, xlo, KD, 2)
        stationary_loop(xhi, xlo, 3)
        stationary(xhi, xlo, KD, 6)
        sum_features(3)
        sum_features(2)
        stationary_loop(xhi, xlo, 3)
        xs += KC_
        stationary(lathi[:, 0:3, :], latlo[:, 0:3, :], 3, HA, fresh=3)
        xs += 3
        stationary(lathi[:, 3:5, :], latlo[:, 3:5, :], 2, 4, fresh=2)
        xs += 2
        moving(lathi[:, 3:5, :], latlo[:, 3:5, :], 2, HA * VD)
        stationary(yhi, ylo, KC_, KD)
        pe.wait_ge(sem["qkv_ready"], 1)
        attention(list(latent_steps()), s_a, pt_a)
        pe.wait_ge(sem["x_ready"], xs + HA)
        xs += HA
        stationary(yhi, ylo, KC_, KD)
        pe.wait_ge(sem["x_ready"], xs + KD)
        xs += KD
        stationary_loop(xhi, xlo, 2)
        sum_features(KD)
        mark["up0"] = feed_forward()
        mark["down0"] = t
        sum_features(KD)
        pe.wait_ge(sem["x_ready"], xs + 2)
        xs += 2
        stationary(p_hi, p_lo, 2, KD)
        mark["ple"] = t
        stationary(xhi, xlo, KD, 2, fresh=KD)
        xs += KD
        sum_features(KD, MEM)
        stationary(xhi, xlo, KD, 6)
        sum_features(KD)

        def memory(m_hi, m_lo):
            nonlocal xs
            pe.wait_ge(sem["x_ready"], xs + KD)
            xs += KD
            stationary(m_hi, m_lo, KD, 2, n=MEM)
            moving(m_hi, m_lo, KD, MH * MDH, tiles=2)

        memory(mem1[1], mem1[2])
        stationary(xhi, xlo, KD, 2, fresh=KD)
        xs += KD
        sum_features(KD)
        sum_tokens()
        stationary(xhi, xlo, KD, 9)
        pe.wait_ge(sem["lr_ready"], 1)
        pe.wait_ge(sem["in_wg"], 16)
        for i in range(TT):
            open_tile(t)
            nc.tensor.matmul(bank(t, GH * GDK), lr[0:GR, i * P:(i + 1) * P], wg[0:GR, :],
                             start=True, stop=True).then_inc(sem["acc_ready"], 1)
            t += 1
        pe.wait_ge(sem["rs_ready"], bc)
        pe.wait_ge(sem["in_sums"], 16)
        for lv in range(1, N_SUMS + 1):
            for hd in range(GH):
                if lv == 1 and hd == 0:
                    pe.wait_ge(sem["la_ready"], 1)
                if e_done >= 4:
                    pe.wait_ge(sem["e_free"], e_done - 3)
                if e_done < 4 and heads_done:
                    pe.wait_ge(sem["o_free"], heads_done)
                for i in range(TT):
                    m = nc.tensor.matmul(ebank[hd][0:GDK, i * P:(i + 1) * P],
                                         la[:, i, hd * GDK:(hd + 1) * GDK], dm[:, lv - 1, :],
                                         start=True, stop=True)
                m.then_inc(sem["e_ready"], 1)
                e_done += 1
            if lv <= N_MASKS:
                for hd in range(GH):
                    open_tile(t)
                    if lv > 1:
                        pe.wait_ge(sem["g_ready"], GH * (lv - 2) + hd + 1)
                    a, b = (kg, qg) if lv == 1 else (f[(lv - 1) % 2], f[(lv - 1) % 2])
                    for i in range(TT):
                        w = slice(i * P, (i + 1) * P)
                        m = nc.tensor.matmul(acc[:, t % 4, w], a[0:GDK, hd, w], b[0:GDK, hd, w],
                                             start=True, stop=True)
                    m.then_inc(sem["acc_ready"], 1)
                    t += 1
                mark["pairs", lv - 1] = t
            if lv <= 6:
                moving(xhi, xlo, KD, 256)
        pe.wait_ge(sem["g_ready"], GH * N_SUMS)
        for i in range(TT):
            open_tile(t)
            for hd in range(GH):
                m = nc.tensor.transpose(acc[:, t % 4, hd * GDK:(hd + 1) * GDK],
                                        kg[0:GDK, hd, i * P:(i + 1) * P], ident[0:GDK, 0:GDK])
            m.then_inc(sem["acc_ready"], 1)
            t += 1
        pe.wait_ge(sem["kout_ready"], TT)
        for i in range(TT):
            for hd in range(GH):
                vcols = slice(hd * GDV, (hd + 1) * GDV)
                w = slice(i * P, (i + 1) * P)
                open_tile(t)
                m = nc.tensor.matmul(bank(t, GDV), at_[:, hd, w], vg[:, i, vcols], start=True, stop=i == 0)
                if i:
                    pe.wait_ge(sem["st_ready"], GH * (i - 1) + hd + 1)
                    m = nc.tensor.matmul(bank(t, GDV), qg[0:GDK, hd, w], st[0:GDK, hd, :], start=False,
                                         stop=True)
                m.then_inc(sem["acc_ready"], 1)
                t += 1
                if i < TT - 1:
                    open_tile(t)
                    nc.tensor.matmul(bank(t, GDV, GDK), kout[:, i, hd * GDK:(hd + 1) * GDK], vg[:, i, vcols],
                                     start=True, stop=True).then_inc(sem["acc_ready"], 1)
                    t += 1
        attention(list(memory_steps(mq1, mk1, mv1)), s_1, pt_1)
        xs += MH
        pe.wait_ge(sem["og_ready"], TT)
        for c in range(6):
            open_tile(t)
            for i in range(TT):
                m = nc.tensor.transpose(acc[:, t % 4, i * P:(i + 1) * P], o_g[:, i, c * P:(c + 1) * P], ident)
            m.then_inc(sem["acc_ready"], 1)
            t += 1
        xs += 6
        pe.wait_ge(sem["x_ready"], xs)
        stationary_loop(xhi, xlo, 2)
        feed_forward()

        stationary(xhi, xlo, KD, 2, fresh=KD)
        xs += KD
        sum_features(KD)
        sum_tokens()
        stationary(xhi, xlo, KD, 6)
        moving(xhi, xlo, KD, NG * NDH)
        moving(xhi, xlo, KD, NG * NDH)
        pe.wait_ge(sem["x_ready"], xs + 2)
        xs += 2
        for j in range(2):
            stationary(zhi[j], zlo[j], LP, 1, n=NG * NCMP)
        mark["windows"] = t
        sum_features(KD, MEM)
        memory(mem2[1], mem2[2])
        pe.wait_ge(sem["hid_ready"], 1)
        open_tile(t)
        nc.tensor.matmul(bank(t, NG * NCMP, NDH), C("w2_0", 0, NDH), hid[:, 0, 0:NG * NCMP], start=True,
                         stop=True).then_inc(sem["acc_ready"], 1)
        t += 1
        pe.wait_ge(sem["hid_ready"], 2)
        open_tile(t)
        for g in range(NG):
            m = nc.tensor.matmul(acc[0:NCMP, t % 4, g * NDH:(g + 1) * NDH], hid[:, 1, g * NCMP:(g + 1) * NCMP],
                                 C("w2_1", 0, NDH), start=True, stop=True)
        m.then_inc(sem["acc_ready"], 1)
        t += 1
        stationary(xhi, xlo, KD, 9, fresh=KD)
        xs += KD
        pe.wait_ge(sem["gln_ready"], 1)
        open_tile(t)
        for i in range(TT):
            m = nc.tensor.transpose(acc[:, t % 4, i * 3 * NH:(i + 1) * 3 * NH],
                                    tmp[0:3 * NH, i * P:(i + 1) * P], ident[0:3 * NH, 0:3 * NH])
        m.then_inc(sem["acc_ready"], 1)
        t += 1
        pe.wait_ge(sem["qkv_ready"], 2)
        pe.wait_ge(sem["in_toep"], 16)
        attention(list(branch_steps()) + list(memory_steps(mq2, mk2, mv2)), s_2, pt_2)
        xs += NH + MH
        pe.wait_ge(sem["x_ready"], xs)
        stationary_loop(xhi, xlo, 2)
        feed_forward()
        sum_features(KD)
        assert un == N_UNITS, un

    @block.vector
    def _(dve):
        n = Count(dve)
        t = 0
        sqs = 0
        rs = 0
        steps_done = 0
        V = nc.vector

        def take(p=P, cols_=S):
            i = t if n.loop is None else n.loop[0] * n.loop[2][sem["acc_free"]] + t
            dve.wait_ge(sem["acc_ready"], i + 1)
            return acc[0:p, t % 4, 0:cols_]

        def give(ins):
            nonlocal t
            n.did(ins, sem["acc_free"])
            t += 1

        def did(ins):
            n.did(ins, sem["dve_step"])

        def split(hi, lo, src, gain=None):
            if gain is None:
                did(V.tensor_copy(hi, src))
                n.did(V.tensor_tensor(lo, src, plain(hi), ALU.subtract), sem["x_ready"])
            else:
                did(V.tensor_scalar(hi, src, gain, None, ALU.mult))
                n.did(V.scalar_tensor_tensor(lo, src, gain, plain(hi), ALU.mult, ALU.subtract),
                      sem["x_ready"])

        def add_square(first, cols_=S):
            nonlocal sqs
            dve.wait_ge(sem["sq_ready"], sqs + 1)
            s = sq[:, sqs % 2, 0:cols_]
            if first:
                ins = V.tensor_copy(sqsum[:, 0:cols_], s)
            else:
                ins = V.tensor_tensor(sqsum[:, 0:cols_], sqsum[:, 0:cols_], s, ALU.add)
            n.did(ins, sem["ss_added"])
            sqs += 1

        def factor(to):
            nonlocal rs
            dve.wait_ge(sem["rs_ready"], rs + 1)
            did(V.reciprocal(to, to))
            rs += 1

        def stage(gain, before=None, squares=True, after=None):
            for k in range(KD):
                if before:
                    before(k)
                split(xhi[:, k, :], xlo[:, k, :], h[:, k, :], C(gain, k) if gain else None)
                if squares and k:
                    add_square(k == 1)
            if squares:
                add_square(False)

        def post_norm(y, gain):
            def go(k):
                did(V.scalar_tensor_tensor(tmp[:, :], y[:, k, :], C(gain, k), rstd[:, :], ALU.mult, ALU.mult))
                n.did(V.tensor_tensor(h[:, k, :], h[:, k, :], tmp[:, :], ALU.add), sem["src_ready"])
            return go

        def residual(k):
            ins = V.tensor_tensor(h[:, k, :], h[:, k, :], take(), ALU.add)
            give(ins)
            n.tell(sem["src_ready"])

        def gather_down(y):
            for k in range(KD):
                give(V.tensor_copy(y[:, k, :], take()))
                n.tell(sem["src_ready"])
                if k:
                    add_square(k == 1)
            add_square(False)

        def feed_forward(which):
            factor(rstd[:, :])
            did(V.memset(u[:, :, 0:2], 0.0))
            per = {sem["acc_free"]: 4, sem["u_ready"]: 4, sem["dve_step"]: 8, sem["c_ready"]: 4,
                   sem["x_ready"]: 2}
            c0 = COL[which]
            a0 = ffn_seen[0]
            with dve.Fori(0, KF_ // 2) as i:
                n.enter(i, per)
                for pair in range(2):
                    for half in range(2):
                        j = 2 * pair + half
                        src = take()
                        give(V.tensor_tensor(u[:, half, 2:], src, rstd[:, :], ALU.mult))
                        n.tell(sem["u_ready"])
                    for half in range(2):
                        j = 2 * pair + half
                        w = [col[:, bass.ds(i * 16 + (c0 + 8 * pair + 4 * half + tap), 1)] for tap in range(2)]
                        dve.wait_ge(sem["a_ready"], i * 4 + (a0 * 4 + j + 1))
                        c = sq[:, half, :]
                        did(V.scalar_tensor_tensor(c, u[:, half, 1:S + 1], w[1], c, ALU.mult, ALU.add))
                        n.did(V.scalar_tensor_tensor(c, u[:, half, 0:S], w[0], c, ALU.mult, ALU.add),
                              sem["c_ready"])
                    dve.wait_ge(sem["v_ready"], i * 2 + (a0 * 2 + pair + 1))
                    did(V.tensor_tensor(sq[:, 0, :], sq[:, 0, :], sq[:, 1, :], ALU.mult))
                    fo = (fhi[:, bass.ds(i * 2 + pair, 1), :].rearrange("p a n -> p (a n)"),
                          flo[:, bass.ds(i * 2 + pair, 1), :].rearrange("p a n -> p (a n)"))
                    split(fo[0], fo[1], sq[:, 0, :])
            n.leave(KF_ // 2)
            t_add(4 * (KF_ // 2 - 1))
            ffn_seen[0] += KF_ // 2

        ffn_seen = [0]

        def t_add(k):
            nonlocal t
            t += k

        def softmaxes(steps, s):
            nonlocal steps_done
            b0 = steps_done

            def high(i):
                w = steps[i]
                dve.wait_ge(sem["sc_ready"], b0 + i + 1)
                if b0 + i >= 2 and i >= 2:
                    dve.wait_ge(sem["t_ready"], b0 + i - 1)
                j, w_n = i % 2, w["n"]
                if w["bias"] is None:
                    did(V.tensor_copy(s[:, j, 0:w_n], sc[:, j, 0:w_n]))
                    n.did(V.tensor_reduce(small[:, 4 + j:5 + j], sc[:, j, 0:w_n], AX, ALU.max), sem["sc_free"])
                else:
                    n.did(V.tensor_tensor_reduce(s[:, j, 0:w_n], sc[:, j, 0:w_n], w["bias"], 1.0, -3e38,
                                                 ALU.add, ALU.max, small[:, 4 + j:5 + j]), sem["sc_free"])
                n.did(V.tensor_scalar(small[:, 6 + j:7 + j], small[:, 4 + j:5 + j], -w["scale"], None,
                                      ALU.mult), sem["s_ready"])

            def normal(i):
                w, j = steps[i], i % 2
                dve.wait_ge(sem["p_ready"], b0 + i + 1)
                r = small[:, 10 + j:11 + j]
                did(V.reciprocal(r, small[:, 8 + j:9 + j]))
                if w["valid"] is not None:
                    did(V.tensor_tensor(r, r, w["valid"], ALU.mult))
                if w["gate"] is not None:
                    did(V.tensor_tensor(r, r, w["gate"], ALU.mult))
                n.did(V.tensor_scalar(s[:, j, 0:w["n"]], s[:, j, 0:w["n"]], r, None, ALU.mult),
                      sem["pn_ready"])

            def output(i):
                w = steps[i]
                if not (w["last"] and w["qt"] == TT - 1):
                    return
                dve.wait_ge(sem["pv_done"], b0 + i + 1)
                hi, lo, tile, at = w["dest"]
                o = slice(at, at + 64)
                did(V.tensor_copy(hi[o, tile, :], pv[0:64, :]))
                n.did(V.tensor_tensor(lo[o, tile, :], pv[0:64, :], plain(hi[o, tile, :]), ALU.subtract),
                      sem["x_ready"])
                n.tell(sem["o_free"])

            for i in range(len(steps) + 3):
                if i < len(steps):
                    high(i)
                if 1 <= i <= len(steps):
                    normal(i - 1)
                if i >= 3:
                    output(i - 3)
            steps_done += len(steps)

        def memory_stage(m, gain):
            for k in range(KD):
                add_square(k == 0, MEM)
            factor(rstd2[:, 0:MEM])
            for k in range(KD):
                did(V.scalar_tensor_tensor(m[0][:, k, :], m[0][:, k, :], C(gain, k), rstd2[:, 0:MEM],
                                           ALU.mult, ALU.mult))
                split(m[1][:, k, :], m[2][:, k, :], m[0][:, k, :])

        def memory_out(mkt, mv):
            for k in range(2):
                give(V.tensor_copy(mkt[:, k, :], take(P, MEM)))
            for i in range(2):
                give(V.tensor_copy(mv[:, i, :], take(P, MH * MDH)))

        for n0, n1 in ((0, S), (S, TW)):
            give(V.tensor_copy(vr[0:NH, n0:n1], take(NH, n1 - n0)))
        n.tell(sem["vr_ready"])

        dve.wait_ge(sem["in_col"], 16)

        def arrived(k):
            if k % 2 == 0:
                dve.wait_ge(in_x[k // 2], 16)

        stage("mix_pre", arrived)
        r = slice(NOPE, P)
        dve.wait_ge(sem["in_pos"], 16)
        a0, a1, a2 = ang[r, 0, :], ang[r, 1, :], ang[r, 2, :]
        magic = 1.5 * 2.0 ** 23
        did(V.tensor_copy(a0, pos_i[r, :]))
        did(V.tensor_scalar(a0, a0, C("inv", p=r), None, ALU.mult))
        did(V.tensor_scalar(a1, a0, 1.0 / (2 * np.pi), C("quarter", p=r), ALU.mult, ALU.add))
        did(V.tensor_scalar(a1, a1, magic, None, ALU.add))
        did(V.tensor_scalar(a1, a1, magic, None, ALU.subtract))
        c1 = 6.28125
        c2 = 0.0019350051879882812
        c3 = 2 * np.pi - c1 - c2
        for part in (c1, c2, c3):
            did(V.scalar_tensor_tensor(a2, a1, -part, a0, ALU.mult, ALU.add))
            did(V.tensor_copy(a0, a2))
        did(V.tensor_scalar(a0, a0, C("halfpi", p=r), None, ALU.add))
        n.did(V.tensor_scalar(a0, a0, 3.1415925, -3.1415925, ALU.min, ALU.max), sem["angle_ready"])
        factor(rstd[:, :])
        did(V.memset(prod[:, 0:2], 0.0))
        for i in range(KC_):
            give(V.tensor_tensor(tmp[:, :], take(), rstd[:, :], ALU.mult))
            give(V.tensor_tensor(prod[:, 2:], take(), rstd[:, :], ALU.mult))
            did(V.tensor_tensor(prod[:, 2:], prod[:, 2:], tmp[:, :], ALU.mult))
            w = [C("conv_a", 3 * i + tap) for tap in range(3)]
            did(V.tensor_scalar(cv[:, :], prod[:, 2:], w[2], None, ALU.mult))
            did(V.scalar_tensor_tensor(cv[:, :], prod[:, 1:S + 1], w[1], cv[:, :], ALU.mult, ALU.add))
            did(V.scalar_tensor_tensor(cv[:, :], prod[:, 0:S], w[0], cv[:, :], ALU.mult, ALU.add))
            give(V.tensor_tensor(tmp[:, :], take(), rstd[:, :], ALU.mult))
            did(V.tensor_tensor(cv[:, :], cv[:, :], tmp[:, :], ALU.mult))
            split(yhi[:, i, :], ylo[:, i, :], cv[:, :])
        dve.wait_ge(sem["sine_ready"], 1)
        did(V.tensor_scalar(cs[r, :], cs[r, :], C("sign", p=r), None, ALU.mult))
        dve.wait_ge(sem["dist_out"], 16)
        for i in range(5):
            give(V.tensor_tensor(lat[:, i, :], take(), rstd[:, :], ALU.mult))
            n.tell(sem["src_ready"])
        give(V.tensor_tensor(kpe[r, :], take()[r, :], rstd[r, :], ALU.mult))
        did(V.tensor_tensor(kpe[r, :], kpe[r, :], cs[r, :], ALU.mult))

        def gate(i):
            give(V.tensor_tensor(sg[:, i, :], take(), rstd[:, :], ALU.mult))
            n.tell(sem["gate_in"])

        for i in range(4):
            gate(i)
        for first, count, gain in ((0, 3, "q_lat"), (3, 2, "kv_lat")):
            for k in range(count):
                add_square(k == 0)
            factor(rstd2[:, :])
            for k in range(count):
                did(V.scalar_tensor_tensor(lat[:, first + k, :], lat[:, first + k, :], C(gain, k),
                                           rstd2[:, :], ALU.mult, ALU.mult))
                split(lathi[:, first + k, :], latlo[:, first + k, :], lat[:, first + k, :])
        for i in range(4, 16):
            gate(i)
        rot, turned = slice(NOPE, QK), slice(QK, P)
        did(V.tensor_copy(tmp[rot, :], kpe[turned, :]))
        did(V.tensor_tensor(kpe[rot, :], kpe[rot, :], tmp[rot, :], ALU.add))
        for i in range(HA):
            did(V.tensor_copy(kf[rot, i, :], kpe[rot, :]))
        for i in range(HA):
            a = take()
            did(V.tensor_tensor(qf[rot, i, :], a[rot, :], cs[rot, :], ALU.mult))
            did(V.tensor_tensor(tmp[rot, :], a[turned, :], cs[turned, :], ALU.mult))
            did(V.tensor_tensor(qf[rot, i, :], qf[rot, i, :], tmp[rot, :], ALU.add))
            give(V.tensor_copy(qf[0:NOPE, i, :], a[0:NOPE, :]))
        for i in range(4):
            a = take()
            did(V.tensor_copy(kf[0:NOPE, 2 * i, :], a[0:NOPE, :]))
            give(V.tensor_copy(kf[0:NOPE, 2 * i + 1, :], a[NOPE:P, :]))
        for i in range(TT):
            give(V.tensor_copy(va[:, i, :], take()))
        n.tell(sem["qkv_ready"])
        for i in range(KD):
            dve.wait_ge(sem["sig_ready"], i + 1)
            give(V.tensor_tensor(sg[:, i, :], sg[:, i, :], take(), ALU.mult))
        dve.wait_ge(sem["in_chunk"], 16)
        softmaxes(list(latent_steps()), s_a)
        for i in range(KD):
            dve.wait_ge(sem["sig_ready"], KD + i + 1)
            give(V.tensor_tensor(tmp[:, :], sg[:, KD + i, :], take(), ALU.mult))
            did(V.tensor_tensor(tmp[:, :], tmp[:, :], sg[:, i, :], ALU.add))
            split(xhi[:, i, :], xlo[:, i, :], tmp[:, :])
        gather_down(y_o)
        factor(rstd[:, :])
        stage("ffn_pre", post_norm(y_o, "mix_post"))
        feed_forward("ffn0")
        dve.wait_ge(sem["in_p"], 16)
        for k in range(2):
            split(p_hi[:, k, :], p_lo[:, k, :], p_f[:, k, :])
        gather_down(y_d)
        factor(rstd[:, :])
        for k in range(KD):
            give(V.tensor_copy(e[:, k, :], take()))
        stage(None, post_norm(y_d, "ffn_post"), squares=False)
        memory_stage(mem1, "nmem0")
        for k in range(KD):
            dve.wait_ge(sem["ple_sig"], k + 1)
            take()
            give(V.tensor_tensor(e[:, k, :], e[:, k, :], gs[:, k % 2, :], ALU.mult))
            n.tell(sem["src_ready"])
            if k:
                add_square(k == 1)
        add_square(False)
        factor(rstd[:, :])
        stage("nmix0", post_norm(e, "ple_post"))

        memory_out(mk1, mv1)
        factor(rstd[:, :])
        factor(rstd_t[:, :])
        give(V.tensor_tensor(lr[0:GR, :], take(GR), rstd[0:GR, :], ALU.mult))
        n.tell(sem["lr_ready"])
        for i in range(GH):
            give(V.scalar_tensor_tensor(qg[0:GDK, i, :], take(GDK), GDK ** -0.5, rstd[0:GDK, :],
                                        ALU.mult, ALU.mult))
        for i in range(GH):
            give(V.tensor_tensor(kg[0:GDK, i, :], take(GDK), rstd[0:GDK, :], ALU.mult))
        for i in range(2):
            give(V.scalar_tensor_tensor(mq1[:, i, :], take(), MDH ** -0.5, rstd[:, :], ALU.mult, ALU.mult))
        for i in range(TT):
            give(V.tensor_tensor(xg[:, i, :], take(P, GH * GDK), row[:, 0:GH * GDK], ALU.add))
        n.tell(sem["gl_raw"])
        dve.wait_ge(sem["gl_ln"], 1)
        n.did(V.scalar_tensor_tensor(la[:, :, :].rearrange("p a b -> p (a b)"),
                                     xg[:, :, :].rearrange("p a b -> p (a b)"), 0.0,
                                     glt[:, :, :].rearrange("p a b -> p (a b)"), ALU.min, ALU.subtract),
              sem["la_ready"])
        dve.wait_ge(sem["in_masks"], 16)
        for lv in range(1, N_SUMS + 1):
            fb = f[lv % 2]
            for hd in range(GH):
                dve.wait_ge(sem["f_ready"], GH * (lv - 1) + hd + 1)
                if lv <= LEVELS:
                    half = 2 ** (lv - 1)

                    def part(x, late):
                        v = x[0:GDK, hd, :].rearrange("p (n b) -> p n b", b=2 * half)
                        return v[:, :, half:2 * half] if late else v[:, :, 0:half]
                    did(V.tensor_tensor(part(fb, True), part(fb, True), part(qg, True), ALU.mult))
                    n.did(V.tensor_tensor(part(fb, False), part(fb, False), part(kg, False), ALU.mult),
                          sem["g_ready"])
                elif lv == LEVELS + 1:
                    did(V.tensor_copy(decay[0:GDK, TT * hd:TT * hd + TT], fb[0:GDK, hd, P - 1:S:P]))
                    n.did(V.tensor_tensor(qg[0:GDK, hd, :], qg[0:GDK, hd, :], fb[0:GDK, hd, :], ALU.mult),
                          sem["g_ready"])
                else:
                    n.did(V.tensor_tensor(kg[0:GDK, hd, :], kg[0:GDK, hd, :], fb[0:GDK, hd, :], ALU.mult),
                          sem["g_ready"])
            if lv <= N_MASKS:
                mask = mk[:, lv - 1:lv, :].to_broadcast([P, TT, P])
                for hd in range(GH):
                    a = take().rearrange("p (a b) -> p a b", b=P)
                    if lv == 1:
                        give(V.tensor_tensor(at_[:, hd, :].rearrange("p (a b) -> p a b", b=P), a, mask, ALU.mult))
                    else:
                        give(V.tensor_tensor(tmp[:, :].rearrange("p (a b) -> p a b", b=P), a, mask, ALU.mult))
                        did(V.tensor_tensor(at_[:, hd, :], at_[:, hd, :], tmp[:, :], ALU.add))
            if lv <= 6:
                to = vg if lv <= 3 else gg
                c = (lv - 1) % 3 * 256
                for i in range(TT):
                    give(V.tensor_scalar(to[:, i, c:c + 256], take(P, 256), rstd_t[:, i:i + 1], None, ALU.mult))
                if lv == 6:
                    n.tell(sem["gates_raw"])
        for i in range(TT):
            give(V.tensor_copy(kout[:, i, :], take(P, GH * GDK)))
            n.tell(sem["kout_ready"])
        for i in range(TT):
            for hd in range(GH):
                vcols = slice(hd * GDV, (hd + 1) * GDV)
                give(V.tensor_copy(o_g[:, i, vcols], take(P, GDV)))
                did(V.tensor_tensor_reduce(tmp[:, 0:GDV], o_g[:, i, vcols], o_g[:, i, vcols], 1.0, 0.0,
                                           ALU.mult, ALU.add, osum[:, GH * i + hd:GH * i + hd + 1]))
                if i < TT - 1:
                    a = take(GDK, GDV)
                    if i == 0:
                        give(V.tensor_copy(st[0:GDK, hd, :], a))
                    else:
                        give(V.scalar_tensor_tensor(st[0:GDK, hd, :], st[0:GDK, hd, :],
                                                    decay[0:GDK, TT * hd + i:TT * hd + i + 1], a, ALU.mult, ALU.add))
                    n.tell(sem["st_ready"])
        n.tell(sem["osq_ready"])
        dve.wait_ge(sem["oroot_ready"], 1)
        ro = oroot[:, :]
        did(V.reciprocal(ro, ro))
        dve.wait_ge(sem["gates_ready"], 1)
        for i in range(TT):
            for hd in range(GH):
                vcols = slice(hd * GDV, (hd + 1) * GDV)
                did(V.scalar_tensor_tensor(o_g[:, i, vcols], o_g[:, i, vcols],
                                           ro[:, GH * i + hd:GH * i + hd + 1],
                                           row[:, ROW["onorm"]:ROW["onorm"] + GDV], ALU.mult, ALU.mult))
            n.did(V.tensor_tensor(o_g[:, i, :], o_g[:, i, :], gg[:, i, :], ALU.mult), sem["og_ready"])
        softmaxes(list(memory_steps(mq1, mk1, mv1)), s_1)
        for c in range(6):
            give(V.tensor_copy(tmp[:, :], take()))
            split(xhi[:, c, :], xlo[:, c, :], tmp[:, :])
        for k in range(KD):
            residual(k)
        stage("nffn1")
        feed_forward("ffn1")
        stage("nkv", residual)

        factor(rstd[:, :])
        factor(rstd_t[:, :])
        for j in range(2):
            for k in range(2):
                a = take()
                for g in range(2):
                    rr = slice(g * NDH, (g + 1) * NDH)
                    did(V.tensor_tensor(z[0:NDH, 2 * k + g, :], a[rr, :], rstd[rr, :], ALU.mult))
                    ins = V.tensor_tensor(z[NDH:P, 2 * k + g, 0:S - 1], a[rr, 1:], rstd[rr, 1:], ALU.mult)
                    if g == 0:
                        did(ins)
                    else:
                        give(ins)
            for part in range(2):
                l0, t0 = part * LP // 2, part * CMP_S
                win = z[:, :, t0:t0 + CMP_S * NCMP].rearrange("p g (c l) -> p l g c", l=CMP_S)[:, 0:CMP_S:2]
                did(V.tensor_tensor(zw[:, l0:l0 + LP // 2, :].rearrange("p l (g c) -> p l g c", g=NG), win,
                                    C(f"pos{j}", l0, LP // 2).unsqueeze(2).unsqueeze(3)
                                    .to_broadcast([P, LP // 2, NG, NCMP]), ALU.add))
            flat = "p a b -> p (a b)"
            split(zhi[j][:, :, :].rearrange(flat), zlo[j][:, :, :].rearrange(flat), zw[:, :, :].rearrange(flat))
        n.tell(sem["z_done"])
        for j in range(2):
            for k in range(2):
                give(V.tensor_tensor(kn[j][:, k, :], take(), rstd[:, :], ALU.mult))
        for j in range(2):
            for i in range(TT):
                give(V.tensor_scalar(vn[j][:, i, :], take(P, NG * NDH), rstd_t[:, i:i + 1], None, ALU.mult))
        nw = NG * NCMP
        for k in range(KD):
            add_square(k == 0, MEM)
        for j in range(2):
            give(V.tensor_scalar(hid[:, j, 0:nw], take(P, nw), C("cb1", j), None, ALU.add))
            n.tell(sem["hid_raw"])
        factor(rstd2[:, 0:MEM])
        for k in range(KD):
            did(V.scalar_tensor_tensor(mem2[0][:, k, :], mem2[0][:, k, :], C("nmem1", k), rstd2[:, 0:MEM],
                                       ALU.mult, ALU.mult))
            split(mem2[1][:, k, :], mem2[2][:, k, :], mem2[0][:, k, :])
        stage("nmix1", squares=False)
        memory_out(mk2, mv2)
        a = take(NDH, nw)
        for g in range(NG):
            rr = slice(g % 2 * NDH, g % 2 * NDH + NDH)
            ins = V.tensor_scalar(kc[rr, g // 2, 0:NCMP], a[:, g * NCMP:(g + 1) * NCMP],
                                  C("cb2", p=slice(0, NDH)), None, ALU.add)
            if g < NG - 1:
                did(ins)
            else:
                give(ins)
        a = take(NCMP, NG * NDH)
        give(V.tensor_tensor(vc[0:NCMP, :].rearrange("p (g d) -> p g d", d=NDH),
                             a.rearrange("p (g d) -> p g d", d=NDH),
                             row[0:NCMP, ROW["cb2r"]:ROW["cb2r"] + NDH].unsqueeze(1)
                             .to_broadcast([NCMP, NG, NDH]), ALU.add))
        for i in range(6):
            give(V.scalar_tensor_tensor(qn[:, i, :], take(), NDH ** -0.5, rstd[:, :], ALU.mult, ALU.mult))
        for i in range(2):
            give(V.scalar_tensor_tensor(mq2[:, i, :], take(), MDH ** -0.5, rstd[:, :], ALU.mult, ALU.mult))
        give(V.tensor_tensor(tmp[0:3 * NH, :], take(3 * NH), rstd[0:3 * NH, :], ALU.mult))
        n.tell(sem["gln_ready"])
        give(V.tensor_copy(gt[:, :, :].rearrange("p a b -> p (a b)"), take(P, TT * 3 * NH)))
        n.tell(sem["gates_raw"])
        dve.wait_ge(sem["gates_ready"], 2)
        dve.wait_ge(sem["in_toep"], 16)
        n.tell(sem["qkv_ready"])
        softmaxes(list(branch_steps()) + list(memory_steps(mq2, mk2, mv2)), s_2)
        for k in range(KD):
            residual(k)
        stage("nffn2")
        feed_forward("ffn2")
        for k in range(KD):
            residual(k)
            if k:
                add_square(k == 1)
        add_square(False)
        factor(rstd[:, :])
        for k in range(KD):
            n.did(V.scalar_tensor_tensor(h[:, k, :], h[:, k, :], C("final", k), rstd[:, :], ALU.mult,
                                         ALU.mult), sem["out_ready"])

    @block.scalar
    def _(act):
        n = Count(act)
        src = 0
        sqs = 0
        bc = 0
        steps_done = 0
        fed = 0
        A = nc.scalar

        def load(to, what, name):
            act.dma_start(to, what).then_inc(sem[name], 16)

        def did(ins):
            n.did(ins, sem["act_step"])

        def square(what):
            nonlocal sqs
            if sqs >= 2:
                act.wait_ge(sem["ss_added"], sqs - 1)
            n.did(A.activation(sq[:, sqs % 2, 0:what.shape[-1]], what, ACT.Square), sem["sq_ready"])
            sqs += 1

        def squares(tiles, arrived=None):
            nonlocal src
            for i, what in enumerate(tiles):
                if arrived:
                    arrived(i)
                else:
                    act.wait_ge(sem["src_ready"], src + 1)
                    src += 1
                square(what)

        def root(to, count):
            nonlocal bc
            act.wait_ge(sem["bc_ready"], bc + 1)
            n.did(A.activation(to, pv[:, 0:to.shape[-1]], ACT.Sqrt, scale=1.0 / count, bias=C("eps")),
                  sem["rs_ready"])
            bc += 1

        def feed_forward(which, func):
            nonlocal fed
            c0 = COL[which]
            per = {sem["a_ready"]: 4, sem["v_ready"]: 2}
            with act.Fori(0, KF_ // 2) as i:
                n.enter(i, per)
                for pair in range(2):
                    for half in range(2):
                        j = 2 * pair + half
                        w2, b = (col[:, bass.ds(i * 16 + (c0 + 8 * pair + 4 * half + x), 1)] for x in (2, 3))
                        act.wait_ge(sem["u_ready"], i * 4 + (4 * fed + j + 1))
                        n.did(A.activation(sq[:, half, :], u[:, half, 2:], ACT.Identity, scale=w2, bias=b),
                              sem["a_ready"])
                    act.wait_ge(sem["c_ready"], i * 4 + (4 * fed + 2 * pair + 1))
                    n.did(A.activation(sq[:, 0, :], sq[:, 0, :], func), sem["v_ready"])
            n.leave(KF_ // 2)
            fed += KF_ // 2

        def softmaxes(steps, s, pts):
            nonlocal steps_done
            b0 = steps_done

            def exps(i):
                w, j = steps[i], i % 2
                act.wait_ge(sem["s_ready"], b0 + i + 1)
                n.did(A.activation(s[:, j, 0:w["n"]], s[:, j, 0:w["n"]], ACT.Exp, scale=w["scale"],
                                   bias=small[:, 6 + j:7 + j], accum_out=small[:, 8 + j:9 + j]),
                      sem["p_ready"])

            def copy(i):
                w = steps[i]
                act.wait_ge(sem["t_ready"], b0 + i + 1)
                if i >= 2:
                    act.wait_ge(sem["pv_done"], b0 + i - 1)
                m = w["blocks"] * P
                n.did(A.activation(pts[0:w["width"], i % 2, 0:m], ptp[0:w["width"], 0:m], ACT.Copy),
                      sem["t_copied"])

            for i in range(len(steps) + 1):
                if i < len(steps):
                    exps(i)
                if i >= 1:
                    copy(i - 1)
            steps_done += len(steps)

        def tiles(x, count=KD):
            return [x[:, k, :] for k in range(count)]

        load(relv[0:BUCKETS + 1, 0:NH], rel, "in_rel")
        load(bk[0:BUCKETS + 1, :], buckets, "in_bk")
        load(col[:, :], cols, "in_col")
        load(const[:, :], consts, "in_const")
        load(row[:, :], rws, "in_row")
        load(pos_i[NOPE:P, :], positions, "in_pos")
        load(chunkm[:, :], chunk, "in_chunk")
        act.wait_ge(sem["vr_ready"], 1)
        act.dma_start(distances.rearrange("h (r n) -> h r n", n=TW),
                      vr[0:NH, :].unsqueeze(1).to_broadcast([NH, P, TW])).then_inc(sem["dist_out"], 16)

        act.wait_ge(sem["in_col"], 16)
        squares(tiles(h), lambda k: act.wait_ge(in_x[k // 2], 16))
        act.wait_ge(sem["angle_ready"], 1)
        n.did(A.activation(cs[NOPE:P, :], ang[NOPE:P, 0, :], ACT.Sin), sem["sine_ready"])
        root(rstd[:, :], D)
        squares([lat[:, k, :] for k in range(3)])
        root(rstd2[:, :], Q_LORA)
        squares([lat[:, k, :] for k in range(3, 5)])
        root(rstd2[:, :], KV_LORA)
        for i in range(2 * KD):
            act.wait_ge(sem["gate_in"], i + 1)
            n.did(A.activation(sg[:, i, :], sg[:, i, :], ACT.Sigmoid), sem["sig_ready"])
        softmaxes(list(latent_steps()), s_a, pt_a)
        squares(tiles(y_o))
        root(rstd[:, :], D)
        squares(tiles(h))
        root(rstd[:, :], D)
        feed_forward("ffn0", ACT.Gelu_apprx_tanh)
        act.wait_ge(sem["acc_ready"], mark["up0"])
        load(p_f[:, :, :], p_t, "in_p")
        squares(tiles(y_d))
        act.wait_ge(sem["acc_ready"], mark["down0"])
        load(mem1[0][:, :, :], mem_t, "in_mem1")
        load(dm[:, :, :], sums, "in_sums")
        load(mk[:, :, :], masks, "in_masks")
        load(wg[0:GR, :], wgate, "in_wg")
        root(rstd[:, :], D)
        src += KD
        squares(tiles(mem1[0]), lambda k: act.wait_ge(sem["in_mem1"], 16))
        root(rstd2[:, 0:MEM], D)
        for k in range(KD + 1):
            if k < KD:
                tile = mark["ple"] + k
                act.wait_ge(sem["acc_ready"], tile + 1)
                if k >= 2:
                    act.wait_ge(sem["acc_free"], tile - 1)
                n.did(A.activation(gs[:, k % 2, :], acc[:, tile % 4, :], ACT.Sigmoid), sem["ple_sig"])
            if k:
                squares([e[:, k - 1, :]])
        root(rstd[:, :], D)
        squares(tiles(h))
        root(rstd[:, :], D)
        root(rstd_t[:, :], D)

        act.wait_ge(sem["gl_raw"], 1)
        flat = "p a b -> p (a b)"
        did(A.activation(glt[:, :, :].rearrange(flat), xg[:, :, :].rearrange(flat), ACT.Abs))
        did(A.activation(glt[:, :, :].rearrange(flat), glt[:, :, :].rearrange(flat), ACT.Exp, scale=-1.0))
        n.did(A.activation(glt[:, :, :].rearrange(flat), glt[:, :, :].rearrange(flat), ACT.Ln, bias=1.0),
              sem["gl_ln"])
        for lv in range(1, N_SUMS + 1):
            for hd in range(GH):
                act.wait_ge(sem["e_ready"], GH * (lv - 1) + hd + 1)
                if lv >= 3:
                    act.wait_ge(sem["acc_ready"], mark["pairs", lv - 2])
                n.did(A.activation(f[lv % 2][0:GDK, hd, :], ebank[hd][0:GDK, :], ACT.Exp), sem["f_ready"])
                n.tell(sem["e_free"])
        act.wait_ge(sem["gates_raw"], 1)
        n.did(A.activation(gg[:, :, :].rearrange(flat), gg[:, :, :].rearrange(flat), ACT.Silu),
              sem["gates_ready"])
        act.wait_ge(sem["osq_ready"], 1)
        n.did(A.activation(oroot[:, :], osum[:, :], ACT.Sqrt, scale=1.0 / GDV, bias=C("eps")),
              sem["oroot_ready"])
        softmaxes(list(memory_steps(mq1, mk1, mv1)), s_1, pt_1)
        squares(tiles(h))
        root(rstd[:, :], D)
        feed_forward("ffn1", ACT.Silu)
        squares(tiles(h))
        root(rstd[:, :], D)
        root(rstd_t[:, :], D)

        act.wait_ge(sem["z_done"], 1)
        load(mem2[0][:, :, :], mem_t, "in_mem2")
        squares(tiles(mem2[0]), lambda k: act.wait_ge(sem["in_mem2"], 16))
        nw = NG * NCMP
        for j in range(2):
            act.wait_ge(sem["hid_raw"], j + 1)
            n.did(A.activation(hid[:, j, 0:nw], hid[:, j, 0:nw], ACT.Silu), sem["hid_ready"])
        act.wait_ge(sem["acc_ready"], mark["windows"])
        act.wait_ge(sem["dist_out"], 16)
        width = TW - 1
        act.dma_start(toep[:, :, :], distances[:, P - 1:P - 1 + P * width]
                      .rearrange("h (p n) -> p h n", n=width)[:, :, 0:S]).then_inc(sem["in_toep"], 16)
        root(rstd2[:, 0:MEM], D)
        act.wait_ge(sem["gates_raw"], 2)
        n.did(A.activation(gt[:, :, :].rearrange(flat), gt[:, :, :].rearrange(flat), ACT.Sigmoid),
              sem["gates_ready"])
        softmaxes(list(branch_steps()) + list(memory_steps(mq2, mk2, mv2)), s_2, pt_2)
        squares(tiles(h))
        root(rstd[:, :], D)
        feed_forward("ffn2", ACT.Silu)
        squares(tiles(h))
        root(rstd[:, :], D)

    ctx.close()



def feature_major(x):
    x = np.asarray(x, np.float32)
    return np.ascontiguousarray(x.T.reshape(-1, P, x.shape[0]).transpose(1, 0, 2))


def kernel(**inputs):
    import concourse.bacc as bacc
    from concourse.bass_utils import run_bass_kernel_spmd as run

    a = {k: np.asarray(v) for k, v in inputs.items()}
    sums, masks = decay_tables()
    arrays = {
        "weights": weight_units(a),
        "x_t": feature_major(a["x"][0]),
        "p_t": feature_major(a["p"][0, 0]),
        "mem_t": feature_major(a["mem_2"][0]),
        "cols": columns(a),
        "rws": rows(a),
        "positions": np.ascontiguousarray(np.broadcast_to(a["positions"].astype(np.int32), (NOPE, S))),
        "rel": np.concatenate([a["rel_bias_2"], np.ones((1, NH), np.float32)]),
        "wgate": np.ascontiguousarray(a["gla_w_gate_up_2"][0]),
        "consts": fixed(),
        "chunk": chunk_mask(),
        "buckets": bucket_table(),
        "sums": sums.reshape(P, N_SUMS, P),
        "masks": masks.reshape(P, N_MASKS, P),
    }
    nc = bacc.Bacc("TRN2", target_bir_lowering=False, num_devices=1)
    args = [nc.dram_tensor(f"in_{k}", v.shape, mybir.dt.from_np(v.dtype), kind="ExternalInput").ap()
            for k, v in arrays.items()]
    args.append(nc.dram_tensor("out_t", (P, KD, S), F32, kind="ExternalOutput").ap())
    build_program(nc, *args)
    r = run(nc, [{f"in_{k}": v for k, v in arrays.items()}], core_ids=[0])
    y = r.results[0]["out_t"]
    return np.ascontiguousarray(y.transpose(2, 1, 0).reshape(1, S, D))
```

```python
from contextlib import ExitStack

import numpy as np

import concourse.bass as bass
from concourse import mybir

P = 128
S = 512
TT = S // P
D = 1024
KD = D // P
EPS = 1e-6
NEG = -1e30
CONV = 512
KC_ = CONV // P
Q_LORA, KV_LORA = 384, 256
HA, NOPE, ROPE, VD = 8, 64, 32, 64
QK = NOPE + ROPE
ROPE_THETA = 10000.0
F_DIM = 2816
KF_ = F_DIM // P
PLE = 256
MEM = 256
MH, MDH = 4, 64
GH, GDK, GDV, GR = 4, 96, 192, 16
NH, NG, NDH = 12, 4, 64
REP = NH // NG
CMP_B, CMP_S, CMP_H = 32, 16, 128
NCMP = (S - CMP_B) // CMP_S + 1
LP = CMP_B // 2
BUCKETS, MAX_DIST = 32, 128
RING = 4
UNIT = 1024
LEVELS = 7
S_CMP = (1 + 2 + 3 + 4) * P
SW = S_CMP + P
S_BUFS, PT_BUFS = 3, 4
TW = 640

ALU = mybir.AluOpType
ACT = mybir.ActivationFunctionType
F32 = mybir.dt.float32
F32R = mybir.dt.float32r
I32 = mybir.dt.int32
AX = mybir.AxisListType.X

NSA_ORDER = [(REP * (2 * t + g) + r) for t in range(NG // 2) for r in range(REP) for g in range(2)]



def _pack(blocks):
    units, at = [], UNIT
    for b in blocks:
        if at + b.shape[1] > UNIT:
            units.append(np.zeros((P, UNIT), np.float32))
            at = 0
        units[-1][:b.shape[0], at:at + b.shape[1]] = b
        at += b.shape[1]
    return units


def _cols(w, first, n=P):
    out = []
    for k in range(-(-w.shape[0] // P)):
        b = np.zeros((P, P), np.float32)
        rows = w[k * P:(k + 1) * P, first:first + n]
        b[:rows.shape[0], :rows.shape[1]] = rows
        out.append(b)
    return out


def _moving(w, first, n):
    return [w[k * P:(k + 1) * P, first:first + n] for k in range(w.shape[0] // P)]


def weight_units(a):
    u = []

    def tiles(w, firsts, n=P):
        u.extend(_pack([b for f in firsts for b in _cols(w, f, n)]))

    def ffn(up, down):
        tiles(up, [f + h for f in range(0, F_DIM, P) for h in (0, F_DIM)])
        for f in range(0, D, P):
            u.extend(_pack(_cols(down, f)))

    def memory(w):
        tiles(w, [0, P])
        u.extend(_pack(_moving(w, MH * MDH, MH * MDH)))

    w = a["w_in"][0]
    c = CONV
    tiles(w, [x + i * P for i in range(KC_) for x in (c, 2 * c, 0)])
    at = 3 * CONV
    tiles(w, range(at, at + Q_LORA + KV_LORA, P))
    at += Q_LORA + KV_LORA
    r = w[:, at:at + ROPE]
    h = ROPE // 2
    turned = np.concatenate([r[:, h:], r[:, :h]], 1)
    tiles(np.concatenate([np.zeros((D, NOPE), np.float32), r, turned], 1), [0])
    at += ROPE
    tiles(w, range(at, at + 2 * D, P))
    q = a["w_q_up"][0].reshape(Q_LORA, HA, QK)
    q = np.concatenate([q, q[:, :, NOPE + h:], q[:, :, NOPE:NOPE + h]], 2).reshape(Q_LORA, HA * P)
    tiles(q, range(0, HA * P, P))
    kv = a["w_kv_up"][0].reshape(KV_LORA, HA, NOPE + VD)
    tiles(kv[:, :, :NOPE].reshape(KV_LORA, -1), range(0, HA * NOPE, P))
    u.extend(_pack(_moving(kv[:, :, NOPE:].reshape(KV_LORA, -1), 0, HA * VD)))
    tiles(a["w_a_out"][0], range(0, D, P))
    tiles(a["w_b_out"][0], range(0, D, P))
    tiles(a["w_o"][0], range(0, D, P))
    ffn(a["w_ffn_up"][0], a["w_ffn_down"][0])
    tiles(a["w_ple_proj"][0], range(0, D, P))
    tiles(a["w_ple_gate"][0], range(0, D, P))

    memory(a["w_mem_kv_2"][0])
    w = a["gla_w_in_2"][0]
    nk, nv = GH * GDK, GH * GDV
    tiles(w, [2 * nk + 2 * nv], GR)
    tiles(w, range(0, 2 * nk, GDK), GDK)
    tiles(w, [2 * nk + 2 * nv + GR + i * P for i in range(2)])
    for first in range(2 * nk, 2 * nk + 2 * nv, 256):
        u.extend(_pack(_moving(w, first, 256)))
    tiles(a["w_out_2"][0], range(0, D, P))
    ffn(a["w_up_2"][0], a["w_down_2"][0])

    w = a["w_kv_shared_2"]
    nk = NG * NDH
    tiles(w, [j * nk + i * P for j in (0, 1, 2, 4) for i in range(2)])
    for j in (3, 5):
        u.extend(_pack(_moving(w, j * nk, nk)))
    for j in range(2):
        tiles(a["cmp_w1_2"][j], [0])
    memory(a["w_mem_kv_2"][1])
    w = a["nsa_w_in_2"][0]
    nq = NH * NDH
    heads = [w[:, NDH * x:NDH * (x + 1)] for x in NSA_ORDER]
    tiles(np.concatenate(heads, 1), range(0, nq, P))
    tiles(w, [nq + 3 * NH + i * P for i in range(2)])
    tiles(w, [nq], 3 * NH)
    tiles(a["w_out_2"][1], range(0, D, P))
    ffn(a["w_up_2"][1], a["w_down_2"][1])
    return np.stack(u)


def _column_layout():
    at, where = 0, {}
    for name, n in [("mix_pre", 8), ("q_lat", 3), ("kv_lat", 2), ("mix_post", 8), ("ffn_pre", 8),
                    ("ffn_post", 8), ("ple_post", 8), ("conv_a", 3 * KC_), ("ffn0", 8 * KF_),
                    ("ffn1", 8 * KF_), ("ffn2", 8 * KF_), ("nmix0", 8), ("nmix1", 8), ("nmem0", 8),
                    ("nmem1", 8), ("nffn1", 8), ("nffn2", 8), ("nkv", 8), ("final", 8), ("cb1", 2),
                    ("cb2", 1), ("pos0", LP), ("pos1", LP), ("w2_0", NDH), ("w2_1", NDH),
                    ("eps", 1), ("inv", 1), ("quarter", 1), ("halfpi", 1), ("sign", 1), ("valid", 1)]:
        where[name] = at
        at += n
    return where, at


COL, N_COL = _column_layout()
ROW = {"bgate": 0, "onorm": GH * GDK, "cb2r": GH * GDK + GDV}
N_ROW = GH * GDK + GDV + NDH


def columns(a):
    out = np.zeros((P, N_COL), np.float32)

    def put(name, v, step=1, shift=0):
        m = np.asarray(v, np.float32).reshape(-1, P).T
        at = COL[name] + shift
        out[:, at:at + step * m.shape[1]:step] = m

    put("mix_pre", a["g_mix_pre"][0])
    put("q_lat", a["g_q_lat"][0])
    put("kv_lat", a["g_kv_lat"][0])
    put("mix_post", a["g_mix_post"][0])
    put("ffn_pre", a["g_ffn_pre"][0])
    put("ffn_post", a["g_ffn_post"][0])
    put("ple_post", a["g_ple_post"][0])
    for j in range(3):
        put("conv_a", a["conv_a_w"][0, j], 3, j)
    for name, w, b in (("ffn0", a["conv_ffn_w"][0], a["b_ffn_conv"][0]),
                       ("ffn1", a["conv_w_2"][0], a["conv_b_2"][0]),
                       ("ffn2", a["conv_w_2"][1], a["conv_b_2"][1])):
        for half in range(2):
            part = slice(half * F_DIM, (half + 1) * F_DIM)
            for j in range(3):
                put(name, w[j, part], 8, 4 * half + j)
            put(name, b[part], 8, 4 * half + 3)
    for i in range(2):
        put(f"nmix{i}", a["norm_mix_2"][i])
        put(f"nmem{i}", a["norm_mem_2"][i])
        put(f"nffn{i + 1}", a["norm_ffn_2"][i])
        out[:, COL["cb1"] + i] = a["cmp_b1_2"][i]
        at = COL[f"pos{i}"]
        out[:, at:at + LP] = a["cmp_pos_2"][i].reshape(LP, P).T
        at = COL[f"w2_{i}"]
        out[:, at:at + NDH] = a["cmp_w2_2"][i]
    put("nkv", a["kv_norm_2"])
    put("final", a["final_norm_2"])
    out[:NDH, COL["cb2"]] = a["cmp_b2_2"][0]
    out[NDH:, COL["cb2"]] = a["cmp_b2_2"][0]
    half = ROPE // 2
    inv = (1.0 / (np.float32(ROPE_THETA) ** (np.arange(half, dtype=np.float32)
                                              * np.float32(2.0 / ROPE)))).astype(np.float32)
    out[NOPE:, COL["inv"]] = np.tile(inv, 4)
    out[:, COL["eps"]] = EPS
    out[NOPE:NOPE + ROPE, COL["quarter"]] = 0.25
    out[NOPE:NOPE + ROPE, COL["halfpi"]] = np.pi / 2
    out[:, COL["sign"]] = 1.0
    out[NOPE + ROPE:NOPE + ROPE + half, COL["sign"]] = -1.0
    out[CMP_B - 1:, COL["valid"]] = 1.0
    return out


def rows(a):
    r = np.concatenate([a["gla_b_gate_2"][0], a["gla_out_norm_2"][0], a["cmp_b2_2"][1]])
    return np.ascontiguousarray(np.broadcast_to(r, (P, N_ROW)))


def bucket_table():
    out = np.zeros((BUCKETS + 1, TW), np.float32)
    exact = BUCKETS // 2
    for n in range(TW):
        d = S - 1 - n
        if d < 0:
            out[BUCKETS, n] = NEG
            continue
        large = exact + int(np.log(max(d, 1) / exact) / np.log(MAX_DIST / exact) * (BUCKETS - exact))
        out[d if d < exact else min(large, BUCKETS - 1), n] = 1.0
    return out


CONST = {"ident": 0, "ones": P}
N_CONST = 2 * P


def fixed():
    out = np.zeros((P, N_CONST), np.float32)
    out[:, :P] = np.eye(P)
    out[:, P:2 * P] = 1.0
    return out


def chunk_mask():
    out = np.zeros((P, S), np.float32)
    out[:64, S - 64:] = NEG
    return out


def decay_tables():
    t, i = np.arange(P)[:, None], np.arange(P)[None, :]
    sums, masks = [], [np.eye(P)]
    for lv in range(1, LEVELS + 1):
        b = 2 ** lv
        mid = i // b * b + b // 2 - 1
        late = i > mid
        sums.append(np.where(late, (t > mid) & (t <= i), (t > i) & (t <= mid)))
        j = np.arange(P)[:, None]
        masks.append((j // b == i // b) & (j % b < b // 2) & (i % b >= b // 2))
    sums += [t <= i, t > i]
    return (np.concatenate(sums, 1).astype(np.float32) / 16.0,
            np.concatenate(masks, 1).astype(np.float32))


N_SUMS, N_MASKS = LEVELS + 2, LEVELS + 1

U_FFN_UP, U_FFN_DOWN = 2 * KF_, 3 * KD
N_UNITS = (34 + 3 + 2 + 4 + 4 + 8 + U_FFN_UP + U_FFN_DOWN + 2 + 8
           + 4 + 11 + 12 + 8 + U_FFN_UP + U_FFN_DOWN
           + 8 + 4 + 4 + 4 + 9 + 8 + U_FFN_UP + U_FFN_DOWN)


class Count:

    def __init__(self, eng):
        self.eng, self.n, self.loop = eng, {}, None

    def did(self, ins, sem, wait=True):
        ins.then_inc(sem, 1)
        self.n[sem] = self.n.get(sem, 0) + 1
        if wait:
            self.eng.wait_ge(sem, self.at(sem))

    def tell(self, sem):
        self.eng.sem_inc(sem, 1)
        self.n[sem] = self.n.get(sem, 0) + 1

    def at(self, sem):
        n = self.n.get(sem, 0)
        if self.loop is None:
            return n
        i, start, per = self.loop
        return i * per[sem] + n if sem in per else n

    def enter(self, i, per):
        self.loop = (i, dict(self.n), per)

    def leave(self, turns):
        _, start, per = self.loop
        for sem, n in self.n.items():
            made = n - start.get(sem, 0)
            assert made == per.get(sem, 0), (sem.name, made)
            self.n[sem] = start.get(sem, 0) + turns * made
        self.loop = None


def build_program(nc, weights, x_t, p_t, mem_t, cols, rws, positions, rel, wgate, consts, chunk, buckets,
                  sums, masks, out):
    ctx = ExitStack()
    base = [17408]

    def fix(name, shape, dt=F32):
        t = nc.alloc_sbuf_tensor_at(name, shape, dt, offset=base[0])
        base[0] += -(-int(np.prod(shape[1:])) * 4 // 32) * 32
        return t

    wraw = fix("wraw", [P, RING, UNIT])
    whi = fix("whi", [P, RING, UNIT], F32R)
    wlo = fix("wlo", [P, RING, UNIT], F32R)
    h = fix("h", [P, KD, S])
    x_at = base[0]
    xhi = fix("xhi", [P, KD, S], F32R)
    xlo = fix("xlo", [P, KD, S], F32R)
    col = fix("col", [P, N_COL])
    row = fix("row", [P, N_ROW])
    const = fix("const", [P, N_CONST])
    rstd = fix("rstd", [P, S])
    u = fix("u", [P, 2, S + 2])
    rstd2 = nc.alloc_sbuf_tensor_at("rstd2", [P, S], F32, offset=base[0] - 4128)
    tmp = nc.alloc_sbuf_tensor_at("tmp", [P, S], F32, offset=base[0] - 2048)
    sqsum = fix("sqsum", [P, S])
    sq = fix("sq", [P, 2, S])
    rstd_t = fix("rstd_t", [P, 4])
    stat = fix("stat", [P, 2, 4, 8])
    decay = fix("decay", [P, GH * TT])
    osum = fix("osum", [P, GH * TT])
    oroot = fix("oroot", [P, GH * TT])
    arena = base[0]
    KB = 1024

    def put(name, shape, at, dt=F32):
        assert arena + at + int(np.prod(shape[1:])) * 4 <= 229344, (name, arena, at)
        return nc.alloc_sbuf_tensor_at(name, shape, dt, offset=arena + at)

    fhi = put("fhi", [P, KF_, S], 0, F32R)
    flo = put("flo", [P, KF_, S], 44 * KB, F32R)
    sg = put("sg", [P, 2 * KD, S], 0)
    lat = put("lat", [P, 5, S], 32 * KB)
    lathi = put("lathi", [P, 5, S], 42 * KB, F32R)
    latlo = put("latlo", [P, 5, S], 52 * KB, F32R)
    yhi = put("yhi", [P, KC_, S], 62 * KB, F32R)
    ylo = put("ylo", [P, KC_, S], 70 * KB, F32R)
    va = put("va", [P, TT, HA * VD], 78 * KB)
    cs = put("cs", [P, S], 86 * KB)
    kpe = put("kpe", [P, S], 84 * KB)
    chunkm = put("chunkm", [P, S], 88 * KB)
    prod = put("prod", [P, S + 2], 78 * KB)
    cv = put("cv", [P, S], 80 * KB + 64)
    pos_i = nc.alloc_sbuf_tensor_at("pos_i", [P, S], I32, offset=arena + 32 * KB)
    ang = put("ang", [P, 3, S], 34 * KB)
    relv = put("relv", [P, 16], 42 * KB)
    bk = put("bk", [P, TW], 42 * KB + 64)
    vr = put("vr", [P, TW], 45 * KB)
    s_a = put("s_a", [P, S_BUFS, SW], 32 * KB)
    pt_a = put("pt_a", [P, PT_BUFS, S], 50 * KB)
    qf = nc.alloc_sbuf_tensor_at("qf", [P, HA, S], F32, offset=x_at)
    kf = nc.alloc_sbuf_tensor_at("kf", [P, HA, S], F32, offset=x_at + 16 * KB)
    y_o = put("y_o", [P, KD, S], 32 * KB)
    y_d = nc.alloc_sbuf_tensor_at("y_d", [P, KD, S], F32, offset=x_at + 16 * KB)
    p_f = nc.alloc_sbuf_tensor_at("p_f", [P, 2, S], F32, offset=x_at)
    p_hi = nc.alloc_sbuf_tensor_at("p_hi", [P, 2, S], F32R, offset=x_at + 4 * KB)
    p_lo = nc.alloc_sbuf_tensor_at("p_lo", [P, 2, S], F32R, offset=x_at + 8 * KB)
    e = put("e", [P, KD, S], 0)
    gs = put("gs", [P, 2, S], 40 * KB)
    qg = put("qg", [P, GH, S], 0)
    kg = put("kg", [P, GH, S], 8 * KB)
    vg = put("vg", [P, TT, GH * GDV], 16 * KB)
    gg = put("gg", [P, TT, GH * GDV], 28 * KB)
    la = put("la", [P, TT, GH * GDK], 40 * KB)
    kout = put("kout", [P, TT, GH * GDK], 40 * KB)
    f = [put(f"f{i}", [P, GH, S], (46 + 8 * i) * KB) for i in range(2)]
    xg = put("xg", [P, TT, GH * GDK], 54 * KB)
    at_ = put("at_", [P, GH, S], 62 * KB)
    dm = put("dm", [P, N_SUMS, P], 70 * KB)
    mk = put("mk", [P, N_MASKS, P], 75 * KB)
    mq1 = put("mq1", [P, 2, S], 79 * KB)
    mk1 = put("mk1", [P, 2, MEM], 83 * KB)
    mv1 = put("mv1", [P, 2, MH * MDH], 85 * KB)
    st = put("st", [P, GH, GDV], 87 * KB)
    lr = put("lr", [P, S], 62 * KB)
    wg = put("wg", [P, GH * GDK], 64 * KB)
    glt = put("glt", [P, TT, GH * GDK], 46 * KB)
    o_g = put("o_g", [P, TT, GH * GDV], 46 * KB)
    s_1 = put("s_1", [P, S_BUFS, SW], 0)
    pt_1 = put("pt_1", [P, PT_BUFS, S], 62 * KB)
    mem1 = [put("mem1", [P, KD, MEM], 16 * KB), put("mem1hi", [P, KD, MEM], 24 * KB, F32R),
            put("mem1lo", [P, KD, MEM], 32 * KB, F32R)]
    qn = put("qn", [P, 6, S], 0)
    toep = put("toep", [P, NH, S], 12 * KB)
    kn = [put("ks", [P, 2, S], 36 * KB), put("kw", [P, 2, S], 40 * KB)]
    vn = [put("vs", [P, TT, NG * NDH], 44 * KB), put("vw", [P, TT, NG * NDH], 48 * KB)]
    kc = put("kc", [P, 2, 32], 52 * KB)
    vc = put("vc", [P, NG * NDH], 52 * KB + 256)
    gt = put("gt", [P, TT, 3 * NH], 52 * KB + 1280)
    mk2 = put("mk2", [P, 2, MEM], 54 * KB)
    mv2 = put("mv2", [P, 2, MH * MDH], 56 * KB)
    mq2 = put("mq2", [P, 2, S], 58 * KB)
    s_2 = put("s_2", [P, S_BUFS, SW], 62 * KB)
    pt_2 = put("pt_2", [P, PT_BUFS, S], 79 * KB)
    z = put("z", [P, NG, S], 58 * KB)
    zw = put("zw", [P, LP, NG * NCMP], 70 * KB)
    zhi = [put(f"zhi{j}", [P, LP, NG * NCMP], 16 * j * KB, F32R) for j in range(2)]
    zlo = [put(f"zlo{j}", [P, LP, NG * NCMP], (8 + 16 * j) * KB, F32R) for j in range(2)]
    hid = put("hid", [P, 2, P], 66 * KB)
    mem2 = [put("mem2", [P, KD, MEM], 58 * KB), put("mem2hi", [P, KD, MEM], 78 * KB, F32R),
            put("mem2lo", [P, KD, MEM], 70 * KB, F32R)]

    acc = ctx.enter_context(nc.psum_tensor("acc", [P, 4, S], F32))
    sc = ctx.enter_context(nc.psum_tensor("sc", [P, 2, S], F32))
    ptp = ctx.enter_context(nc.psum_tensor("ptp", [P, S], F32))
    pv = ctx.enter_context(nc.psum_tensor("pv", [P, S], F32))
    pvs = [ptp[:, :], pv[:, :]]
    ebank = [sc[:, 0, :], sc[:, 1, :], ptp[:, :], pv[:, :]]
    distances = nc.dram_tensor("distances", [NH, P * TW], F32, kind="Internal").ap()

    ident, ones = const[:, 0:P], const[:, P:2 * P]

    def C(name, i=0, n=1, p=slice(None)):
        return col[p, COL[name] + i:COL[name] + i + n]

    def plain(ap):
        return ap.bitcast(F32)

    names = ("w_open w_split out_ready out_done w_used w_hi acc_free x_ready acc_ready ss_added rs_ready e_free "
             "o_free bc_ready sc_free sc_ready pn_ready t_copied t_ready pv_done in_rel in_bk in_const "
             "qkv_ready lr_ready in_wg in_sums la_ready e_ready g_ready kout_ready st_ready og_ready "
             "hid_ready gln_ready in_toep dve_step sq_ready src_ready u_ready c_ready a_ready v_ready "
             "s_ready p_ready vr_ready in_col in_pos angle_ready sine_ready dist_out gate_in sig_ready "
             "in_chunk in_p ple_sig gl_raw gl_ln in_masks f_ready gates_raw osq_ready oroot_ready "
             "gates_ready z_done hid_raw act_step in_row in_mem1 in_mem2").split()
    sem = {n: ctx.enter_context(nc.semaphore(n)) for n in names}
    loaded = [ctx.enter_context(nc.semaphore(f"w_loaded{j}")) for j in range(RING)]
    in_x = [ctx.enter_context(nc.semaphore(f"in_x{j}")) for j in range(4)]
    mark = {}

    def causal_wave(q, k, bias, v, dest, **more):
        offs = [sum(range(i + 1)) * P for i in range(TT)]
        items = [dict(bank=i, col=0, q=q(i), k=k(slice(0, (i + 1) * P)), n=(i + 1) * P,
                      bias=bias[:, S - (i + 1) * P:S], off=offs[i]) for i in range(TT)]
        turns = [dict(width=P, first=b, v=v(b), src=[offs[i] + b * P for i in range(b, TT)])
                 for b in range(TT)]
        return dict(items=items, turns=turns, dest=dest, scale=1.0, gates=[], opens=True, closes=True) | more

    def latent_waves():
        for hd in range(HA):
            yield causal_wave(lambda i: qf[0:QK, hd, i * P:(i + 1) * P], lambda w: kf[0:QK, hd, w], chunkm,
                              lambda b: va[:, b, hd * VD:(hd + 1) * VD],
                              (yhi, ylo, hd // 2, hd % 2 * VD), scale=QK ** -0.5)

    def memory_waves(mq, mkt, mv):
        for hd in range(MH):
            p = slice(hd % 2 * MDH, hd % 2 * MDH + MDH)
            items = [dict(bank=i, col=0, q=mq[p, hd // 2, i * P:(i + 1) * P], k=mkt[p, hd // 2, :], n=MEM,
                          bias=None, off=MEM * i) for i in range(TT)]
            turns = [dict(width=P, first=0, v=mv[:, b, hd * MDH:(hd + 1) * MDH],
                          src=[MEM * i + b * P for i in range(TT)]) for b in range(MEM // P)]
            yield dict(items=items, turns=turns, dest=(xhi, xlo, 6 + hd // 2, hd % 2 * MDH), scale=1.0,
                       gates=[], opens=True, closes=True)

    def branch_waves():
        for hd in range(NH):
            g, r = hd // REP, hd % REP
            p = slice(g % 2 * NDH, g % 2 * NDH + NDH)
            vcols = slice(g * NDH, (g + 1) * NDH)

            def q(i):
                return qn[p, g // 2 * REP + r, i * P:(i + 1) * P]

            for b in range(2):
                w = causal_wave(q, lambda keys: kn[b][p, g // 2, keys], toep[:, hd, :],
                                lambda kb: vn[b][:, kb, vcols], (xhi, xlo, hd // 2, hd % 2 * NDH),
                                opens=b == 0, closes=b == 1)
                w["gates"] = [(0, gt[:, :, 3 * hd + 1 + b])]
                if b == 0:
                    for i in range(TT):
                        n = min(NCMP, 7 + 8 * i)
                        first = S - P + CMP_B - 1 - P * i
                        w["items"].insert(i + 1, dict(
                            bank=0, col=P + 32 * i, q=q(i), k=kc[p, g // 2, 0:n], n=n,
                            bias=toep[:, hd, first:first + CMP_S * (n - 1) + 1:CMP_S], off=S_CMP + 32 * i))
                    w["turns"].append(dict(width=32, first=0, v=vc[0:32, vcols],
                                           src=[S_CMP + 32 * i for i in range(TT)]))
                    w["gates"] = [(1, gt[:, :, 3 * hd]), (5, gt[:, 1:TT, 3 * hd + 1]), (0, gt[:, 0:1, 3 * hd + 1])]
                    w["valid"] = 1
                yield w

    block = ctx.enter_context(nc.Block(no_gpsimd_drain=False))

    @block.sync
    def _(sp):
        for j in range(4):
            sp.dma_start(h[:, 2 * j:2 * j + 2, :], x_t[:, 2 * j:2 * j + 2, :]).then_inc(in_x[j], 16)

        def load(unit, j):
            sp.dma_start(wraw[:, j, :], weights[unit]).then_inc(loaded[j], 16)

        for j in range(RING):
            load(j, j)
        with sp.Fori(1, N_UNITS // RING) as i:
            for j in range(RING):
                sp.wait_ge(sem["w_split"], i * RING + (j - RING + 1))
                load(i * RING + j, j)
        for unit in range(N_UNITS // RING * RING, N_UNITS):
            sp.wait_ge(sem["w_split"], unit - RING + 1)
            load(unit, unit % RING)
        for k in range(KD):
            sp.wait_ge(sem["out_ready"], k + 1)
            sp.dma_start(out[:, k, :], h[:, k, :]).then_inc(sem["out_done"], 16)
        sp.wait_ge(sem["out_done"], 16 * KD)

    @block.gpsimd
    def _(pool):
        def split(unit, j, turn, used):
            pool.wait_ge(loaded[j], turn)
            if used is not None:
                pool.wait_ge(sem["w_used"], used)
            pool.sem_inc(sem["w_open"], 1)
            nc.gpsimd.tensor_scalar(whi[:, j, :], wraw[:, j, :], 1.0, 1.0, ALU.mult, ALU.mult).then_inc(sem["w_hi"], 1)
            pool.wait_ge(sem["w_hi"], unit + 1)
            nc.gpsimd.tensor_tensor(wlo[:, j, :], wraw[:, j, :], plain(whi[:, j, :]),
                                    ALU.subtract).then_inc(sem["w_split"], 1)

        for j in range(RING):
            split(j, j, 16, None)
        with pool.Fori(1, N_UNITS // RING) as i:
            for j in range(RING):
                split(i * RING + j, j, i * 16 + 16, i * RING + (j - RING + 1))
        for unit in range(N_UNITS // RING * RING, N_UNITS):
            split(unit, unit % RING, 16 * (unit // RING + 1), unit - RING + 1)

    @block.tensor
    def _(pe):
        t = 0
        un = 0
        xs = 0
        bc = 0
        ss = 0
        steps_done = heads_done = e_done = 0
        turned = banks = 0

        def bank(tile, n=S, p=P):
            return acc[0:p, tile % 4, 0:n]

        def open_tile(tile, turn=None):
            if turn is not None:
                pe.wait_ge(sem["acc_free"], turn)
            elif tile >= 4:
                pe.wait_ge(sem["acc_free"], tile - 3)

        def three(o, a_hi, a_lo, b_hi, b_lo, start, stop, begins=False, done=None):
            m = nc.tensor.matmul(o, a_hi, b_hi, start=start, stop=False)
            if begins:
                m.then_inc(sem["w_used"], 1)
            nc.tensor.matmul(o, a_lo, b_hi, start=False, stop=False)
            m = nc.tensor.matmul(o, a_hi, b_lo, start=False, stop=stop)
            if done is not None:
                m.then_inc(done, 1)

        def stationary(x_hi, x_lo, kts, tiles, n=S, fresh=0):
            nonlocal t, un
            piece = 0
            for m in range(tiles):
                open_tile(t)
                for k in range(kts):
                    if piece % 8 == 0:
                        pe.wait_ge(sem["w_split"], un + 1)
                    if m == 0 and k < fresh:
                        pe.wait_ge(sem["x_ready"], xs + k + 1)
                    slot, c = un % RING, piece % 8 * P
                    three(bank(t, n), whi[:, slot, c:c + P], wlo[:, slot, c:c + P], x_hi[:, k, 0:n],
                          x_lo[:, k, 0:n], k == 0, k == kts - 1, piece % 8 == 0 and un > 0,
                          sem["acc_ready"] if k == kts - 1 else None)
                    piece += 1
                    if piece % 8 == 0 or (m == tiles - 1 and k == kts - 1):
                        piece = -(-piece // 8) * 8
                        un += 1
                t += 1

        def stationary_loop(x_hi, x_lo, turns, groups=4, kts=KD):
            nonlocal t, un
            per = -(-kts // 8)
            assert groups % 4 == 0
            with pe.Fori(0, turns) as i:
                for m in range(groups):
                    open_tile(t + m, i * groups + (t + m - 3))
                    for k in range(kts):
                        unit = m * per + k // 8
                        if k % 8 == 0:
                            pe.wait_ge(sem["w_split"], i * (groups * per) + (un + unit + 1))
                        slot, c = (un + unit) % RING, k % 8 * P
                        three(bank(t + m), whi[:, slot, c:c + P], wlo[:, slot, c:c + P], x_hi[:, k, :],
                              x_lo[:, k, :], k == 0, k == kts - 1, k % 8 == 0,
                              sem["acc_ready"] if k == kts - 1 else None)
            t += turns * groups
            un += turns * groups * per

        def moving(x_hi, x_lo, kts, n, tiles=TT):
            nonlocal t, un
            for i in range(tiles):
                open_tile(t + i)
            per = UNIT // n
            for k in range(kts):
                if k % per == 0:
                    pe.wait_ge(sem["w_split"], un + 1)
                slot, c = un % RING, k % per * n
                for i in range(tiles):
                    a = slice(i * P, (i + 1) * P)
                    three(bank(t + i, n), x_hi[:, k, a], x_lo[:, k, a], whi[:, slot, c:c + n],
                          wlo[:, slot, c:c + n], k == 0, k == kts - 1, k % per == 0 and i == 0,
                          sem["acc_ready"] if k == kts - 1 else None)
                if k % per == per - 1 or k == kts - 1:
                    un += 1
            t += tiles

        def sum_features(n, cols_=S):
            nonlocal bc, ss
            ss += n
            pe.wait_ge(sem["ss_added"], ss)
            if bc:
                pe.wait_ge(sem["rs_ready"], bc)
            if e_done:
                pe.wait_ge(sem["e_free"], e_done)
            if heads_done:
                pe.wait_ge(sem["o_free"], heads_done)
            nc.tensor.matmul(pv[:, 0:cols_], ones, sqsum[:, 0:cols_], start=True, stop=True)\
                .then_inc(sem["bc_ready"], 1)
            bc += 1

        def sum_tokens():
            nonlocal bc
            pe.wait_ge(sem["rs_ready"], bc)
            for i in range(TT):
                m = nc.tensor.matmul(pv[:, i:i + 1], sqsum[:, i * P:(i + 1) * P], ones[:, 0:1],
                                     start=True, stop=True)
            m.then_inc(sem["bc_ready"], 1)
            bc += 1

        def attention(waves, s, pts):
            nonlocal steps_done, heads_done, turned, banks
            pe.wait_ge(sem["acc_free"], t)
            if e_done:
                pe.wait_ge(sem["e_free"], e_done)
            pe.wait_ge(sem["rs_ready"], bc)

            def scores(w):
                nonlocal banks
                for b in range(TT):
                    if banks >= TT:
                        pe.wait_ge(sem["sc_free"], banks - TT + 1)
                    for x in [x for x in w["items"] if x["bank"] == b]:
                        m = nc.tensor.matmul(acc[:, b, x["col"]:x["col"] + x["n"]], x["q"], x["k"],
                                             start=True, stop=True)
                    m.then_inc(sem["sc_ready"], 1)
                    banks += 1

            def values(w, k, at):
                x = w["turns"][k]
                pe.wait_ge(sem["t_copied"], at + k + 1)
                if w["opens"] and k == 0 and heads_done >= 2:
                    pe.wait_ge(sem["o_free"], heads_done - 1)
                n = len(x["src"]) * P
                nc.tensor.matmul(pvs[heads_done % 2][0:64, S - n:S], x["v"],
                                 pts[0:x["width"], (at + k) % PT_BUFS, 0:n], start=w["opens"] and k == 0,
                                 stop=w["closes"] and k == len(w["turns"]) - 1,
                                 skip_group_check=True).then_inc(sem["pv_done"], 1)

            def turns(w, i):
                nonlocal turned, heads_done
                at = turned
                pe.wait_ge(sem["pn_ready"], steps_done + i + 1)
                for k, x in enumerate(w["turns"]):
                    if at + k >= 2:
                        pe.wait_ge(sem["t_copied"], at + k - 1)
                    for b, c in enumerate(x["src"]):
                        m = nc.tensor.transpose(sc[0:x["width"], (at + k) % 2, b * P:(b + 1) * P],
                                                s[:, i % S_BUFS, c:c + x["width"]], ident)
                    m.then_inc(sem["t_ready"], 1)
                    if k:
                        values(w, k - 1, at)
                values(w, len(w["turns"]) - 1, at)
                turned += len(w["turns"])
                heads_done += w["closes"]

            for i in range(len(waves) + 1):
                if i < len(waves):
                    scores(waves[i])
                if i:
                    turns(waves[i - 1], i - 1)
            steps_done += len(waves)
            pe.wait_ge(sem["sc_free"], banks)
            pe.wait_ge(sem["t_copied"], turned)

        def feed_forward():
            nonlocal xs
            stationary(xhi, xlo, KD, 2, fresh=KD)
            xs += KD
            sum_features(KD)
            stationary(xhi, xlo, KD, 2)
            stationary_loop(xhi, xlo, (U_FFN_UP - 4) // 4)
            up = t
            xs += KF_
            pe.wait_ge(sem["x_ready"], xs)
            stationary_loop(fhi, flo, 2, kts=KF_)
            return up

        pe.wait_ge(sem["in_rel"], 16)
        pe.wait_ge(sem["in_bk"], 16)
        for n0, n1 in ((0, S), (S, TW)):
            open_tile(t)
            nc.tensor.matmul(bank(t, n1 - n0, NH), relv[0:BUCKETS + 1, 0:NH], bk[0:BUCKETS + 1, n0:n1],
                             start=True, stop=True).then_inc(sem["acc_ready"], 1)
            t += 1

        pe.wait_ge(sem["in_const"], 16)
        stationary(xhi, xlo, KD, 2, fresh=KD)
        xs += KD
        sum_features(KD)
        stationary(xhi, xlo, KD, 2)
        stationary_loop(xhi, xlo, 3)
        stationary(xhi, xlo, KD, 6)
        sum_features(3)
        sum_features(2)
        stationary_loop(xhi, xlo, 3)
        xs += KC_
        stationary(lathi[:, 0:3, :], latlo[:, 0:3, :], 3, HA, fresh=3)
        xs += 3
        stationary(lathi[:, 3:5, :], latlo[:, 3:5, :], 2, 4, fresh=2)
        xs += 2
        moving(lathi[:, 3:5, :], latlo[:, 3:5, :], 2, HA * VD)
        stationary(yhi, ylo, KC_, KD)
        pe.wait_ge(sem["qkv_ready"], 1)
        attention(list(latent_waves()), s_a, pt_a)
        pe.wait_ge(sem["x_ready"], xs + HA)
        xs += HA
        stationary(yhi, ylo, KC_, KD)
        pe.wait_ge(sem["x_ready"], xs + KD)
        xs += KD
        stationary_loop(xhi, xlo, 2)
        sum_features(KD)
        mark["up0"] = feed_forward()
        mark["down0"] = t
        sum_features(KD)
        pe.wait_ge(sem["x_ready"], xs + 2)
        xs += 2
        stationary(p_hi, p_lo, 2, KD)
        mark["ple"] = t
        stationary(xhi, xlo, KD, 2, fresh=KD)
        xs += KD
        sum_features(KD, MEM)
        stationary(xhi, xlo, KD, 6)
        sum_features(KD)

        def memory(m_hi, m_lo):
            nonlocal xs
            pe.wait_ge(sem["x_ready"], xs + KD)
            xs += KD
            stationary(m_hi, m_lo, KD, 2, n=MEM)
            moving(m_hi, m_lo, KD, MH * MDH, tiles=2)

        memory(mem1[1], mem1[2])
        stationary(xhi, xlo, KD, 2, fresh=KD)
        xs += KD
        sum_features(KD)
        sum_tokens()
        stationary(xhi, xlo, KD, 9)
        pe.wait_ge(sem["lr_ready"], 1)
        pe.wait_ge(sem["in_wg"], 16)
        for i in range(TT):
            open_tile(t)
            nc.tensor.matmul(bank(t, GH * GDK), lr[0:GR, i * P:(i + 1) * P], wg[0:GR, :],
                             start=True, stop=True).then_inc(sem["acc_ready"], 1)
            t += 1
        pe.wait_ge(sem["rs_ready"], bc)
        pe.wait_ge(sem["in_sums"], 16)
        for lv in range(1, N_SUMS + 1):
            for hd in range(GH):
                if lv == 1 and hd == 0:
                    pe.wait_ge(sem["la_ready"], 1)
                if e_done >= 4:
                    pe.wait_ge(sem["e_free"], e_done - 3)
                if e_done < 4:
                    pe.wait_ge(sem["o_free"], heads_done)
                    pe.wait_ge(sem["t_copied"], turned)
                for i in range(TT):
                    m = nc.tensor.matmul(ebank[hd][0:GDK, i * P:(i + 1) * P],
                                         la[:, i, hd * GDK:(hd + 1) * GDK], dm[:, lv - 1, :],
                                         start=True, stop=True)
                m.then_inc(sem["e_ready"], 1)
                e_done += 1
            if lv <= N_MASKS:
                for hd in range(GH):
                    open_tile(t)
                    if lv > 1:
                        pe.wait_ge(sem["g_ready"], GH * (lv - 2) + hd + 1)
                    a, b = (kg, qg) if lv == 1 else (f[(lv - 1) % 2], f[(lv - 1) % 2])
                    for i in range(TT):
                        w = slice(i * P, (i + 1) * P)
                        m = nc.tensor.matmul(acc[:, t % 4, w], a[0:GDK, hd, w], b[0:GDK, hd, w],
                                             start=True, stop=True)
                    m.then_inc(sem["acc_ready"], 1)
                    t += 1
                mark["pairs", lv - 1] = t
            if lv <= 6:
                moving(xhi, xlo, KD, 256)
        pe.wait_ge(sem["g_ready"], GH * N_SUMS)
        for i in range(TT):
            open_tile(t)
            for hd in range(GH):
                m = nc.tensor.transpose(acc[:, t % 4, hd * GDK:(hd + 1) * GDK],
                                        kg[0:GDK, hd, i * P:(i + 1) * P], ident[0:GDK, 0:GDK])
            m.then_inc(sem["acc_ready"], 1)
            t += 1
        pe.wait_ge(sem["kout_ready"], TT)
        for i in range(TT):
            for hd in range(GH):
                vcols = slice(hd * GDV, (hd + 1) * GDV)
                w = slice(i * P, (i + 1) * P)
                open_tile(t)
                m = nc.tensor.matmul(bank(t, GDV), at_[:, hd, w], vg[:, i, vcols], start=True, stop=i == 0)
                if i:
                    pe.wait_ge(sem["st_ready"], GH * (i - 1) + hd + 1)
                    m = nc.tensor.matmul(bank(t, GDV), qg[0:GDK, hd, w], st[0:GDK, hd, :], start=False,
                                         stop=True)
                m.then_inc(sem["acc_ready"], 1)
                t += 1
                if i < TT - 1:
                    open_tile(t)
                    nc.tensor.matmul(bank(t, GDV, GDK), kout[:, i, hd * GDK:(hd + 1) * GDK], vg[:, i, vcols],
                                     start=True, stop=True).then_inc(sem["acc_ready"], 1)
                    t += 1
        attention(list(memory_waves(mq1, mk1, mv1)), s_1, pt_1)
        xs += MH
        pe.wait_ge(sem["og_ready"], TT)
        for c in range(6):
            open_tile(t)
            for i in range(TT):
                m = nc.tensor.transpose(acc[:, t % 4, i * P:(i + 1) * P], o_g[:, i, c * P:(c + 1) * P], ident)
            m.then_inc(sem["acc_ready"], 1)
            t += 1
        xs += 6
        pe.wait_ge(sem["x_ready"], xs)
        stationary_loop(xhi, xlo, 2)
        feed_forward()

        stationary(xhi, xlo, KD, 2, fresh=KD)
        xs += KD
        sum_features(KD)
        sum_tokens()
        stationary(xhi, xlo, KD, 6)
        moving(xhi, xlo, KD, NG * NDH)
        moving(xhi, xlo, KD, NG * NDH)
        pe.wait_ge(sem["x_ready"], xs + 2)
        xs += 2
        for j in range(2):
            stationary(zhi[j], zlo[j], LP, 1, n=NG * NCMP)
        mark["windows"] = t
        sum_features(KD, MEM)
        memory(mem2[1], mem2[2])
        pe.wait_ge(sem["hid_ready"], 1)
        open_tile(t)
        nc.tensor.matmul(bank(t, NG * NCMP, NDH), C("w2_0", 0, NDH), hid[:, 0, 0:NG * NCMP], start=True,
                         stop=True).then_inc(sem["acc_ready"], 1)
        t += 1
        pe.wait_ge(sem["hid_ready"], 2)
        open_tile(t)
        for g in range(NG):
            m = nc.tensor.matmul(acc[0:NCMP, t % 4, g * NDH:(g + 1) * NDH], hid[:, 1, g * NCMP:(g + 1) * NCMP],
                                 C("w2_1", 0, NDH), start=True, stop=True)
        m.then_inc(sem["acc_ready"], 1)
        t += 1
        stationary(xhi, xlo, KD, 9, fresh=KD)
        xs += KD
        pe.wait_ge(sem["gln_ready"], 1)
        open_tile(t)
        for i in range(TT):
            m = nc.tensor.transpose(acc[:, t % 4, i * 3 * NH:(i + 1) * 3 * NH],
                                    tmp[0:3 * NH, i * P:(i + 1) * P], ident[0:3 * NH, 0:3 * NH])
        m.then_inc(sem["acc_ready"], 1)
        t += 1
        pe.wait_ge(sem["qkv_ready"], 2)
        pe.wait_ge(sem["in_toep"], 16)
        attention(list(branch_waves()) + list(memory_waves(mq2, mk2, mv2)), s_2, pt_2)
        xs += NH + MH
        pe.wait_ge(sem["x_ready"], xs)
        stationary_loop(xhi, xlo, 2)
        feed_forward()
        sum_features(KD)
        assert un == N_UNITS, un

    @block.vector
    def _(dve):
        n = Count(dve)
        t = 0
        sqs = 0
        rs = 0
        waves_done = banks = turned = exps = heads = 0
        V = nc.vector

        def take(p=P, cols_=S):
            i = t if n.loop is None else n.loop[0] * n.loop[2][sem["acc_free"]] + t
            dve.wait_ge(sem["acc_ready"], i + 1)
            return acc[0:p, t % 4, 0:cols_]

        def give(ins):
            nonlocal t
            n.did(ins, sem["acc_free"])
            t += 1

        def did(ins):
            n.did(ins, sem["dve_step"])

        def split(hi, lo, src, gain=None):
            if gain is None:
                did(V.tensor_copy(hi, src))
                n.did(V.tensor_tensor(lo, src, plain(hi), ALU.subtract), sem["x_ready"])
            else:
                did(V.tensor_scalar(hi, src, gain, None, ALU.mult))
                n.did(V.scalar_tensor_tensor(lo, src, gain, plain(hi), ALU.mult, ALU.subtract),
                      sem["x_ready"])

        def add_square(first, cols_=S):
            nonlocal sqs
            dve.wait_ge(sem["sq_ready"], sqs + 1)
            s = sq[:, sqs % 2, 0:cols_]
            if first:
                ins = V.tensor_copy(sqsum[:, 0:cols_], s)
            else:
                ins = V.tensor_tensor(sqsum[:, 0:cols_], sqsum[:, 0:cols_], s, ALU.add)
            n.did(ins, sem["ss_added"])
            sqs += 1

        def factor(to):
            nonlocal rs
            dve.wait_ge(sem["rs_ready"], rs + 1)
            did(V.reciprocal(to, to))
            rs += 1

        def stage(gain, before=None, squares=True, after=None):
            for k in range(KD):
                if before:
                    before(k)
                split(xhi[:, k, :], xlo[:, k, :], h[:, k, :], C(gain, k) if gain else None)
                if squares and k:
                    add_square(k == 1)
            if squares:
                add_square(False)

        def post_norm(y, gain):
            def go(k):
                did(V.scalar_tensor_tensor(tmp[:, :], y[:, k, :], C(gain, k), rstd[:, :], ALU.mult, ALU.mult))
                n.did(V.tensor_tensor(h[:, k, :], h[:, k, :], tmp[:, :], ALU.add), sem["src_ready"])
            return go

        def residual(k):
            ins = V.tensor_tensor(h[:, k, :], h[:, k, :], take(), ALU.add)
            give(ins)
            n.tell(sem["src_ready"])

        def gather_down(y):
            for k in range(KD):
                give(V.tensor_copy(y[:, k, :], take()))
                n.tell(sem["src_ready"])
                if k:
                    add_square(k == 1)
            add_square(False)

        def feed_forward(which):
            factor(rstd[:, :])
            did(V.memset(u[:, :, 0:2], 0.0))
            per = {sem["acc_free"]: 4, sem["u_ready"]: 4, sem["dve_step"]: 8, sem["c_ready"]: 4,
                   sem["x_ready"]: 2}
            c0 = COL[which]
            a0 = ffn_seen[0]
            with dve.Fori(0, KF_ // 2) as i:
                n.enter(i, per)
                for pair in range(2):
                    for half in range(2):
                        j = 2 * pair + half
                        src = take()
                        give(V.tensor_tensor(u[:, half, 2:], src, rstd[:, :], ALU.mult))
                        n.tell(sem["u_ready"])
                    for half in range(2):
                        j = 2 * pair + half
                        w = [col[:, bass.ds(i * 16 + (c0 + 8 * pair + 4 * half + tap), 1)] for tap in range(2)]
                        dve.wait_ge(sem["a_ready"], i * 4 + (a0 * 4 + j + 1))
                        c = sq[:, half, :]
                        did(V.scalar_tensor_tensor(c, u[:, half, 1:S + 1], w[1], c, ALU.mult, ALU.add))
                        n.did(V.scalar_tensor_tensor(c, u[:, half, 0:S], w[0], c, ALU.mult, ALU.add),
                              sem["c_ready"])
                    dve.wait_ge(sem["v_ready"], i * 2 + (a0 * 2 + pair + 1))
                    did(V.tensor_tensor(sq[:, 0, :], sq[:, 0, :], sq[:, 1, :], ALU.mult))
                    fo = (fhi[:, bass.ds(i * 2 + pair, 1), :].rearrange("p a n -> p (a n)"),
                          flo[:, bass.ds(i * 2 + pair, 1), :].rearrange("p a n -> p (a n)"))
                    split(fo[0], fo[1], sq[:, 0, :])
            n.leave(KF_ // 2)
            t_add(4 * (KF_ // 2 - 1))
            ffn_seen[0] += KF_ // 2

        ffn_seen = [0]

        def t_add(k):
            nonlocal t
            t += k

        def softmaxes(waves, s):
            nonlocal waves_done, banks, turned, exps, heads
            w0 = waves_done
            turn_at = [turned]
            for w in waves:
                turn_at.append(turn_at[-1] + len(w["turns"]))

            def high(i):
                nonlocal banks
                w, b, st_ = waves[i], i % S_BUFS, stat[:, i % 2]
                if i >= S_BUFS:
                    dve.wait_ge(sem["t_ready"], turn_at[i - S_BUFS + 1])
                for k, x in enumerate(w["items"]):
                    last = k == len(w["items"]) - 1 or w["items"][k + 1]["bank"] != x["bank"]
                    if k == 0 or w["items"][k - 1]["bank"] != x["bank"]:
                        dve.wait_ge(sem["sc_ready"], banks + 1)
                    to, of = s[:, b, x["off"]:x["off"] + x["n"]], acc[:, x["bank"], x["col"]:x["col"] + x["n"]]
                    if x["bias"] is None:
                        n.did(V.tensor_copy(to, of), sem["dve_step"], False)
                        ins = V.tensor_reduce(st_[:, 0, k:k + 1], of, AX, ALU.max)
                    else:
                        ins = V.tensor_tensor_reduce(to, of, x["bias"], 1.0, -3e38, ALU.add, ALU.max,
                                                     st_[:, 0, k:k + 1])
                    n.did(ins, sem["sc_free" if last else "dve_step"], False)
                    banks += last
                dve.wait_ge(sem["sc_free"], banks)
                m = len(w["items"])
                n.did(V.tensor_scalar(st_[:, 1, 0:m], st_[:, 0, 0:m], -w["scale"], None, ALU.mult),
                      sem["s_ready"], False)

            def normal(i):
                nonlocal exps
                w, b, st_ = waves[i], i % S_BUFS, stat[:, i % 2]
                m = len(w["items"])
                exps += m
                dve.wait_ge(sem["p_ready"], exps)
                r = st_[:, 3, :]
                did(V.reciprocal(r[:, 0:m], st_[:, 2, 0:m]))
                for first, g in w["gates"]:
                    part = r[:, first:first + g.shape[1]]
                    n.did(V.tensor_tensor(part, part, g, ALU.mult), sem["dve_step"], False)
                dve.wait_ge(sem["dve_step"], n.at(sem["dve_step"]))
                if "valid" in w:
                    part = r[:, w["valid"]:w["valid"] + 1]
                    did(V.tensor_tensor(part, part, C("valid"), ALU.mult))
                for k, x in enumerate(w["items"]):
                    p_ = s[:, b, x["off"]:x["off"] + x["n"]]
                    n.did(V.tensor_scalar(p_, p_, r[:, k:k + 1], None, ALU.mult),
                          sem["pn_ready" if k == m - 1 else "dve_step"], False)

            def output(i):
                nonlocal heads
                w = waves[i]
                if not w["closes"]:
                    return
                dve.wait_ge(sem["pv_done"], turn_at[i + 1])
                hi, lo, tile, at = w["dest"]
                o, of = slice(at, at + 64), pvs[heads % 2][0:64, :]
                did(V.tensor_copy(hi[o, tile, :], of))
                n.did(V.tensor_tensor(lo[o, tile, :], of, plain(hi[o, tile, :]), ALU.subtract),
                      sem["x_ready"])
                n.tell(sem["o_free"])
                heads += 1

            for i in range(len(waves) + 2):
                if 1 <= i <= len(waves):
                    normal(i - 1)
                if i < len(waves):
                    high(i)
                if i >= 2:
                    output(i - 2)
            waves_done += len(waves)
            turned = turn_at[-1]

        def memory_stage(m, gain):
            for k in range(KD):
                add_square(k == 0, MEM)
            factor(rstd2[:, 0:MEM])
            for k in range(KD):
                did(V.scalar_tensor_tensor(m[0][:, k, :], m[0][:, k, :], C(gain, k), rstd2[:, 0:MEM],
                                           ALU.mult, ALU.mult))
                split(m[1][:, k, :], m[2][:, k, :], m[0][:, k, :])

        def memory_out(mkt, mv):
            for k in range(2):
                give(V.tensor_copy(mkt[:, k, :], take(P, MEM)))
            for i in range(2):
                give(V.tensor_copy(mv[:, i, :], take(P, MH * MDH)))

        for n0, n1 in ((0, S), (S, TW)):
            give(V.tensor_copy(vr[0:NH, n0:n1], take(NH, n1 - n0)))
        n.tell(sem["vr_ready"])

        dve.wait_ge(sem["in_col"], 16)

        def arrived(k):
            if k % 2 == 0:
                dve.wait_ge(in_x[k // 2], 16)

        stage("mix_pre", arrived)
        r = slice(NOPE, P)
        dve.wait_ge(sem["in_pos"], 16)
        a0, a1, a2 = ang[r, 0, :], ang[r, 1, :], ang[r, 2, :]
        magic = 1.5 * 2.0 ** 23
        did(V.tensor_copy(a0, pos_i[r, :]))
        did(V.tensor_scalar(a0, a0, C("inv", p=r), None, ALU.mult))
        did(V.tensor_scalar(a1, a0, 1.0 / (2 * np.pi), C("quarter", p=r), ALU.mult, ALU.add))
        did(V.tensor_scalar(a1, a1, magic, None, ALU.add))
        did(V.tensor_scalar(a1, a1, magic, None, ALU.subtract))
        c1 = 6.28125
        c2 = 0.0019350051879882812
        c3 = 2 * np.pi - c1 - c2
        for part in (c1, c2, c3):
            did(V.scalar_tensor_tensor(a2, a1, -part, a0, ALU.mult, ALU.add))
            did(V.tensor_copy(a0, a2))
        did(V.tensor_scalar(a0, a0, C("halfpi", p=r), None, ALU.add))
        n.did(V.tensor_scalar(a0, a0, 3.1415925, -3.1415925, ALU.min, ALU.max), sem["angle_ready"])
        factor(rstd[:, :])
        did(V.memset(prod[:, 0:2], 0.0))
        for i in range(KC_):
            give(V.tensor_tensor(tmp[:, :], take(), rstd[:, :], ALU.mult))
            give(V.tensor_tensor(prod[:, 2:], take(), rstd[:, :], ALU.mult))
            did(V.tensor_tensor(prod[:, 2:], prod[:, 2:], tmp[:, :], ALU.mult))
            w = [C("conv_a", 3 * i + tap) for tap in range(3)]
            did(V.tensor_scalar(cv[:, :], prod[:, 2:], w[2], None, ALU.mult))
            did(V.scalar_tensor_tensor(cv[:, :], prod[:, 1:S + 1], w[1], cv[:, :], ALU.mult, ALU.add))
            did(V.scalar_tensor_tensor(cv[:, :], prod[:, 0:S], w[0], cv[:, :], ALU.mult, ALU.add))
            give(V.tensor_tensor(tmp[:, :], take(), rstd[:, :], ALU.mult))
            did(V.tensor_tensor(cv[:, :], cv[:, :], tmp[:, :], ALU.mult))
            split(yhi[:, i, :], ylo[:, i, :], cv[:, :])
        dve.wait_ge(sem["sine_ready"], 1)
        did(V.tensor_scalar(cs[r, :], cs[r, :], C("sign", p=r), None, ALU.mult))
        dve.wait_ge(sem["dist_out"], 16)
        for i in range(5):
            give(V.tensor_tensor(lat[:, i, :], take(), rstd[:, :], ALU.mult))
            n.tell(sem["src_ready"])
        give(V.tensor_tensor(kpe[r, :], take()[r, :], rstd[r, :], ALU.mult))
        did(V.tensor_tensor(kpe[r, :], kpe[r, :], cs[r, :], ALU.mult))

        def gate(i):
            give(V.tensor_tensor(sg[:, i, :], take(), rstd[:, :], ALU.mult))
            n.tell(sem["gate_in"])

        for i in range(4):
            gate(i)
        for first, count, gain in ((0, 3, "q_lat"), (3, 2, "kv_lat")):
            for k in range(count):
                add_square(k == 0)
            factor(rstd2[:, :])
            for k in range(count):
                did(V.scalar_tensor_tensor(lat[:, first + k, :], lat[:, first + k, :], C(gain, k),
                                           rstd2[:, :], ALU.mult, ALU.mult))
                split(lathi[:, first + k, :], latlo[:, first + k, :], lat[:, first + k, :])
        for i in range(4, 16):
            gate(i)
        rot, swapped = slice(NOPE, QK), slice(QK, P)
        did(V.tensor_copy(tmp[rot, :], kpe[swapped, :]))
        did(V.tensor_tensor(kpe[rot, :], kpe[rot, :], tmp[rot, :], ALU.add))
        for i in range(HA):
            did(V.tensor_copy(kf[rot, i, :], kpe[rot, :]))
        for i in range(HA):
            a = take()
            did(V.tensor_tensor(qf[rot, i, :], a[rot, :], cs[rot, :], ALU.mult))
            did(V.tensor_tensor(tmp[rot, :], a[swapped, :], cs[swapped, :], ALU.mult))
            did(V.tensor_tensor(qf[rot, i, :], qf[rot, i, :], tmp[rot, :], ALU.add))
            give(V.tensor_copy(qf[0:NOPE, i, :], a[0:NOPE, :]))
        for i in range(4):
            a = take()
            did(V.tensor_copy(kf[0:NOPE, 2 * i, :], a[0:NOPE, :]))
            give(V.tensor_copy(kf[0:NOPE, 2 * i + 1, :], a[NOPE:P, :]))
        for i in range(TT):
            give(V.tensor_copy(va[:, i, :], take()))
        n.tell(sem["qkv_ready"])
        for i in range(KD):
            dve.wait_ge(sem["sig_ready"], i + 1)
            give(V.tensor_tensor(sg[:, i, :], sg[:, i, :], take(), ALU.mult))
        dve.wait_ge(sem["in_chunk"], 16)
        softmaxes(list(latent_waves()), s_a)
        for i in range(KD):
            dve.wait_ge(sem["sig_ready"], KD + i + 1)
            give(V.tensor_tensor(tmp[:, :], sg[:, KD + i, :], take(), ALU.mult))
            did(V.tensor_tensor(tmp[:, :], tmp[:, :], sg[:, i, :], ALU.add))
            split(xhi[:, i, :], xlo[:, i, :], tmp[:, :])
        gather_down(y_o)
        factor(rstd[:, :])
        stage("ffn_pre", post_norm(y_o, "mix_post"))
        feed_forward("ffn0")
        dve.wait_ge(sem["in_p"], 16)
        for k in range(2):
            split(p_hi[:, k, :], p_lo[:, k, :], p_f[:, k, :])
        gather_down(y_d)
        factor(rstd[:, :])
        for k in range(KD):
            give(V.tensor_copy(e[:, k, :], take()))
        stage(None, post_norm(y_d, "ffn_post"), squares=False)
        memory_stage(mem1, "nmem0")
        for k in range(KD):
            dve.wait_ge(sem["ple_sig"], k + 1)
            take()
            give(V.tensor_tensor(e[:, k, :], e[:, k, :], gs[:, k % 2, :], ALU.mult))
            n.tell(sem["src_ready"])
            if k:
                add_square(k == 1)
        add_square(False)
        factor(rstd[:, :])
        stage("nmix0", post_norm(e, "ple_post"))

        memory_out(mk1, mv1)
        factor(rstd[:, :])
        factor(rstd_t[:, :])
        give(V.tensor_tensor(lr[0:GR, :], take(GR), rstd[0:GR, :], ALU.mult))
        n.tell(sem["lr_ready"])
        for i in range(GH):
            give(V.scalar_tensor_tensor(qg[0:GDK, i, :], take(GDK), GDK ** -0.5, rstd[0:GDK, :],
                                        ALU.mult, ALU.mult))
        for i in range(GH):
            give(V.tensor_tensor(kg[0:GDK, i, :], take(GDK), rstd[0:GDK, :], ALU.mult))
        for i in range(2):
            give(V.scalar_tensor_tensor(mq1[:, i, :], take(), MDH ** -0.5, rstd[:, :], ALU.mult, ALU.mult))
        for i in range(TT):
            give(V.tensor_tensor(xg[:, i, :], take(P, GH * GDK), row[:, 0:GH * GDK], ALU.add))
        n.tell(sem["gl_raw"])
        dve.wait_ge(sem["gl_ln"], 1)
        n.did(V.scalar_tensor_tensor(la[:, :, :].rearrange("p a b -> p (a b)"),
                                     xg[:, :, :].rearrange("p a b -> p (a b)"), 0.0,
                                     glt[:, :, :].rearrange("p a b -> p (a b)"), ALU.min, ALU.subtract),
              sem["la_ready"])
        dve.wait_ge(sem["in_masks"], 16)
        for lv in range(1, N_SUMS + 1):
            fb = f[lv % 2]
            for hd in range(GH):
                dve.wait_ge(sem["f_ready"], GH * (lv - 1) + hd + 1)
                if lv <= LEVELS:
                    half = 2 ** (lv - 1)

                    def part(x, late):
                        v = x[0:GDK, hd, :].rearrange("p (n b) -> p n b", b=2 * half)
                        return v[:, :, half:2 * half] if late else v[:, :, 0:half]
                    did(V.tensor_tensor(part(fb, True), part(fb, True), part(qg, True), ALU.mult))
                    n.did(V.tensor_tensor(part(fb, False), part(fb, False), part(kg, False), ALU.mult),
                          sem["g_ready"])
                elif lv == LEVELS + 1:
                    did(V.tensor_copy(decay[0:GDK, TT * hd:TT * hd + TT], fb[0:GDK, hd, P - 1:S:P]))
                    n.did(V.tensor_tensor(qg[0:GDK, hd, :], qg[0:GDK, hd, :], fb[0:GDK, hd, :], ALU.mult),
                          sem["g_ready"])
                else:
                    n.did(V.tensor_tensor(kg[0:GDK, hd, :], kg[0:GDK, hd, :], fb[0:GDK, hd, :], ALU.mult),
                          sem["g_ready"])
            if lv <= N_MASKS:
                mask = mk[:, lv - 1:lv, :].to_broadcast([P, TT, P])
                for hd in range(GH):
                    a = take().rearrange("p (a b) -> p a b", b=P)
                    if lv == 1:
                        give(V.tensor_tensor(at_[:, hd, :].rearrange("p (a b) -> p a b", b=P), a, mask, ALU.mult))
                    else:
                        give(V.tensor_tensor(tmp[:, :].rearrange("p (a b) -> p a b", b=P), a, mask, ALU.mult))
                        did(V.tensor_tensor(at_[:, hd, :], at_[:, hd, :], tmp[:, :], ALU.add))
            if lv <= 6:
                to = vg if lv <= 3 else gg
                c = (lv - 1) % 3 * 256
                for i in range(TT):
                    give(V.tensor_scalar(to[:, i, c:c + 256], take(P, 256), rstd_t[:, i:i + 1], None, ALU.mult))
                if lv == 6:
                    n.tell(sem["gates_raw"])
        for i in range(TT):
            give(V.tensor_copy(kout[:, i, :], take(P, GH * GDK)))
            n.tell(sem["kout_ready"])
        for i in range(TT):
            for hd in range(GH):
                vcols = slice(hd * GDV, (hd + 1) * GDV)
                give(V.tensor_copy(o_g[:, i, vcols], take(P, GDV)))
                did(V.tensor_tensor_reduce(tmp[:, 0:GDV], o_g[:, i, vcols], o_g[:, i, vcols], 1.0, 0.0,
                                           ALU.mult, ALU.add, osum[:, GH * i + hd:GH * i + hd + 1]))
                if i < TT - 1:
                    a = take(GDK, GDV)
                    if i == 0:
                        give(V.tensor_copy(st[0:GDK, hd, :], a))
                    else:
                        give(V.scalar_tensor_tensor(st[0:GDK, hd, :], st[0:GDK, hd, :],
                                                    decay[0:GDK, TT * hd + i:TT * hd + i + 1], a, ALU.mult, ALU.add))
                    n.tell(sem["st_ready"])
        n.tell(sem["osq_ready"])
        dve.wait_ge(sem["oroot_ready"], 1)
        ro = oroot[:, :]
        did(V.reciprocal(ro, ro))
        dve.wait_ge(sem["gates_ready"], 1)
        for i in range(TT):
            for hd in range(GH):
                vcols = slice(hd * GDV, (hd + 1) * GDV)
                did(V.scalar_tensor_tensor(o_g[:, i, vcols], o_g[:, i, vcols],
                                           ro[:, GH * i + hd:GH * i + hd + 1],
                                           row[:, ROW["onorm"]:ROW["onorm"] + GDV], ALU.mult, ALU.mult))
            n.did(V.tensor_tensor(o_g[:, i, :], o_g[:, i, :], gg[:, i, :], ALU.mult), sem["og_ready"])
        softmaxes(list(memory_waves(mq1, mk1, mv1)), s_1)
        for c in range(6):
            give(V.tensor_copy(tmp[:, :], take()))
            split(xhi[:, c, :], xlo[:, c, :], tmp[:, :])
        for k in range(KD):
            residual(k)
        stage("nffn1")
        feed_forward("ffn1")
        stage("nkv", residual)

        factor(rstd[:, :])
        factor(rstd_t[:, :])
        for j in range(2):
            for k in range(2):
                a = take()
                for g in range(2):
                    rr = slice(g * NDH, (g + 1) * NDH)
                    did(V.tensor_tensor(z[0:NDH, 2 * k + g, :], a[rr, :], rstd[rr, :], ALU.mult))
                    ins = V.tensor_tensor(z[NDH:P, 2 * k + g, 0:S - 1], a[rr, 1:], rstd[rr, 1:], ALU.mult)
                    if g == 0:
                        did(ins)
                    else:
                        give(ins)
            for part in range(2):
                l0, t0 = part * LP // 2, part * CMP_S
                win = z[:, :, t0:t0 + CMP_S * NCMP].rearrange("p g (c l) -> p l g c", l=CMP_S)[:, 0:CMP_S:2]
                did(V.tensor_tensor(zw[:, l0:l0 + LP // 2, :].rearrange("p l (g c) -> p l g c", g=NG), win,
                                    C(f"pos{j}", l0, LP // 2).unsqueeze(2).unsqueeze(3)
                                    .to_broadcast([P, LP // 2, NG, NCMP]), ALU.add))
            flat = "p a b -> p (a b)"
            split(zhi[j][:, :, :].rearrange(flat), zlo[j][:, :, :].rearrange(flat), zw[:, :, :].rearrange(flat))
        n.tell(sem["z_done"])
        for j in range(2):
            for k in range(2):
                give(V.tensor_tensor(kn[j][:, k, :], take(), rstd[:, :], ALU.mult))
        for j in range(2):
            for i in range(TT):
                give(V.tensor_scalar(vn[j][:, i, :], take(P, NG * NDH), rstd_t[:, i:i + 1], None, ALU.mult))
        nw = NG * NCMP
        for k in range(KD):
            add_square(k == 0, MEM)
        for j in range(2):
            give(V.tensor_scalar(hid[:, j, 0:nw], take(P, nw), C("cb1", j), None, ALU.add))
            n.tell(sem["hid_raw"])
        factor(rstd2[:, 0:MEM])
        for k in range(KD):
            did(V.scalar_tensor_tensor(mem2[0][:, k, :], mem2[0][:, k, :], C("nmem1", k), rstd2[:, 0:MEM],
                                       ALU.mult, ALU.mult))
            split(mem2[1][:, k, :], mem2[2][:, k, :], mem2[0][:, k, :])
        stage("nmix1", squares=False)
        memory_out(mk2, mv2)
        a = take(NDH, nw)
        for g in range(NG):
            rr = slice(g % 2 * NDH, g % 2 * NDH + NDH)
            ins = V.tensor_scalar(kc[rr, g // 2, 0:NCMP], a[:, g * NCMP:(g + 1) * NCMP],
                                  C("cb2", p=slice(0, NDH)), None, ALU.add)
            if g < NG - 1:
                did(ins)
            else:
                give(ins)
        did(V.memset(vc[:, :], 0.0))
        a = take(NCMP, NG * NDH)
        give(V.tensor_tensor(vc[0:NCMP, :].rearrange("p (g d) -> p g d", d=NDH),
                             a.rearrange("p (g d) -> p g d", d=NDH),
                             row[0:NCMP, ROW["cb2r"]:ROW["cb2r"] + NDH].unsqueeze(1)
                             .to_broadcast([NCMP, NG, NDH]), ALU.add))
        for i in range(6):
            give(V.scalar_tensor_tensor(qn[:, i, :], take(), NDH ** -0.5, rstd[:, :], ALU.mult, ALU.mult))
        for i in range(2):
            give(V.scalar_tensor_tensor(mq2[:, i, :], take(), MDH ** -0.5, rstd[:, :], ALU.mult, ALU.mult))
        give(V.tensor_tensor(tmp[0:3 * NH, :], take(3 * NH), rstd[0:3 * NH, :], ALU.mult))
        n.tell(sem["gln_ready"])
        give(V.tensor_copy(gt[:, :, :].rearrange("p a b -> p (a b)"), take(P, TT * 3 * NH)))
        n.tell(sem["gates_raw"])
        dve.wait_ge(sem["gates_ready"], 2)
        did(V.memset(s_2[:, :, S_CMP:SW], 0.0))
        dve.wait_ge(sem["in_toep"], 16)
        n.tell(sem["qkv_ready"])
        softmaxes(list(branch_waves()) + list(memory_waves(mq2, mk2, mv2)), s_2)
        for k in range(KD):
            residual(k)
        stage("nffn2")
        feed_forward("ffn2")
        for k in range(KD):
            residual(k)
            if k:
                add_square(k == 1)
        add_square(False)
        factor(rstd[:, :])
        for k in range(KD):
            n.did(V.scalar_tensor_tensor(h[:, k, :], h[:, k, :], C("final", k), rstd[:, :], ALU.mult,
                                         ALU.mult), sem["out_ready"])

    @block.scalar
    def _(act):
        n = Count(act)
        src = 0
        sqs = 0
        bc = 0
        waves_done = turned = 0
        fed = 0
        A = nc.scalar

        def load(to, what, name):
            act.dma_start(to, what).then_inc(sem[name], 16)

        def did(ins):
            n.did(ins, sem["act_step"])

        def square(what):
            nonlocal sqs
            if sqs >= 2:
                act.wait_ge(sem["ss_added"], sqs - 1)
            n.did(A.activation(sq[:, sqs % 2, 0:what.shape[-1]], what, ACT.Square), sem["sq_ready"])
            sqs += 1

        def squares(tiles, arrived=None):
            nonlocal src
            for i, what in enumerate(tiles):
                if arrived:
                    arrived(i)
                else:
                    act.wait_ge(sem["src_ready"], src + 1)
                    src += 1
                square(what)

        def root(to, count):
            nonlocal bc
            act.wait_ge(sem["bc_ready"], bc + 1)
            n.did(A.activation(to, pv[:, 0:to.shape[-1]], ACT.Sqrt, scale=1.0 / count, bias=C("eps")),
                  sem["rs_ready"])
            bc += 1

        def feed_forward(which, func):
            nonlocal fed
            c0 = COL[which]
            per = {sem["a_ready"]: 4, sem["v_ready"]: 2}
            with act.Fori(0, KF_ // 2) as i:
                n.enter(i, per)
                for pair in range(2):
                    for half in range(2):
                        j = 2 * pair + half
                        w2, b = (col[:, bass.ds(i * 16 + (c0 + 8 * pair + 4 * half + x), 1)] for x in (2, 3))
                        act.wait_ge(sem["u_ready"], i * 4 + (4 * fed + j + 1))
                        n.did(A.activation(sq[:, half, :], u[:, half, 2:], ACT.Identity, scale=w2, bias=b),
                              sem["a_ready"])
                    act.wait_ge(sem["c_ready"], i * 4 + (4 * fed + 2 * pair + 1))
                    n.did(A.activation(sq[:, 0, :], sq[:, 0, :], func), sem["v_ready"])
            n.leave(KF_ // 2)
            fed += KF_ // 2

        def softmaxes(waves, s, pts):
            nonlocal waves_done, turned
            for i in range(len(waves) + 1):
                items = waves[i]["items"] if i < len(waves) else []
                turns = waves[i - 1]["turns"] if i else []
                if items:
                    items = list(enumerate(items))
                copies = list(enumerate(turns))
                for k in range(max(len(items), len(copies))):
                    if k < len(copies):
                        x = copies[k][1]
                        act.wait_ge(sem["t_ready"], turned + 1)
                        if turned >= PT_BUFS:
                            act.wait_ge(sem["pv_done"], turned - PT_BUFS + 1)
                        m = len(x["src"]) * P
                        n.did(A.activation(pts[0:x["width"], turned % PT_BUFS, 0:m],
                                           sc[0:x["width"], turned % 2, 0:m], ACT.Copy), sem["t_copied"],
                              False)
                        turned += 1
                    if k < len(items):
                        x, st_ = items[k][1], stat[:, i % 2]
                        if k == 0:
                            act.wait_ge(sem["s_ready"], waves_done + i + 1)
                        p_ = s[:, i % S_BUFS, x["off"]:x["off"] + x["n"]]
                        n.did(A.activation(p_, p_, ACT.Exp, scale=waves[i]["scale"], bias=st_[:, 1, k:k + 1],
                                           accum_out=st_[:, 2, k:k + 1]), sem["p_ready"], False)
            waves_done += len(waves)

        def tiles(x, count=KD):
            return [x[:, k, :] for k in range(count)]

        load(relv[0:BUCKETS + 1, 0:NH], rel, "in_rel")
        load(bk[0:BUCKETS + 1, :], buckets, "in_bk")
        load(col[:, :], cols, "in_col")
        load(const[:, :], consts, "in_const")
        load(row[:, :], rws, "in_row")
        load(pos_i[NOPE:P, :], positions, "in_pos")
        load(chunkm[:, :], chunk, "in_chunk")
        act.wait_ge(sem["vr_ready"], 1)
        act.dma_start(distances.rearrange("h (r n) -> h r n", n=TW),
                      vr[0:NH, :].unsqueeze(1).to_broadcast([NH, P, TW])).then_inc(sem["dist_out"], 16)

        act.wait_ge(sem["in_col"], 16)
        squares(tiles(h), lambda k: act.wait_ge(in_x[k // 2], 16))
        act.wait_ge(sem["angle_ready"], 1)
        n.did(A.activation(cs[NOPE:P, :], ang[NOPE:P, 0, :], ACT.Sin), sem["sine_ready"])
        root(rstd[:, :], D)
        squares([lat[:, k, :] for k in range(3)])
        root(rstd2[:, :], Q_LORA)
        squares([lat[:, k, :] for k in range(3, 5)])
        root(rstd2[:, :], KV_LORA)
        for i in range(2 * KD):
            act.wait_ge(sem["gate_in"], i + 1)
            n.did(A.activation(sg[:, i, :], sg[:, i, :], ACT.Sigmoid), sem["sig_ready"])
        softmaxes(list(latent_waves()), s_a, pt_a)
        squares(tiles(y_o))
        root(rstd[:, :], D)
        squares(tiles(h))
        root(rstd[:, :], D)
        feed_forward("ffn0", ACT.Gelu_apprx_tanh)
        act.wait_ge(sem["acc_ready"], mark["up0"])
        load(p_f[:, :, :], p_t, "in_p")
        squares(tiles(y_d))
        act.wait_ge(sem["acc_ready"], mark["down0"])
        load(mem1[0][:, :, :], mem_t, "in_mem1")
        load(dm[:, :, :], sums, "in_sums")
        load(mk[:, :, :], masks, "in_masks")
        load(wg[0:GR, :], wgate, "in_wg")
        root(rstd[:, :], D)
        src += KD
        squares(tiles(mem1[0]), lambda k: act.wait_ge(sem["in_mem1"], 16))
        root(rstd2[:, 0:MEM], D)
        for k in range(KD + 1):
            if k < KD:
                tile = mark["ple"] + k
                act.wait_ge(sem["acc_ready"], tile + 1)
                if k >= 2:
                    act.wait_ge(sem["acc_free"], tile - 1)
                n.did(A.activation(gs[:, k % 2, :], acc[:, tile % 4, :], ACT.Sigmoid), sem["ple_sig"])
            if k:
                squares([e[:, k - 1, :]])
        root(rstd[:, :], D)
        squares(tiles(h))
        root(rstd[:, :], D)
        root(rstd_t[:, :], D)

        act.wait_ge(sem["gl_raw"], 1)
        flat = "p a b -> p (a b)"
        did(A.activation(glt[:, :, :].rearrange(flat), xg[:, :, :].rearrange(flat), ACT.Abs))
        did(A.activation(glt[:, :, :].rearrange(flat), glt[:, :, :].rearrange(flat), ACT.Exp, scale=-1.0))
        n.did(A.activation(glt[:, :, :].rearrange(flat), glt[:, :, :].rearrange(flat), ACT.Ln, bias=1.0),
              sem["gl_ln"])
        for lv in range(1, N_SUMS + 1):
            for hd in range(GH):
                act.wait_ge(sem["e_ready"], GH * (lv - 1) + hd + 1)
                if lv >= 3:
                    act.wait_ge(sem["acc_ready"], mark["pairs", lv - 2])
                n.did(A.activation(f[lv % 2][0:GDK, hd, :], ebank[hd][0:GDK, :], ACT.Exp), sem["f_ready"])
                n.tell(sem["e_free"])
        act.wait_ge(sem["gates_raw"], 1)
        n.did(A.activation(gg[:, :, :].rearrange(flat), gg[:, :, :].rearrange(flat), ACT.Silu),
              sem["gates_ready"])
        act.wait_ge(sem["osq_ready"], 1)
        n.did(A.activation(oroot[:, :], osum[:, :], ACT.Sqrt, scale=1.0 / GDV, bias=C("eps")),
              sem["oroot_ready"])
        softmaxes(list(memory_waves(mq1, mk1, mv1)), s_1, pt_1)
        squares(tiles(h))
        root(rstd[:, :], D)
        feed_forward("ffn1", ACT.Silu)
        squares(tiles(h))
        root(rstd[:, :], D)
        root(rstd_t[:, :], D)

        act.wait_ge(sem["z_done"], 1)
        load(mem2[0][:, :, :], mem_t, "in_mem2")
        squares(tiles(mem2[0]), lambda k: act.wait_ge(sem["in_mem2"], 16))
        nw = NG * NCMP
        for j in range(2):
            act.wait_ge(sem["hid_raw"], j + 1)
            n.did(A.activation(hid[:, j, 0:nw], hid[:, j, 0:nw], ACT.Silu), sem["hid_ready"])
        act.wait_ge(sem["acc_ready"], mark["windows"])
        act.wait_ge(sem["dist_out"], 16)
        width = TW - 1
        act.dma_start(toep[:, :, :], distances[:, P - 1:P - 1 + P * width]
                      .rearrange("h (p n) -> p h n", n=width)[:, :, 0:S]).then_inc(sem["in_toep"], 16)
        root(rstd2[:, 0:MEM], D)
        act.wait_ge(sem["gates_raw"], 2)
        n.did(A.activation(gt[:, :, :].rearrange(flat), gt[:, :, :].rearrange(flat), ACT.Sigmoid),
              sem["gates_ready"])
        softmaxes(list(branch_waves()) + list(memory_waves(mq2, mk2, mv2)), s_2, pt_2)
        squares(tiles(h))
        root(rstd[:, :], D)
        feed_forward("ffn2", ACT.Silu)
        squares(tiles(h))
        root(rstd[:, :], D)

    ctx.close()



def feature_major(x):
    x = np.asarray(x, np.float32)
    return np.ascontiguousarray(x.T.reshape(-1, P, x.shape[0]).transpose(1, 0, 2))


def kernel(**inputs):
    import concourse.bacc as bacc
    from concourse.bass_utils import run_bass_kernel_spmd as run

    a = {k: np.asarray(v) for k, v in inputs.items()}
    sums, masks = decay_tables()
    arrays = {
        "weights": weight_units(a),
        "x_t": feature_major(a["x"][0]),
        "p_t": feature_major(a["p"][0, 0]),
        "mem_t": feature_major(a["mem_2"][0]),
        "cols": columns(a),
        "rws": rows(a),
        "positions": np.ascontiguousarray(np.broadcast_to(a["positions"].astype(np.int32), (NOPE, S))),
        "rel": np.concatenate([a["rel_bias_2"], np.ones((1, NH), np.float32)]),
        "wgate": np.ascontiguousarray(a["gla_w_gate_up_2"][0]),
        "consts": fixed(),
        "chunk": chunk_mask(),
        "buckets": bucket_table(),
        "sums": sums.reshape(P, N_SUMS, P),
        "masks": masks.reshape(P, N_MASKS, P),
    }
    nc = bacc.Bacc("TRN2", target_bir_lowering=False, num_devices=1)
    args = [nc.dram_tensor(f"in_{k}", v.shape, mybir.dt.from_np(v.dtype), kind="ExternalInput").ap()
            for k, v in arrays.items()]
    args.append(nc.dram_tensor("out_t", (P, KD, S), F32, kind="ExternalOutput").ap())
    build_program(nc, *args)
    r = run(nc, [{f"in_{k}": v for k, v in arrays.items()}], core_ids=[0])
    y = r.results[0]["out_t"]
    return np.ascontiguousarray(y.transpose(2, 1, 0).reshape(1, S, D))
```

```python
from contextlib import ExitStack

import numpy as np

import concourse.bass as bass
from concourse import mybir

P = 128
S = 512
TT = S // P
D = 1024
KD = D // P
EPS = 1e-6
NEG = -1e30
CONV = 512
KC_ = CONV // P
Q_LORA, KV_LORA = 384, 256
HA, NOPE, ROPE, VD = 8, 64, 32, 64
QK = NOPE + ROPE
ROPE_THETA = 10000.0
F_DIM = 2816
KF_ = F_DIM // P
PLE = 256
MEM = 256
MH, MDH = 4, 64
GH, GDK, GDV, GR = 4, 96, 192, 16
NH, NG, NDH = 12, 4, 64
REP = NH // NG
CMP_B, CMP_S, CMP_H = 32, 16, 128
NCMP = (S - CMP_B) // CMP_S + 1
LP = CMP_B // 2
BUCKETS, MAX_DIST = 32, 128
RING = 4
RAW = 2
UNIT = 1024
LEVELS = 7
S_CMP = (1 + 2 + 3 + 4) * P
SW = S_CMP + P
S_BUFS = 3
WIDE = 3
TW = 640

ALU = mybir.AluOpType
ACT = mybir.ActivationFunctionType
F32 = mybir.dt.float32
F32R = mybir.dt.float32r
I32 = mybir.dt.int32
AX = mybir.AxisListType.X

NSA_ORDER = [(REP * (2 * t + g) + r) for t in range(NG // 2) for r in range(REP) for g in range(2)]



def _pack(blocks):
    units, at = [], UNIT
    for b in blocks:
        if at + b.shape[1] > UNIT:
            units.append(np.zeros((P, UNIT), np.float32))
            at = 0
        units[-1][:b.shape[0], at:at + b.shape[1]] = b
        at += b.shape[1]
    return units


def _cols(w, first, n=P):
    out = []
    for k in range(-(-w.shape[0] // P)):
        b = np.zeros((P, P), np.float32)
        rows = w[k * P:(k + 1) * P, first:first + n]
        b[:rows.shape[0], :rows.shape[1]] = rows
        out.append(b)
    return out


def _moving(w, first, n):
    return [w[k * P:(k + 1) * P, first:first + n] for k in range(w.shape[0] // P)]


def weight_units(a):
    u = []

    def tiles(w, firsts, n=P):
        u.extend(_pack([b for f in firsts for b in _cols(w, f, n)]))

    def spread(cols_):
        u.extend(_pack([c[k] for k in range(KD) for c in cols_[:WIDE]] + sum(cols_[WIDE:], [])))

    def starts(w, firsts, n=P):
        return [_cols(w, f, n) for f in firsts]

    def ffn(up, down):
        spread(starts(up, [f + h for f in range(0, F_DIM, P) for h in (0, F_DIM)]))
        for f in range(0, D, P):
            u.extend(_pack(_cols(down, f)))

    def memory(w):
        k, v = starts(w, [0, P]), _moving(w, MH * MDH, MH * MDH)
        u.extend(_pack([b for x in zip(*k, v) for b in x]))

    w = a["w_in"][0]
    c = CONV
    spread(starts(w, [x + i * P for i in range(KC_) for x in (c, 2 * c, 0)]))
    at = 3 * CONV
    tiles(w, range(at, at + Q_LORA + KV_LORA, P))
    at += Q_LORA + KV_LORA
    r = w[:, at:at + ROPE]
    h = ROPE // 2
    turned = np.concatenate([r[:, h:], r[:, :h]], 1)
    tiles(np.concatenate([np.zeros((D, NOPE), np.float32), r, turned], 1), [0])
    at += ROPE
    tiles(w, range(at, at + 2 * D, P))
    q = a["w_q_up"][0].reshape(Q_LORA, HA, QK)
    q = np.concatenate([q, q[:, :, NOPE + h:], q[:, :, NOPE:NOPE + h]], 2).reshape(Q_LORA, HA * P)
    tiles(q, range(0, HA * P, P))
    kv = a["w_kv_up"][0].reshape(KV_LORA, HA, NOPE + VD)
    tiles(kv[:, :, :NOPE].reshape(KV_LORA, -1), range(0, HA * NOPE, P))
    u.extend(_pack(_moving(kv[:, :, NOPE:].reshape(KV_LORA, -1), 0, HA * VD)))
    tiles(a["w_a_out"][0], range(0, D, P))
    tiles(a["w_b_out"][0], range(0, D, P))
    tiles(a["w_o"][0], range(0, D, P))
    memory(a["w_mem_kv_2"][0])
    ffn(a["w_ffn_up"][0], a["w_ffn_down"][0])
    tiles(a["w_ple_proj"][0], range(0, D, P))
    spread(starts(a["w_ple_gate"][0], range(0, D, P)))

    memory(a["w_mem_kv_2"][1])
    w = a["gla_w_in_2"][0]
    nk, nv = GH * GDK, GH * GDV
    spread(starts(w, [2 * nk + 2 * nv], GR) + starts(w, range(0, 2 * nk, GDK), GDK)
           + starts(w, [2 * nk + 2 * nv + GR + i * P for i in range(2)]))
    for first in range(2 * nk, 2 * nk + 2 * nv, 256):
        u.extend(_pack(_moving(w, first, 256)))
    spread(starts(a["w_out_2"][0], range(0, D, P)))
    ffn(a["w_up_2"][0], a["w_down_2"][0])

    w = a["w_kv_shared_2"]
    nk = NG * NDH
    spread(starts(w, [j * nk + i * P for j in (0, 1, 2, 4) for i in range(2)]))
    for j in (3, 5):
        u.extend(_pack(_moving(w, j * nk, nk)))
    w = a["nsa_w_in_2"][0]
    nq = NH * NDH
    heads = [w[:, NDH * x:NDH * (x + 1)] for x in NSA_ORDER]
    spread(starts(np.concatenate(heads, 1), range(0, nq, P)))
    for j in range(2):
        tiles(a["cmp_w1_2"][j], [0])
    tiles(w, [nq + 3 * NH + i * P for i in range(2)])
    tiles(w, [nq], 3 * NH)
    tiles(a["w_out_2"][1], range(0, D, P))
    ffn(a["w_up_2"][1], a["w_down_2"][1])
    return np.stack(u)


def _column_layout():
    at, where = 0, {}
    for name, n in [("mix_pre", 8), ("q_lat", 3), ("kv_lat", 2), ("mix_post", 8), ("ffn_pre", 8),
                    ("ffn_post", 8), ("ple_post", 8), ("conv_a", 3 * KC_), ("ffn0", 8 * KF_),
                    ("ffn1", 8 * KF_), ("ffn2", 8 * KF_), ("nmix0", 8), ("nmix1", 8), ("nmem0", 8),
                    ("nmem1", 8), ("nffn1", 8), ("nffn2", 8), ("nkv", 8), ("final", 8), ("cb1", 2),
                    ("cb2", 1), ("pos0", LP), ("pos1", LP), ("w2_0", NDH), ("w2_1", NDH),
                    ("eps", 1), ("inv", 1), ("quarter", 1), ("halfpi", 1), ("sign", 1), ("valid", 1)]:
        where[name] = at
        at += n
    return where, at


COL, N_COL = _column_layout()
ROW = {"bgate": 0, "onorm": GH * GDK, "cb2r": GH * GDK + GDV}
N_ROW = GH * GDK + GDV + NDH


def columns(a):
    out = np.zeros((P, N_COL), np.float32)

    def put(name, v, step=1, shift=0):
        m = np.asarray(v, np.float32).reshape(-1, P).T
        at = COL[name] + shift
        out[:, at:at + step * m.shape[1]:step] = m

    put("mix_pre", a["g_mix_pre"][0])
    put("q_lat", a["g_q_lat"][0])
    put("kv_lat", a["g_kv_lat"][0])
    put("mix_post", a["g_mix_post"][0])
    put("ffn_pre", a["g_ffn_pre"][0])
    put("ffn_post", a["g_ffn_post"][0])
    put("ple_post", a["g_ple_post"][0])
    for j in range(3):
        put("conv_a", a["conv_a_w"][0, j], 3, j)
    for name, w, b in (("ffn0", a["conv_ffn_w"][0], a["b_ffn_conv"][0]),
                       ("ffn1", a["conv_w_2"][0], a["conv_b_2"][0]),
                       ("ffn2", a["conv_w_2"][1], a["conv_b_2"][1])):
        for half in range(2):
            part = slice(half * F_DIM, (half + 1) * F_DIM)
            for j in range(3):
                put(name, w[j, part], 8, 4 * half + j)
            put(name, b[part], 8, 4 * half + 3)
    for i in range(2):
        put(f"nmix{i}", a["norm_mix_2"][i])
        put(f"nmem{i}", a["norm_mem_2"][i])
        put(f"nffn{i + 1}", a["norm_ffn_2"][i])
        out[:, COL["cb1"] + i] = a["cmp_b1_2"][i]
        at = COL[f"pos{i}"]
        out[:, at:at + LP] = a["cmp_pos_2"][i].reshape(LP, P).T
        at = COL[f"w2_{i}"]
        out[:, at:at + NDH] = a["cmp_w2_2"][i]
    put("nkv", a["kv_norm_2"])
    put("final", a["final_norm_2"])
    out[:NDH, COL["cb2"]] = a["cmp_b2_2"][0]
    out[NDH:, COL["cb2"]] = a["cmp_b2_2"][0]
    half = ROPE // 2
    inv = (1.0 / (np.float32(ROPE_THETA) ** (np.arange(half, dtype=np.float32)
                                              * np.float32(2.0 / ROPE)))).astype(np.float32)
    out[NOPE:, COL["inv"]] = np.tile(inv, 4)
    out[:, COL["eps"]] = EPS
    out[NOPE:NOPE + ROPE, COL["quarter"]] = 0.25
    out[NOPE:NOPE + ROPE, COL["halfpi"]] = np.pi / 2
    out[:, COL["sign"]] = 1.0
    out[NOPE + ROPE:NOPE + ROPE + half, COL["sign"]] = -1.0
    out[CMP_B - 1:, COL["valid"]] = 1.0
    return out


def rows(a):
    r = np.concatenate([a["gla_b_gate_2"][0], a["gla_out_norm_2"][0], a["cmp_b2_2"][1]])
    return np.ascontiguousarray(np.broadcast_to(r, (P, N_ROW)))


def bucket_table():
    out = np.zeros((BUCKETS + 1, TW), np.float32)
    exact = BUCKETS // 2
    for n in range(TW):
        d = S - 1 - n
        if d < 0:
            out[BUCKETS, n] = NEG
            continue
        large = exact + int(np.log(max(d, 1) / exact) / np.log(MAX_DIST / exact) * (BUCKETS - exact))
        out[d if d < exact else min(large, BUCKETS - 1), n] = 1.0
    return out


CONST = {"ident": 0, "ones": P}
N_CONST = 2 * P


def fixed():
    out = np.zeros((P, N_CONST), np.float32)
    out[:, :P] = np.eye(P)
    out[:, P:2 * P] = 1.0
    return out


def chunk_mask():
    out = np.zeros((P, S), np.float32)
    out[:64, S - 64:] = NEG
    return out


def decay_tables():
    t, i = np.arange(P)[:, None], np.arange(P)[None, :]
    sums, masks = [], [np.eye(P)]
    for lv in range(1, LEVELS + 1):
        b = 2 ** lv
        mid = i // b * b + b // 2 - 1
        late = i > mid
        sums.append(np.where(late, (t > mid) & (t <= i), (t > i) & (t <= mid)))
        j = np.arange(P)[:, None]
        masks.append((j // b == i // b) & (j % b < b // 2) & (i % b >= b // 2))
    sums += [t <= i, t > i]
    return (np.concatenate(sums, 1).astype(np.float32) / 16.0,
            np.concatenate(masks, 1).astype(np.float32))


N_SUMS, N_MASKS = LEVELS + 2, LEVELS + 1

U_FFN_UP, U_FFN_DOWN = 2 * KF_, 3 * KD
N_UNITS = (34 + 3 + 2 + 4 + 4 + 8 + U_FFN_UP + U_FFN_DOWN + 2 + 8
           + 4 + 11 + 12 + 8 + U_FFN_UP + U_FFN_DOWN
           + 8 + 4 + 4 + 4 + 9 + 8 + U_FFN_UP + U_FFN_DOWN)


class Count:

    def __init__(self, eng):
        self.eng, self.n, self.loop = eng, {}, None

    def did(self, ins, sem, wait=True):
        ins.then_inc(sem, 1)
        self.n[sem] = self.n.get(sem, 0) + 1
        if wait:
            self.eng.wait_ge(sem, self.at(sem))

    def tell(self, sem):
        self.eng.sem_inc(sem, 1)
        self.n[sem] = self.n.get(sem, 0) + 1

    def at(self, sem):
        n = self.n.get(sem, 0)
        if self.loop is None:
            return n
        i, start, per = self.loop
        return i * per[sem] + n if sem in per else n

    def enter(self, i, per):
        self.loop = (i, dict(self.n), per)

    def leave(self, turns):
        _, start, per = self.loop
        for sem, n in self.n.items():
            made = n - start.get(sem, 0)
            assert made == per.get(sem, 0), (sem.name, made)
            self.n[sem] = start.get(sem, 0) + turns * made
        self.loop = None


def build_program(nc, weights, x_t, p_t, mem_t, cols, rws, positions, rel, wgate, consts, chunk, buckets,
                  sums, masks, out):
    ctx = ExitStack()
    base = [17408]

    def fix(name, shape, dt=F32):
        t = nc.alloc_sbuf_tensor_at(name, shape, dt, offset=base[0])
        base[0] += -(-int(np.prod(shape[1:])) * 4 // 32) * 32
        return t

    wraw = fix("wraw", [P, RAW, UNIT])
    whi = fix("whi", [P, RING, UNIT], F32R)
    wlo = fix("wlo", [P, RING, UNIT], F32R)
    h = fix("h", [P, KD, S])
    x_at = base[0]
    xhi = fix("xhi", [P, KD, S], F32R)
    xlo = fix("xlo", [P, KD, S], F32R)
    col = fix("col", [P, N_COL])
    row = fix("row", [P, N_ROW])
    const = fix("const", [P, N_CONST])
    rstd = fix("rstd", [P, S])
    u = fix("u", [P, 2, S + 2])
    rstd2 = nc.alloc_sbuf_tensor_at("rstd2", [P, S], F32, offset=base[0] - 4128)
    tmp = nc.alloc_sbuf_tensor_at("tmp", [P, S], F32, offset=base[0] - 2048)
    sqsum = fix("sqsum", [P, S])
    sq = fix("sq", [P, 2, S])
    rstd_t = fix("rstd_t", [P, 4])
    mkt = [fix(f"mkt{i}", [P, 2, MEM]) for i in range(2)]
    mv = [fix(f"mv{i}", [P, 2, MH * MDH]) for i in range(2)]
    rstd_m = fix("rstd_m", [P, MEM])
    rstd_mt = fix("rstd_mt", [P, 2])
    stat = fix("stat", [P, S_BUFS, 4, 8])
    spare = fix("spare", [P, 1])
    decay = fix("decay", [P, GH * TT])
    osum = fix("osum", [P, GH * TT])
    oroot = fix("oroot", [P, GH * TT])
    arena = base[0]
    KB = 1024

    def put(name, shape, at, dt=F32):
        assert arena + at + int(np.prod(shape[1:])) * 4 <= 229344, (name, arena, at)
        return nc.alloc_sbuf_tensor_at(name, shape, dt, offset=arena + at)

    fhi = put("fhi", [P, KF_, S], 0, F32R)
    flo = put("flo", [P, KF_, S], 44 * KB, F32R)
    sg = put("sg", [P, 2 * KD, S], 0)
    lat = put("lat", [P, 5, S], 32 * KB)
    lathi = put("lathi", [P, 5, S], 42 * KB, F32R)
    latlo = put("latlo", [P, 5, S], 52 * KB, F32R)
    yhi = put("yhi", [P, KC_, S], 62 * KB, F32R)
    ylo = put("ylo", [P, KC_, S], 70 * KB, F32R)
    va = put("va", [P, TT, HA * VD], 78 * KB)
    cs = put("cs", [P, S], 86 * KB)
    kpe = put("kpe", [P, S], 84 * KB)
    chunkm = put("chunkm", [P, S], 88 * KB)
    prod = put("prod", [P, S + 2], 78 * KB)
    rstd3 = put("rstd3", [P, S], 78 * KB)
    cv = put("cv", [P, S], 80 * KB + 64)
    pos_i = nc.alloc_sbuf_tensor_at("pos_i", [P, S], I32, offset=arena + 32 * KB)
    ang = put("ang", [P, 3, S], 34 * KB)
    relv = put("relv", [P, 16], 42 * KB)
    bk = put("bk", [P, TW], 42 * KB + 64)
    vr = put("vr", [P, TW], 45 * KB)
    s_a = put("s_a", [P, S_BUFS, SW], 32 * KB)
    pt_a = put("pt_a", [P, 2, S_CMP], 50 * KB)
    qf = nc.alloc_sbuf_tensor_at("qf", [P, HA, S], F32, offset=x_at)
    kf = nc.alloc_sbuf_tensor_at("kf", [P, HA, S], F32, offset=x_at + 16 * KB)
    y_o = put("y_o", [P, KD, S], 32 * KB)
    y_d = nc.alloc_sbuf_tensor_at("y_d", [P, KD, S], F32, offset=x_at + 16 * KB)
    p_f = nc.alloc_sbuf_tensor_at("p_f", [P, 2, S], F32, offset=x_at)
    p_hi = nc.alloc_sbuf_tensor_at("p_hi", [P, 2, S], F32R, offset=x_at + 4 * KB)
    p_lo = nc.alloc_sbuf_tensor_at("p_lo", [P, 2, S], F32R, offset=x_at + 8 * KB)
    e = put("e", [P, KD, S], 0)
    gs = put("gs", [P, 2, S], 40 * KB)
    qg = put("qg", [P, GH, S], 0)
    kg = put("kg", [P, GH, S], 8 * KB)
    vg = put("vg", [P, TT, GH * GDV], 16 * KB)
    gg = put("gg", [P, TT, GH * GDV], 28 * KB)
    la = put("la", [P, TT, GH * GDK], 40 * KB)
    kout = put("kout", [P, TT, GH * GDK], 40 * KB)
    f = [put(f"f{i}", [P, GH, S], (46 + 8 * i) * KB) for i in range(2)]
    xg = put("xg", [P, TT, GH * GDK], 54 * KB)
    at_ = put("at_", [P, GH, S], 62 * KB)
    dm = put("dm", [P, N_SUMS, P], 70 * KB)
    mk = put("mk", [P, N_MASKS, P], 75 * KB)
    mq1 = put("mq1", [P, 2, S], 79 * KB)
    st = put("st", [P, GH, GDV], 87 * KB)
    lr = put("lr", [P, S], 62 * KB)
    wg = put("wg", [P, GH * GDK], 64 * KB)
    glt = put("glt", [P, TT, GH * GDK], 46 * KB)
    o_g = put("o_g", [P, TT, GH * GDV], 46 * KB)
    s_1 = put("s_1", [P, S_BUFS, SW], 0)
    pt_1 = put("pt_1", [P, 2, 2 * S], 62 * KB)
    mem = [[put(f"mem{i}", [P, KD, MEM], a * KB), put(f"mem{i}hi", [P, KD, MEM], b * KB, F32R),
            put(f"mem{i}lo", [P, KD, MEM], c * KB, F32R)] for i, (a, b, c) in
           enumerate([(80, 64, 72), (16, 24, 32)])]
    qn = put("qn", [P, 6, S], 0)
    toep = put("toep", [P, NH, S], 12 * KB)
    kn = [put("ks", [P, 2, S], 36 * KB), put("kw", [P, 2, S], 40 * KB)]
    vn = [put("vs", [P, TT, NG * NDH], 44 * KB), put("vw", [P, TT, NG * NDH], 48 * KB)]
    kc = put("kc", [P, 2, 32], 52 * KB)
    vc = put("vc", [P, NG * NDH], 52 * KB + 256)
    gt = put("gt", [P, TT, 3 * NH], 52 * KB + 1280)
    mq2 = put("mq2", [P, 2, S], 86 * KB + 512)
    s_2 = put("s_2", [P, S_BUFS, SW], 54 * KB)
    pt_2 = put("pt_2", [P, 2, S_CMP + S], 70 * KB + 512)
    z = put("z", [P, NG, S], 12 * KB)
    zw = put("zw", [P, LP, NG * NCMP], 20 * KB)
    zhi = [put(f"zhi{j}", [P, LP, NG * NCMP], at * KB, F32R) for j, at in enumerate((62, 78))]
    zlo = [put(f"zlo{j}", [P, LP, NG * NCMP], at * KB, F32R) for j, at in enumerate((70, 54))]
    hid = sq

    acc = ctx.enter_context(nc.psum_tensor("acc", [P, 4, S], F32))
    sc = ctx.enter_context(nc.psum_tensor("sc", [P, 2, S], F32))
    ptp = ctx.enter_context(nc.psum_tensor("ptp", [P, S], F32))
    pv = ctx.enter_context(nc.psum_tensor("pv", [P, S], F32))
    pvs = [ptp[:, :], pv[:, :]]
    ebank = [sc[:, 0, :], sc[:, 1, :], ptp[:, :], pv[:, :]]
    distances = nc.dram_tensor("distances", [NH, P * TW], F32, kind="Internal").ap()

    ident, ones = const[:, 0:P], const[:, P:2 * P]

    def C(name, i=0, n=1, p=slice(None)):
        return col[p, COL[name] + i:COL[name] + i + n]

    def plain(ap):
        return ap.bitcast(F32)

    names = ("w_open w_split out_ready out_done w_used w_hi acc_free x_ready acc_ready ss_added rs_ready e_free "
             "o_free bc_ready sc_free sc_ready pn_ready t_copied t_ready pv_done in_rel in_bk in_const "
             "qkv_ready lr_ready in_wg in_sums la_ready e_ready g_ready kout_ready st_ready og_ready "
             "hid_ready gln_ready in_toep dve_step sq_ready src_ready u_ready c_ready a_ready v_ready "
             "s_ready p_ready vr_ready in_col in_pos angle_ready sine_ready dist_out gate_in sig_ready "
             "in_chunk in_p ple_sig gl_raw gl_ln in_masks f_ready gates_raw o_raw oroot_ready "
             "gates_ready hid_raw act_step in_row in_mem0 in_mem1 z_done hi_ready kpe_ready q_copied e_copied").split()
    sem = {n: ctx.enter_context(nc.semaphore(n)) for n in names}
    loaded = [ctx.enter_context(nc.semaphore(f"w_loaded{j}")) for j in range(RING)]
    in_x = [ctx.enter_context(nc.semaphore(f"in_x{j}")) for j in range(4)]
    mark = {}

    def causal_wave(q, k, bias, v, dest, **more):
        offs = [sum(range(i + 1)) * P for i in range(TT)]
        items = [dict(bank=i, col=0, q=q(i), k=k(slice(0, (i + 1) * P)), n=(i + 1) * P,
                      bias=bias[:, S - (i + 1) * P:S], off=offs[i]) for i in range(TT)]
        turns = [dict(width=P, first=b, v=v(b), src=[offs[i] + b * P for i in range(b, TT)])
                 for b in range(TT)]
        return dict(items=items, turns=turns, dest=dest, scale=1.0, gates=[], opens=True, closes=True) | more

    def place(w, k):
        at = sum(len(x["src"]) for x in w["turns"][:k]) * P
        return at, at + len(w["turns"][k]["src"]) * P

    def last_on(w, k, before):
        a0, a1 = place(w, k)
        return max([j + 1 for j in range(len(before["turns"]))
                    if place(before, j)[0] < a1 and a0 < place(before, j)[1]], default=0)

    def latent_waves():
        for hd in range(HA):
            yield causal_wave(lambda i: qf[0:QK, hd, i * P:(i + 1) * P], lambda w: kf[0:QK, hd, w], chunkm,
                              lambda b: va[:, b, hd * VD:(hd + 1) * VD],
                              (yhi, ylo, hd // 2, hd % 2 * VD), scale=QK ** -0.5)

    def memory_waves(mq, layer):
        for hd in range(MH):
            p = slice(hd % 2 * MDH, hd % 2 * MDH + MDH)
            items = [dict(bank=i, col=0, q=mq[p, hd // 2, i * P:(i + 1) * P], k=mkt[layer][p, hd // 2, :], n=MEM,
                          bias=None, off=MEM * i) for i in range(TT)]
            turns = [dict(width=P, first=0, v=mv[layer][:, b, hd * MDH:(hd + 1) * MDH],
                          src=[MEM * i + b * P for i in range(TT)]) for b in range(MEM // P)]
            yield dict(items=items, turns=turns, dest=(xhi, xlo, 6 + hd // 2, hd % 2 * MDH), scale=1.0,
                       gates=[], opens=True, closes=True)

    def branch_waves():
        def head(hd, b):
            g, r = hd // REP, hd % REP
            p = slice(g % 2 * NDH, g % 2 * NDH + NDH)
            vcols = slice(g * NDH, (g + 1) * NDH)

            def q(i):
                return qn[p, g // 2 * REP + r, i * P:(i + 1) * P]

            w = causal_wave(q, lambda keys: kn[b][p, g // 2, keys], toep[:, hd, :],
                            lambda kb: vn[b][:, kb, vcols], (xhi, xlo, hd // 2, hd % 2 * NDH),
                            opens=b == 0, closes=b == 1)
            w["gates"] = [(0, gt[:, :, 3 * hd + 1 + b])]
            if b == 0:
                for i in range(TT):
                    n = min(NCMP, 7 + 8 * i)
                    first = S - P + CMP_B - 1 - P * i
                    w["items"].insert(i + 1, dict(
                        bank=0, col=P + 32 * i, q=q(i), k=kc[p, g // 2, 0:n], n=n,
                        bias=toep[:, hd, first:first + CMP_S * (n - 1) + 1:CMP_S], off=S_CMP + 32 * i))
                w["turns"].append(dict(width=32, first=0, v=vc[0:32, vcols],
                                       src=[S_CMP + 32 * i for i in range(TT)]))
                w["gates"] = [(1, gt[:, :, 3 * hd]), (5, gt[:, 1:TT, 3 * hd + 1]), (0, gt[:, 0:1, 3 * hd + 1])]
                w["valid"] = 1
            return w

        for pair in range(0, NH, 2):
            for b in range(2):
                for hd in (pair, pair + 1):
                    yield head(hd, b)

    block = ctx.enter_context(nc.Block(no_gpsimd_drain=False))

    @block.sync
    def _(sp):
        def load(unit, j):
            sp.dma_start(wraw[:, j % RAW, :], weights[unit]).then_inc(loaded[j], 16)

        for j in range(4):
            sp.dma_start(h[:, 2 * j:2 * j + 2, :], x_t[:, 2 * j:2 * j + 2, :]).then_inc(in_x[j], 16)
            if j < RAW:
                load(j, j)
        for j in range(RAW, RING):
            sp.wait_ge(sem["w_split"], j - RAW + 1)
            load(j, j)
        with sp.Fori(1, N_UNITS // RING) as i:
            for j in range(RING):
                sp.wait_ge(sem["w_split"], i * RING + (j - RAW + 1))
                load(i * RING + j, j)
        for unit in range(N_UNITS // RING * RING, N_UNITS):
            sp.wait_ge(sem["w_split"], unit - RAW + 1)
            load(unit, unit % RING)
        for k in range(KD):
            sp.wait_ge(sem["out_ready"], k + 1)
            sp.dma_start(out[:, k, :], h[:, k, :]).then_inc(sem["out_done"], 16)
        sp.wait_ge(sem["out_done"], 16 * KD)

    @block.gpsimd
    def _(pool):
        def split(unit, j, turn, used):
            pool.wait_ge(loaded[j], turn)
            if used is not None:
                pool.wait_ge(sem["w_used"], used)
            pool.sem_inc(sem["w_open"], 1)
            nc.gpsimd.tensor_scalar(whi[:, j, :], wraw[:, j % RAW, :], 1.0, 1.0, ALU.mult, ALU.mult).then_inc(sem["w_hi"], 1)
            pool.wait_ge(sem["w_hi"], unit + 1)
            nc.gpsimd.tensor_tensor(wlo[:, j, :], wraw[:, j % RAW, :], plain(whi[:, j, :]),
                                    ALU.subtract).then_inc(sem["w_split"], 1)

        for j in range(RING):
            split(j, j, 16, None)
        with pool.Fori(1, N_UNITS // RING) as i:
            for j in range(RING):
                split(i * RING + j, j, i * 16 + 16, i * RING + (j - RING + 1))
        for unit in range(N_UNITS // RING * RING, N_UNITS):
            split(unit, unit % RING, 16 * (unit // RING + 1), unit - RING + 1)

    @block.tensor
    def _(pe):
        t = 0
        un = 0
        xs = 0
        bc = 0
        ss = 0
        steps_done = pairs_done = e_done = 0
        turned = banks = 0

        def bank(tile, n=S, p=P):
            return acc[0:p, tile % 4, 0:n]

        def open_tile(tile, turn=None):
            if turn is not None:
                pe.wait_ge(sem["acc_free"], turn)
            elif tile >= 4:
                pe.wait_ge(sem["acc_free"], tile - 3)

        def three(o, a_hi, a_lo, b_hi, b_lo, start, stop, begins=False, done=None):
            m = nc.tensor.matmul(o, a_hi, b_hi, start=start, stop=False)
            if begins:
                m.then_inc(sem["w_used"], 1)
            nc.tensor.matmul(o, a_lo, b_hi, start=False, stop=False)
            m = nc.tensor.matmul(o, a_hi, b_lo, start=False, stop=stop)
            if done is not None:
                m.then_inc(done, 1)

        def spread(x_hi, x_lo, arrivals=None, between=None):
            nonlocal t, un
            if arrivals is None:
                arrivals = {k: xs + k + 1 for k in range(KD)}
            for m in range(WIDE):
                open_tile(t + m)
            for k in range(KD):
                if between and k in between:
                    between[k]()
                if k in arrivals:
                    pe.wait_ge(sem["x_ready"], arrivals[k])
                for m in range(WIDE):
                    piece = k * WIDE + m
                    if piece % 8 == 0:
                        pe.wait_ge(sem["w_split"], un + 1)
                    slot, c = un % RING, piece % 8 * P
                    three(bank(t + m), whi[:, slot, c:c + P], wlo[:, slot, c:c + P], x_hi[:, k, :],
                          x_lo[:, k, :], k == 0, k == KD - 1, piece % 8 == 0 and un > 0,
                          sem["acc_ready"] if k == KD - 1 else None)
                    un += piece % 8 == 7
            t += WIDE

        def stationary(x_hi, x_lo, kts, tiles, n=S, fresh=0, late=None, between=None):
            nonlocal t, un
            piece = 0
            for m in range(tiles):
                open_tile(t)
                for k in range(kts):
                    if piece % 8 == 0:
                        pe.wait_ge(sem["w_split"], un + 1)
                    if m == 0 and k < fresh and (late is None or k == 0 or k > late):
                        pe.wait_ge(sem["x_ready"], xs + (k if late is None else max(k, late)) + 1)
                    if between and m in between and k == kts // 4:
                        between[m]()
                    slot, c = un % RING, piece % 8 * P
                    three(bank(t, n), whi[:, slot, c:c + P], wlo[:, slot, c:c + P], x_hi[:, k, 0:n],
                          x_lo[:, k, 0:n], k == 0, k == kts - 1, piece % 8 == 0 and un > 0,
                          sem["acc_ready"] if k == kts - 1 else None)
                    piece += 1
                    if piece % 8 == 0 or (m == tiles - 1 and k == kts - 1):
                        piece = -(-piece // 8) * 8
                        un += 1
                t += 1

        def stationary_loop(x_hi, x_lo, turns, groups=4, kts=KD):
            nonlocal t, un
            per = -(-kts // 8)
            assert groups % 4 == 0
            with pe.Fori(0, turns) as i:
                for m in range(groups):
                    open_tile(t + m, i * groups + (t + m - 3))
                    for k in range(kts):
                        unit = m * per + k // 8
                        if k % 8 == 0:
                            pe.wait_ge(sem["w_split"], i * (groups * per) + (un + unit + 1))
                        slot, c = (un + unit) % RING, k % 8 * P
                        three(bank(t + m), whi[:, slot, c:c + P], wlo[:, slot, c:c + P], x_hi[:, k, :],
                              x_lo[:, k, :], k == 0, k == kts - 1, k % 8 == 0,
                              sem["acc_ready"] if k == kts - 1 else None)
            t += turns * groups
            un += turns * groups * per

        def moving(x_hi, x_lo, kts, n, tiles=TT):
            nonlocal t, un
            for i in range(tiles):
                open_tile(t + i)
            per = UNIT // n
            for k in range(kts):
                if k % per == 0:
                    pe.wait_ge(sem["w_split"], un + 1)
                slot, c = un % RING, k % per * n
                for i in range(tiles):
                    a = slice(i * P, (i + 1) * P)
                    three(bank(t + i, n), x_hi[:, k, a], x_lo[:, k, a], whi[:, slot, c:c + n],
                          wlo[:, slot, c:c + n], k == 0, k == kts - 1, k % per == 0 and i == 0,
                          sem["acc_ready"] if k == kts - 1 else None)
                if k % per == per - 1 or k == kts - 1:
                    un += 1
            t += tiles

        def half_moving(half):
            nonlocal t, un
            for i in range(2):
                open_tile(t + i)
            for k in range(KD):
                if k % 4 == 0:
                    pe.wait_ge(sem["w_split"], un + k // 4 + 1)
                slot, c = (un + k // 4) % RING, k % 4 * 256
                for i in range(2):
                    a = slice((2 * half + i) * P, (2 * half + i + 1) * P)
                    three(bank(t + i, 256), xhi[:, k, a], xlo[:, k, a], whi[:, slot, c:c + 256],
                          wlo[:, slot, c:c + 256], k == 0, k == KD - 1, half and k % 4 == 0 and i == 0,
                          sem["acc_ready"] if k == KD - 1 else None)
            un += 2 * half
            t += 2

        def sum_features(n, cols_=S):
            nonlocal bc, ss
            ss += n
            pe.wait_ge(sem["ss_added"], ss)
            if bc:
                pe.wait_ge(sem["rs_ready"], bc)
            if e_done:
                pe.wait_ge(sem["e_free"], e_done)
            if pairs_done:
                pe.wait_ge(sem["o_free"], pairs_done)
            nc.tensor.matmul(pv[:, 0:cols_], ones, sqsum[:, 0:cols_], start=True, stop=True)\
                .then_inc(sem["bc_ready"], 1)
            bc += 1

        def sum_tokens(tiles=TT):
            nonlocal bc
            pe.wait_ge(sem["rs_ready"], bc)
            for i in range(tiles):
                m = nc.tensor.matmul(pv[:, i:i + 1], sqsum[:, i * P:(i + 1) * P], ones[:, 0:1],
                                     start=True, stop=True)
            m.then_inc(sem["bc_ready"], 1)
            bc += 1

        def memory(layer, between):
            nonlocal t, un, xs
            _, m_hi, m_lo = mem[layer]
            for i in range(4):
                open_tile(t + i)
            for k in range(KD):
                pe.wait_ge(sem["x_ready"], xs + k + 1)
                if k % 2 == 0:
                    pe.wait_ge(sem["w_split"], un + 1)
                if k == 2:
                    between()
                slot, c = un % RING, k % 2 * (UNIT // 2)
                first, last = k == 0, k == KD - 1
                done = sem["acc_ready"] if last else None
                for i in range(2):
                    w = slice(c + i * P, c + (i + 1) * P)
                    three(bank(t + i, MEM), whi[:, slot, w], wlo[:, slot, w], m_hi[:, k, :], m_lo[:, k, :],
                          first, last, k % 2 == 0 and i == 0, done)
                w = slice(c + 2 * P, c + UNIT // 2)
                for i in range(2):
                    a = slice(i * P, (i + 1) * P)
                    three(bank(t + 2 + i, MH * MDH), m_hi[:, k, a], m_lo[:, k, a], whi[:, slot, w],
                          wlo[:, slot, w], first, last, done=done)
                un += k % 2
            t += 4
            xs += KD

        def attention(waves, s, pts):
            nonlocal steps_done, turned, banks
            pe.wait_ge(sem["acc_free"], t)
            if e_done:
                pe.wait_ge(sem["e_free"], e_done)
            pe.wait_ge(sem["rs_ready"], bc)

            def scores(w):
                nonlocal banks
                for b in range(TT):
                    if banks >= TT:
                        pe.wait_ge(sem["sc_free"], banks - TT + 1)
                    for x in [x for x in w["items"] if x["bank"] == b]:
                        m = nc.tensor.matmul(acc[:, b, x["col"]:x["col"] + x["n"]], x["q"], x["k"],
                                             start=True, stop=True)
                    m.then_inc(sem["sc_ready"], 1)
                    banks += 1

            def turn(w, k):
                nonlocal turned
                if turned >= 2:
                    pe.wait_ge(sem["t_copied"], turned - 1)
                x = w["turns"][k]
                for b, c in enumerate(x["src"]):
                    m = nc.tensor.transpose(sc[0:x["width"], turned % 2, b * P:(b + 1) * P],
                                            w["s"][:, c:c + x["width"]], ident)
                m.then_inc(sem["t_ready"], 1)
                turned += 1

            def values(pair, k):
                nonlocal pairs_done
                last = k == len(pair[1]["turns"]) - 1
                pe.wait_ge(sem["t_copied"], pair[1]["at"] + k + 1)
                if pair[0]["opens"] and k == 0 and pairs_done >= 2:
                    pe.wait_ge(sem["o_free"], pairs_done - 1)
                for odd, w in enumerate(pair):
                    x = w["turns"][k]
                    n, (c0, c1) = len(x["src"]) * P, place(w, k)
                    m = nc.tensor.matmul(pvs[pairs_done % 2][odd * 64:odd * 64 + 64, S - n:S], x["v"],
                                         pts[0:x["width"], odd, c0:c1], start=w["opens"] and k == 0,
                                         stop=w["closes"] and last, skip_group_check=True)
                m.then_inc(sem["pv_done"], 1)
                pairs_done += last and pair[0]["closes"]

            for i in range(-1, len(waves) + 2):
                w = waves[i - 1] if 0 <= i - 1 < len(waves) else None
                odd = (i - 1) % 2
                before = waves[i - 3:i - 1] if i >= 2 and not odd else None
                if before:
                    n = len(before[1]["turns"])
                    late = [k for k in (n - 2, n - 1) if n > 2 or k]
                if i + 1 < len(waves):
                    scores(waves[i + 1])
                if w:
                    w["s"], w["at"] = s[:, (i - 1) % S_BUFS], turned
                    pe.wait_ge(sem["pn_ready"], steps_done + i)
                    turn(w, 0)
                if before:
                    values(before, late[0])
                if w:
                    turn(w, 1)
                if before and len(late) > 1:
                    values(before, late[1])
                if w:
                    pair = waves[i - 2:i]
                    for k in range(2, len(w["turns"])):
                        if odd:
                            values(pair, k - 2)
                        turn(w, k)
                    if odd and len(w["turns"]) == 2:
                        values(pair, 0)
            steps_done += len(waves)
            pe.wait_ge(sem["sc_free"], banks)
            pe.wait_ge(sem["t_copied"], turned)

        def feed_forward(squared):
            nonlocal xs
            norm = {(1 if squared else 0): lambda: sum_features(KD)}
            spread(xhi, xlo, between=norm if squared else None)
            xs += KD
            stationary(xhi, xlo, KD, 1, between=None if squared else norm)
            stationary_loop(xhi, xlo, (U_FFN_UP - 4) // 4)
            up = t
            stationary(fhi, flo, KF_, 1, fresh=KF_, late=KF_ - 4)
            xs += KF_
            for _ in range(KD - 1):
                stationary(fhi, flo, KF_, 1)
            return up

        pe.wait_ge(sem["in_const"], 16)
        spread(xhi, xlo)
        xs += KD
        stationary(xhi, xlo, KD, 1, between={0: lambda: sum_features(KD)})
        stationary_loop(xhi, xlo, 2)
        pe.wait_ge(sem["in_rel"], 16)
        pe.wait_ge(sem["in_bk"], 16)
        for n0, n1 in ((0, S), (S, TW)):
            open_tile(t)
            nc.tensor.matmul(bank(t, n1 - n0, NH), relv[0:BUCKETS + 1, 0:NH], bk[0:BUCKETS + 1, n0:n1],
                             start=True, stop=True).then_inc(sem["acc_ready"], 1)
            t += 1

        stationary_loop(xhi, xlo, 2)
        stationary(xhi, xlo, KD, 2, between={0: lambda: sum_features(3), 1: lambda: sum_features(2)})
        stationary_loop(xhi, xlo, 3)
        xs += KC_
        mark["q"] = t
        stationary(lathi[:, 0:3, :], latlo[:, 0:3, :], 3, HA, fresh=3)
        xs += 3
        stationary(lathi[:, 3:5, :], latlo[:, 3:5, :], 2, 4, fresh=2)
        xs += 2
        moving(lathi[:, 3:5, :], latlo[:, 3:5, :], 2, HA * VD)
        stationary(yhi, ylo, KC_, KD)
        pe.wait_ge(sem["qkv_ready"], 2)
        attention(list(latent_waves()), s_a, pt_a)
        pe.wait_ge(sem["x_ready"], xs + HA // 2)
        xs += HA // 2
        stationary(yhi, ylo, KC_, KD)
        pe.wait_ge(sem["x_ready"], xs + KD)
        xs += KD
        stationary(xhi, xlo, KD, 3)
        sum_features(KD, MEM)
        sum_tokens(MEM // P)
        stationary(xhi, xlo, KD, KD - 3)
        memory(0, lambda: sum_features(KD))
        mark["up0"] = feed_forward(False)
        mark["down0"] = t
        pe.wait_ge(sem["x_ready"], xs + 2)
        xs += 2
        stationary(p_hi, p_lo, 2, KD, between={1: lambda: sum_features(KD)})
        mark["ple"] = t
        spread(xhi, xlo)
        xs += KD
        stationary(xhi, xlo, KD, 5)

        memory(1, lambda: sum_features(KD))
        spread(xhi, xlo)
        xs += KD
        stationary(xhi, xlo, KD, 1, between={0: lambda: sum_features(KD)})
        sum_tokens()
        stationary(xhi, xlo, KD, 7)
        pe.wait_ge(sem["lr_ready"], 1)
        pe.wait_ge(sem["in_wg"], 16)
        for i in range(TT):
            open_tile(t)
            nc.tensor.matmul(bank(t, GH * GDK), lr[0:GR, i * P:(i + 1) * P], wg[0:GR, :],
                             start=True, stop=True).then_inc(sem["acc_ready"], 1)
            t += 1
        pe.wait_ge(sem["in_sums"], 16)
        halves = 0
        for lv in range(1, N_SUMS + 1):
            if lv <= N_MASKS:
                for hd in range(GH):
                    open_tile(t)
                    if lv > 1:
                        pe.wait_ge(sem["g_ready"], GH * (lv - 2) + hd + 1)
                    a, b = (kg, qg) if lv == 1 else (f[(lv - 1) % 2], f[(lv - 1) % 2])
                    for i in range(TT):
                        w = slice(i * P, (i + 1) * P)
                        m = nc.tensor.matmul(acc[:, t % 4, w], a[0:GDK, hd, w], b[0:GDK, hd, w],
                                             start=True, stop=True)
                    m.then_inc(sem["acc_ready"], 1)
                    t += 1
                mark["pairs", lv - 1] = t
            if lv == 1:
                for _ in range(2):
                    half_moving(halves % 2)
                    halves += 1
                pe.wait_ge(sem["rs_ready"], bc)
                pe.wait_ge(sem["la_ready"], 1)
            for hd in range(GH):
                if e_done >= 4:
                    pe.wait_ge(sem["e_free"], e_done - 3)
                if e_done < 4:
                    pe.wait_ge(sem["o_free"], pairs_done)
                    pe.wait_ge(sem["t_copied"], turned)
                for i in range(TT):
                    m = nc.tensor.matmul(ebank[hd][0:GDK, i * P:(i + 1) * P],
                                         la[:, i, hd * GDK:(hd + 1) * GDK], dm[:, lv - 1, :],
                                         start=True, stop=True)
                m.then_inc(sem["e_ready"], 1)
                e_done += 1
            for _ in range(2 if lv == 1 else 1):
                half_moving(halves % 2)
                halves += 1
        pe.wait_ge(sem["g_ready"], GH * N_SUMS)
        for i in range(TT):
            open_tile(t)
            for hd in range(GH):
                m = nc.tensor.transpose(acc[:, t % 4, hd * GDK:(hd + 1) * GDK],
                                        kg[0:GDK, hd, i * P:(i + 1) * P], ident[0:GDK, 0:GDK])
            m.then_inc(sem["acc_ready"], 1)
            t += 1
        pe.wait_ge(sem["kout_ready"], TT)
        for i in range(TT):
            for hd in range(GH):
                vcols = slice(hd * GDV, (hd + 1) * GDV)
                w = slice(i * P, (i + 1) * P)
                open_tile(t)
                m = nc.tensor.matmul(bank(t, GDV), at_[:, hd, w], vg[:, i, vcols], start=True, stop=i == 0)
                if i:
                    pe.wait_ge(sem["st_ready"], GH * (i - 1) + hd + 1)
                    m = nc.tensor.matmul(bank(t, GDV), qg[0:GDK, hd, w], st[0:GDK, hd, :], start=False,
                                         stop=True)
                m.then_inc(sem["acc_ready"], 1)
                t += 1
                if i < TT - 1:
                    open_tile(t)
                    nc.tensor.matmul(bank(t, GDV, GDK), kout[:, i, hd * GDK:(hd + 1) * GDK], vg[:, i, vcols],
                                     start=True, stop=True).then_inc(sem["acc_ready"], 1)
                    t += 1
        mark["og"] = t
        for i in range(TT):
            pe.wait_ge(sem["og_ready"], i + 1)
            for first, last in ((0, 4), (4, 6)):
                open_tile(t)
                for c in range(first, last):
                    m = nc.tensor.transpose(acc[:, t % 4, (c - first) * P:(c - first + 1) * P],
                                            o_g[:, i, c * P:(c + 1) * P], ident)
                m.then_inc(sem["acc_ready"], 1)
                t += 1
        turned_in = xs + 2 * TT
        attention(list(memory_waves(mq1, 0)), s_1, pt_1)
        xs = turned_in + MH // 2
        spread(xhi, xlo, {0: turned_in, 6: xs})
        stationary(xhi, xlo, KD, 5)
        feed_forward(True)

        spread(xhi, xlo, between={5: lambda: sum_features(KD)})
        xs += KD
        stationary(xhi, xlo, KD, 1)
        sum_tokens()
        stationary(xhi, xlo, KD, 4)
        moving(xhi, xlo, KD, NG * NDH)
        moving(xhi, xlo, KD, NG * NDH)
        pe.wait_ge(sem["x_ready"], xs + 2)
        xs += 2
        spread(xhi, xlo)
        xs += KD
        stationary(xhi, xlo, KD, 3)
        for j in range(2):
            stationary(zhi[j], zlo[j], LP, 1, n=NG * NCMP)
        stationary(xhi, xlo, KD, 3)
        pe.wait_ge(sem["gln_ready"], 1)
        open_tile(t)
        for i in range(TT):
            m = nc.tensor.transpose(acc[:, t % 4, i * 3 * NH:(i + 1) * 3 * NH],
                                    tmp[0:3 * NH, i * P:(i + 1) * P], ident[0:3 * NH, 0:3 * NH])
        m.then_inc(sem["acc_ready"], 1)
        t += 1
        pe.wait_ge(sem["hid_ready"], 1)
        open_tile(t)
        nc.tensor.matmul(bank(t, NG * NCMP, NDH), C("w2_0", 0, NDH), hid[:, 0, 0:NG * NCMP], start=True,
                         stop=True).then_inc(sem["acc_ready"], 1)
        t += 1
        pe.wait_ge(sem["hid_ready"], 2)
        open_tile(t)
        for g in range(NG):
            m = nc.tensor.matmul(acc[0:NCMP, t % 4, g * NDH:(g + 1) * NDH], hid[:, 1, g * NCMP:(g + 1) * NCMP],
                                 C("w2_1", 0, NDH), start=True, stop=True)
        m.then_inc(sem["acc_ready"], 1)
        t += 1
        pe.wait_ge(sem["qkv_ready"], 3)
        pe.wait_ge(sem["in_toep"], 16)
        attention(list(branch_waves()) + list(memory_waves(mq2, 1)), s_2, pt_2)
        xs += (NH + MH) // 2
        pe.wait_ge(sem["x_ready"], xs)
        stationary_loop(xhi, xlo, 2)
        feed_forward(True)
        sum_features(KD)
        assert un == N_UNITS, un

    @block.vector
    def _(dve):
        n = Count(dve)
        t = 0
        sqs = 0
        rs = 0
        his = 0
        waves_done = banks = turned = exps = pairs = valued = 0
        V = nc.vector

        def take(p=P, cols_=S):
            i = t if n.loop is None else n.loop[0] * n.loop[2][sem["acc_free"]] + t
            dve.wait_ge(sem["acc_ready"], i + 1)
            return acc[0:p, t % 4, 0:cols_]

        def give(ins):
            nonlocal t
            n.did(ins, sem["acc_free"])
            t += 1

        def did(ins):
            n.did(ins, sem["dve_step"])

        def split(hi, lo, src, gain=None):
            if gain is None:
                did(V.tensor_copy(hi, src))
                n.did(V.tensor_tensor(lo, src, plain(hi), ALU.subtract), sem["x_ready"])
            else:
                did(V.tensor_scalar(hi, src, gain, None, ALU.mult))
                n.did(V.scalar_tensor_tensor(lo, src, gain, plain(hi), ALU.mult, ALU.subtract),
                      sem["x_ready"])

        def add_square(first, cols_=S):
            nonlocal sqs
            dve.wait_ge(sem["sq_ready"], sqs + 1)
            s = sq[:, sqs % 2, 0:cols_]
            if first:
                ins = V.tensor_copy(sqsum[:, 0:cols_], s)
            else:
                dve.wait_ge(sem["ss_added"], sqs)
                ins = V.tensor_tensor(sqsum[:, 0:cols_], sqsum[:, 0:cols_], s, ALU.add)
            n.did(ins, sem["ss_added"], False)
            sqs += 1

        def factor(to):
            nonlocal rs
            dve.wait_ge(sem["rs_ready"], rs + 1)
            did(V.reciprocal(to, to))
            rs += 1

        def stage(gain, before=None, squares=True, late=False):
            for k in range(KD):
                if before:
                    before(k)
                split(xhi[:, k, :], xlo[:, k, :], h[:, k, :], C(gain, k) if gain else None)
                if squares and k:
                    add_square(k == 1)
                if late and k == 0:
                    add_square(False)
            if squares:
                add_square(False)

        def stage_after(y, post, gain, squares=True, meanwhile=None):
            nonlocal his
            for k in range(KD + 1):
                part = (tmp, rstd2)[k % 2][:, :]
                if k < KD:
                    n.did(V.scalar_tensor_tensor(part, y[:, k, :], C(post, k), rstd[:, :], ALU.mult, ALU.mult),
                          sem["dve_step"], False)
                if k:
                    dve.wait_ge(sem["hi_ready"], his + k)
                    high, low, at = plain(xhi[:, k - 1, :]), xlo[:, k - 1, :], h[:, k - 1, :]
                    if gain is None:
                        ins = V.tensor_tensor(low, at, high, ALU.subtract)
                    else:
                        ins = V.scalar_tensor_tensor(low, at, C(gain, k - 1), high, ALU.mult, ALU.subtract)
                    n.did(ins, sem["x_ready"], False)
                if k < KD:
                    dve.wait_ge(sem["dve_step"], n.at(sem["dve_step"]))
                    n.did(V.tensor_tensor(h[:, k, :], h[:, k, :], part, ALU.add), sem["src_ready"], False)
                if squares and k >= 2:
                    add_square(k == 2)
                if k == 0 and meanwhile:
                    meanwhile()
            if squares:
                add_square(False)
            his += KD

        def residual(k):
            ins = V.tensor_tensor(h[:, k, :], h[:, k, :], take(), ALU.add)
            give(ins)
            n.tell(sem["src_ready"])

        def gather_down(y):
            for k in range(KD):
                give(V.tensor_copy(y[:, k, :], take()))
                n.tell(sem["src_ready"])
                if k:
                    add_square(k == 1)
            add_square(False)

        def feed_forward(which):
            factor(rstd[:, :])
            did(V.memset(u[:, :, 0:2], 0.0))
            per = {sem["acc_free"]: 4, sem["u_ready"]: 4, sem["dve_step"]: 8, sem["c_ready"]: 4,
                   sem["x_ready"]: 2}
            c0 = COL[which]
            a0 = ffn_seen[0]
            with dve.Fori(0, KF_ // 2) as i:
                n.enter(i, per)
                for pair in range(2):
                    for half in range(2):
                        j = 2 * pair + half
                        src = take()
                        give(V.tensor_tensor(u[:, half, 2:], src, rstd[:, :], ALU.mult))
                        n.tell(sem["u_ready"])
                    for half in range(2):
                        j = 2 * pair + half
                        w = [col[:, bass.ds(i * 16 + (c0 + 8 * pair + 4 * half + tap), 1)] for tap in range(2)]
                        dve.wait_ge(sem["a_ready"], i * 4 + (a0 * 4 + j + 1))
                        c = sq[:, half, :]
                        did(V.scalar_tensor_tensor(c, u[:, half, 1:S + 1], w[1], c, ALU.mult, ALU.add))
                        n.did(V.scalar_tensor_tensor(c, u[:, half, 0:S], w[0], c, ALU.mult, ALU.add),
                              sem["c_ready"])
                    dve.wait_ge(sem["v_ready"], i * 2 + (a0 * 2 + pair + 1))
                    did(V.tensor_tensor(sq[:, 0, :], sq[:, 0, :], sq[:, 1, :], ALU.mult))
                    fo = (fhi[:, bass.ds(i * 2 + pair, 1), :].rearrange("p a n -> p (a n)"),
                          flo[:, bass.ds(i * 2 + pair, 1), :].rearrange("p a n -> p (a n)"))
                    split(fo[0], fo[1], sq[:, 0, :])
            n.leave(KF_ // 2)
            t_add(4 * (KF_ // 2 - 1))
            ffn_seen[0] += KF_ // 2

        ffn_seen = [0]

        def t_add(k):
            nonlocal t
            t += k

        def softmaxes(waves, s):
            nonlocal waves_done, banks, turned, exps, pairs, valued
            w0 = waves_done
            turn_at = [turned]
            for w in waves:
                turn_at.append(turn_at[-1] + len(w["turns"]))

            def high(i):
                nonlocal banks
                w, b, st_ = waves[i], i % S_BUFS, stat[:, i % S_BUFS]
                if i >= S_BUFS:
                    dve.wait_ge(sem["t_ready"], turn_at[i - S_BUFS + 1])
                for k, x in enumerate(w["items"]):
                    last = k == len(w["items"]) - 1 or w["items"][k + 1]["bank"] != x["bank"]
                    if k == 0 or w["items"][k - 1]["bank"] != x["bank"]:
                        dve.wait_ge(sem["sc_ready"], banks + 1)
                    to, of = s[:, b, x["off"]:x["off"] + x["n"]], acc[:, x["bank"], x["col"]:x["col"] + x["n"]]
                    if x["bias"] is None:
                        n.did(V.tensor_copy(to, of), sem["dve_step"], False)
                        ins = V.tensor_reduce(st_[:, 0, k:k + 1], of, AX, ALU.max)
                    else:
                        ins = V.tensor_tensor_reduce(to, of, x["bias"], 1.0, -3e38, ALU.add, ALU.max,
                                                     st_[:, 0, k:k + 1])
                    n.did(ins, sem["sc_free" if last else "dve_step"], False)
                    banks += last
                dve.wait_ge(sem["sc_free"], banks)
                m = len(w["items"])
                n.did(V.tensor_scalar(st_[:, 1, 0:m], st_[:, 0, 0:m], -w["scale"], None, ALU.mult),
                      sem["s_ready"], False)

            def normal(i):
                nonlocal exps
                w, b, st_ = waves[i], i % S_BUFS, stat[:, i % S_BUFS]
                m = len(w["items"])
                exps += m
                dve.wait_ge(sem["p_ready"], exps)
                r = st_[:, 3, :]
                did(V.reciprocal(r[:, 0:m], st_[:, 2, 0:m]))
                for first, g in w["gates"]:
                    part = r[:, first:first + g.shape[1]]
                    n.did(V.tensor_tensor(part, part, g, ALU.mult), sem["dve_step"], False)
                dve.wait_ge(sem["dve_step"], n.at(sem["dve_step"]))
                if "valid" in w:
                    part = r[:, w["valid"]:w["valid"] + 1]
                    did(V.tensor_tensor(part, part, C("valid"), ALU.mult))
                for k, x in enumerate(w["items"]):
                    p_ = s[:, b, x["off"]:x["off"] + x["n"]]
                    n.did(V.tensor_scalar(p_, p_, r[:, k:k + 1], None, ALU.mult),
                          sem["pn_ready" if k == m - 1 else "dve_step"], False)

            def output(i):
                nonlocal pairs, valued
                w = waves[i]
                if i % 2 == 0:
                    return
                valued += len(w["turns"])
                if not w["closes"]:
                    return
                dve.wait_ge(sem["pv_done"], valued)
                hi, lo, tile, _ = w["dest"]
                of = pvs[pairs % 2]
                did(V.tensor_copy(hi[:, tile, :], of))
                n.did(V.tensor_tensor(lo[:, tile, :], of, plain(hi[:, tile, :]), ALU.subtract),
                      sem["x_ready"])
                n.tell(sem["o_free"])
                pairs += 1

            for i in range(-1, len(waves) + 2):
                if i + 1 < len(waves):
                    high(i + 1)
                if i >= 2:
                    output(i - 2)
                if 0 <= i < len(waves):
                    normal(i)
            waves_done += len(waves)
            turned = turn_at[-1]

        def memory_stage(layer, k):
            split(mem[layer][1][:, k, :], mem[layer][2][:, k, :], mem[layer][0][:, k, :], C(f"nmem{layer}", k))

        def memory_out(layer):
            for k in range(2):
                give(V.tensor_tensor(mkt[layer][:, k, :], take(P, MEM), rstd_m[:, :], ALU.mult))
            for i in range(2):
                give(V.tensor_scalar(mv[layer][:, i, :], take(P, MH * MDH), rstd_mt[:, i:i + 1], None, ALU.mult))

        dve.wait_ge(sem["in_col"], 16)

        def arrived(k):
            if k % 2 == 0:
                dve.wait_ge(in_x[k // 2], 16)

        stage("mix_pre", arrived)
        factor(rstd[:, :])
        def angles():
            dve.wait_ge(sem["in_pos"], 16)
            a0, a1, a2 = ang[r, 0, :], ang[r, 1, :], ang[r, 2, :]
            magic = 1.5 * 2.0 ** 23
            did(V.tensor_copy(a0, pos_i[r, :]))
            did(V.tensor_scalar(a0, a0, C("inv", p=r), None, ALU.mult))
            did(V.tensor_scalar(a1, a0, 1.0 / (2 * np.pi), C("quarter", p=r), ALU.mult, ALU.add))
            did(V.tensor_scalar(a1, a1, magic, None, ALU.add))
            did(V.tensor_scalar(a1, a1, magic, None, ALU.subtract))
            c1 = 6.28125
            c2 = 0.0019350051879882812
            c3 = 2 * np.pi - c1 - c2
            for part in (c1, c2, c3):
                did(V.scalar_tensor_tensor(a2, a1, -part, a0, ALU.mult, ALU.add))
                did(V.tensor_copy(a0, a2))
            did(V.tensor_scalar(a0, a0, C("halfpi", p=r), None, ALU.add))
            n.did(V.tensor_scalar(a0, a0, 3.1415925, -3.1415925, ALU.min, ALU.max), sem["angle_ready"])

        did(V.memset(prod[:, 0:2], 0.0))
        r = slice(NOPE, P)
        for i in range(KC_):
            give(V.tensor_tensor(tmp[:, :], take(), rstd[:, :], ALU.mult))
            give(V.tensor_tensor(prod[:, 2:], take(), rstd[:, :], ALU.mult))
            did(V.tensor_tensor(prod[:, 2:], prod[:, 2:], tmp[:, :], ALU.mult))
            w = [C("conv_a", 3 * i + tap) for tap in range(3)]
            did(V.tensor_scalar(cv[:, :], prod[:, 2:], w[2], None, ALU.mult))
            did(V.scalar_tensor_tensor(cv[:, :], prod[:, 1:S + 1], w[1], cv[:, :], ALU.mult, ALU.add))
            did(V.scalar_tensor_tensor(cv[:, :], prod[:, 0:S], w[0], cv[:, :], ALU.mult, ALU.add))
            give(V.tensor_tensor(tmp[:, :], take(), rstd[:, :], ALU.mult))
            did(V.tensor_tensor(cv[:, :], cv[:, :], tmp[:, :], ALU.mult))
            split(yhi[:, i, :], ylo[:, i, :], cv[:, :])
            if i == 1:
                angles()
        for n0, n1 in ((0, S), (S, TW)):
            give(V.tensor_copy(vr[0:NH, n0:n1], take(NH, n1 - n0)))
        n.tell(sem["vr_ready"])
        dve.wait_ge(sem["sine_ready"], 1)
        did(V.tensor_scalar(cs[r, :], cs[r, :], C("sign", p=r), None, ALU.mult))
        for i in range(5):
            give(V.tensor_tensor(lat[:, i, :], take(), rstd[:, :], ALU.mult))
            n.tell(sem["src_ready"])
        give(V.tensor_tensor(kpe[r, :], take()[r, :], rstd[r, :], ALU.mult))
        did(V.tensor_tensor(kpe[r, :], kpe[r, :], cs[r, :], ALU.mult))

        def gate(i):
            give(V.tensor_tensor(sg[:, i, :], take(), rstd[:, :], ALU.mult))
            n.tell(sem["gate_in"])

        for k in range(3):
            add_square(k == 0)
        for i in range(2):
            gate(i)
        dve.wait_ge(sem["rs_ready"], rs + 1)
        for k in range(2):
            add_square(k == 0)
        for i in range(2, 4):
            gate(i)
        dve.wait_ge(sem["dist_out"], 16)
        for first, count, gain, root in ((0, 3, "q_lat", rstd2), (3, 2, "kv_lat", rstd3)):
            factor(root[:, :])
            for k in range(count):
                did(V.scalar_tensor_tensor(lat[:, first + k, :], lat[:, first + k, :], C(gain, k),
                                           root[:, :], ALU.mult, ALU.mult))
                split(lathi[:, first + k, :], latlo[:, first + k, :], lat[:, first + k, :])
        for i in range(4, 16):
            gate(i)
        rot, swapped = slice(NOPE, QK), slice(QK, P)
        did(V.tensor_copy(tmp[rot, :], kpe[swapped, :]))
        did(V.tensor_tensor(kpe[rot, :], kpe[rot, :], tmp[rot, :], ALU.add))
        n.tell(sem["kpe_ready"])
        for i in range(HA):
            a = take()
            n.did(V.tensor_tensor(qf[rot, i, :], a[rot, :], cs[rot, :], ALU.mult), sem["dve_step"], False)
            dve.wait_ge(sem["q_copied"], i + 1)
            ins = V.tensor_tensor(tmp[rot, :], a[swapped, :], cs[swapped, :], ALU.mult)
            give(ins)
            did(V.tensor_tensor(qf[rot, i, :], qf[rot, i, :], tmp[rot, :], ALU.add))
        for i in range(4):
            a = take()
            n.did(V.tensor_copy(kf[0:NOPE, 2 * i, :], a[0:NOPE, :]), sem["dve_step"], False)
            dve.wait_ge(sem["q_copied"], HA + i + 1)
            give(V.tensor_copy(kf[0:NOPE, 2 * i + 1, 0:P], a[NOPE:P, 0:P]))
        for i in range(TT):
            give(V.tensor_copy(va[:, i, :], take()))
        n.tell(sem["qkv_ready"])
        for i in range(KD):
            dve.wait_ge(sem["sig_ready"], i + 1)
            give(V.tensor_tensor(sg[:, i, :], sg[:, i, :], take(), ALU.mult))
        dve.wait_ge(sem["in_chunk"], 16)
        softmaxes(list(latent_waves()), s_a)
        for i in range(KD):
            dve.wait_ge(sem["sig_ready"], KD + i + 1)
            give(V.tensor_tensor(tmp[:, :], sg[:, KD + i, :], take(), ALU.mult))
            did(V.tensor_tensor(tmp[:, :], tmp[:, :], sg[:, i, :], ALU.add))
            split(xhi[:, i, :], xlo[:, i, :], tmp[:, :])
        dve.wait_ge(sem["in_mem0"], 16)
        for k in range(KD):
            memory_stage(0, k)
            add_square(k == 0, MEM)
        factor(rstd_m[:, :])
        factor(rstd_mt[:, :])
        gather_down(y_o)
        factor(rstd[:, :])
        stage_after(y_o, "mix_post", "ffn_pre", meanwhile=lambda: memory_out(0))
        feed_forward("ffn0")
        dve.wait_ge(sem["in_p"], 16)
        for k in range(2):
            split(p_hi[:, k, :], p_lo[:, k, :], p_f[:, k, :])
        gather_down(y_d)
        for k in range(KD):
            if k == 2:
                factor(rstd[:, :])
            dve.wait_ge(sem["e_copied"], k + 1)
            n.tell(sem["acc_free"])
        t_add(KD)
        stage_after(y_d, "ffn_post", None, squares=False)
        dve.wait_ge(sem["in_mem1"], 16)
        for k in range(KD):
            dve.wait_ge(sem["ple_sig"], k + 1)
            take()
            give(V.tensor_tensor(e[:, k, :], e[:, k, :], gs[:, k % 2, :], ALU.mult))
            n.tell(sem["src_ready"])
            memory_stage(1, k)
            if k:
                add_square(k == 1)
        add_square(False)
        factor(rstd[:, :])
        stage_after(e, "ple_post", "nmix0", meanwhile=lambda: memory_out(1))

        factor(rstd[:, :])
        give(V.tensor_tensor(lr[0:GR, :], take(GR), rstd[0:GR, :], ALU.mult))
        n.tell(sem["lr_ready"])
        for i in range(GH):
            give(V.scalar_tensor_tensor(qg[0:GDK, i, :], take(GDK), GDK ** -0.5, rstd[0:GDK, :],
                                        ALU.mult, ALU.mult))
        for i in range(GH):
            give(V.tensor_tensor(kg[0:GDK, i, :], take(GDK), rstd[0:GDK, :], ALU.mult))
        for i in range(2):
            give(V.scalar_tensor_tensor(mq1[:, i, :], take(), MDH ** -0.5, rstd[:, :], ALU.mult, ALU.mult))
        factor(rstd_t[:, :])
        for i in range(TT):
            give(V.tensor_tensor(xg[:, i, :], take(P, GH * GDK), row[:, 0:GH * GDK], ALU.add))
        n.tell(sem["gl_raw"])
        halves = 0

        def take_half():
            nonlocal halves
            to = vg if halves < 6 else gg
            c = halves // 2 % 3 * 256
            for i in range(halves % 2 * 2, halves % 2 * 2 + 2):
                give(V.tensor_scalar(to[:, i, c:c + 256], take(P, 256), rstd_t[:, i:i + 1], None, ALU.mult))
            halves += 1

        dve.wait_ge(sem["in_masks"], 16)
        for lv in range(1, N_SUMS + 1):
            fb = f[lv % 2]
            if lv <= N_MASKS:
                mask = mk[:, lv - 1:lv, :].to_broadcast([P, TT, P])
                for hd in range(GH):
                    a = take().rearrange("p (a b) -> p a b", b=P)
                    if lv == 1:
                        give(V.tensor_tensor(at_[:, hd, :].rearrange("p (a b) -> p a b", b=P), a, mask, ALU.mult))
                    else:
                        give(V.tensor_tensor(tmp[:, :].rearrange("p (a b) -> p a b", b=P), a, mask, ALU.mult))
                        did(V.tensor_tensor(at_[:, hd, :], at_[:, hd, :], tmp[:, :], ALU.add))
            if lv == 1:
                take_half()
                dve.wait_ge(sem["gl_ln"], 1)
                n.did(V.scalar_tensor_tensor(la[:, :, :].rearrange("p a b -> p (a b)"),
                                             xg[:, :, :].rearrange("p a b -> p (a b)"), 0.0,
                                             glt[:, :, :].rearrange("p a b -> p (a b)"), ALU.min, ALU.subtract),
                      sem["la_ready"])
                take_half()
            for hd in range(GH):
                dve.wait_ge(sem["f_ready"], GH * (lv - 1) + hd + 1)
                if lv <= LEVELS:
                    half = 2 ** (lv - 1)

                    def part(x, late):
                        v = x[0:GDK, hd, :].rearrange("p (n b) -> p n b", b=2 * half)
                        return v[:, :, half:2 * half] if late else v[:, :, 0:half]
                    n.did(V.tensor_tensor(part(fb, True), part(fb, True), part(qg, True), ALU.mult),
                          sem["dve_step"], False)
                    n.did(V.tensor_tensor(part(fb, False), part(fb, False), part(kg, False), ALU.mult),
                          sem["g_ready"], False)
                elif lv == LEVELS + 1:
                    n.did(V.tensor_copy(decay[0:GDK, TT * hd:TT * hd + TT], fb[0:GDK, hd, P - 1:S:P]),
                          sem["dve_step"], False)
                    n.did(V.tensor_tensor(qg[0:GDK, hd, :], qg[0:GDK, hd, :], fb[0:GDK, hd, :], ALU.mult),
                          sem["g_ready"], False)
                else:
                    n.did(V.tensor_tensor(kg[0:GDK, hd, :], kg[0:GDK, hd, :], fb[0:GDK, hd, :], ALU.mult),
                          sem["g_ready"], False)
            for _ in range(2 if lv == 1 else 1):
                take_half()
        n.tell(sem["gates_raw"])
        for i in range(TT):
            give(V.tensor_copy(kout[:, i, :], take(P, GH * GDK)))
            n.tell(sem["kout_ready"])
        def og_norm(i):
            dve.wait_ge(sem["oroot_ready"], i + 1)
            ro = oroot[:, GH * i:GH * (i + 1)]
            did(V.reciprocal(ro, ro))
            for hd in range(GH):
                vcols = slice(hd * GDV, (hd + 1) * GDV)
                n.did(V.scalar_tensor_tensor(o_g[:, i, vcols], o_g[:, i, vcols], ro[:, hd:hd + 1],
                                             gg[:, i, vcols], ALU.mult, ALU.mult),
                      sem["og_ready" if hd == GH - 1 else "dve_step"], False)

        for i in range(TT):
            for hd in range(GH):
                vcols = slice(hd * GDV, (hd + 1) * GDV)
                give(V.tensor_copy(o_g[:, i, vcols], take(P, GDV)))
                n.tell(sem["o_raw"])
                if i < TT - 1:
                    a = take(GDK, GDV)
                    if i == 0:
                        give(V.tensor_copy(st[0:GDK, hd, :], a))
                    else:
                        give(V.scalar_tensor_tensor(st[0:GDK, hd, :], st[0:GDK, hd, :],
                                                    decay[0:GDK, TT * hd + i:TT * hd + i + 1], a, ALU.mult, ALU.add))
                    n.tell(sem["st_ready"])
            if i:
                og_norm(i - 1)
            if i == 0:
                dve.wait_ge(sem["gates_ready"], 1)
            for to in ([0, 1], [2], [3], [])[i]:
                gates = gg[:, to, :].rearrange("p (h d) -> p h d", d=GDV)
                n.did(V.tensor_tensor(gates, gates, row[:, ROW["onorm"]:ROW["onorm"] + GDV].unsqueeze(1)
                                      .to_broadcast([P, GH, GDV]), ALU.mult), sem["dve_step"], False)
        def og_out(i):
            nonlocal his
            for first, last in ((0, 4), (4, 6)):
                a = take(P, (last - first) * P).rearrange("p (c n) -> p c n", n=P)
                to = slice(i * P, (i + 1) * P)
                dve.wait_ge(sem["hi_ready"], his + 1)
                his += 1
                ins = V.tensor_tensor(xlo[:, first:last, to], a, plain(xhi[:, first:last, to]), ALU.subtract)
                give(ins)
                n.tell(sem["x_ready"])

        og_norm(TT - 1)
        for i in range(TT - 1):
            og_out(i)
        og_out(TT - 1)
        softmaxes(list(memory_waves(mq1, 0)), s_1)
        for k in range(KD):
            residual(k)
            if k:
                add_square(k == 1)
        stage("nffn1", squares=False, late=True)
        feed_forward("ffn1")
        stage("nkv", residual)

        factor(rstd[:, :])
        for j in range(2):
            for k in range(2):
                a = take()
                for g in range(2):
                    rr = slice(g * NDH, (g + 1) * NDH)
                    did(V.tensor_tensor(z[0:NDH, 2 * k + g, :], a[rr, :], rstd[rr, :], ALU.mult))
                    ins = V.tensor_tensor(z[NDH:P, 2 * k + g, 0:S - 1], a[rr, 1:], rstd[rr, 1:], ALU.mult)
                    if g == 0:
                        did(ins)
                    else:
                        give(ins)
            for part in range(2):
                l0, t0 = part * LP // 2, part * CMP_S
                win = z[:, :, t0:t0 + CMP_S * NCMP].rearrange("p g (c l) -> p l g c", l=CMP_S)[:, 0:CMP_S:2]
                did(V.tensor_tensor(zw[:, l0:l0 + LP // 2, :].rearrange("p l (g c) -> p l g c", g=NG), win,
                                    C(f"pos{j}", l0, LP // 2).unsqueeze(2).unsqueeze(3)
                                    .to_broadcast([P, LP // 2, NG, NCMP]), ALU.add))
            flat = "p a b -> p (a b)"
            split(zhi[j][:, :, :].rearrange(flat), zlo[j][:, :, :].rearrange(flat), zw[:, :, :].rearrange(flat))
        n.tell(sem["z_done"])
        for j in range(2):
            for k in range(2):
                give(V.tensor_tensor(kn[j][:, k, :], take(), rstd[:, :], ALU.mult))
        factor(rstd_t[:, :])
        for j in range(2):
            for i in range(TT):
                give(V.tensor_scalar(vn[j][:, i, :], take(P, NG * NDH), rstd_t[:, i:i + 1], None, ALU.mult))
        nw = NG * NCMP
        stage("nmix1", squares=False)
        for i in range(6):
            give(V.scalar_tensor_tensor(qn[:, i, :], take(), NDH ** -0.5, rstd[:, :], ALU.mult, ALU.mult))
        for j in range(2):
            give(V.tensor_scalar(hid[:, j, 0:nw], take(P, nw), C("cb1", j), None, ALU.add))
            n.tell(sem["hid_raw"])
        for i in range(2):
            give(V.scalar_tensor_tensor(mq2[:, i, :], take(), MDH ** -0.5, rstd[:, :], ALU.mult, ALU.mult))
        give(V.tensor_tensor(tmp[0:3 * NH, :], take(3 * NH), rstd[0:3 * NH, :], ALU.mult))
        n.tell(sem["gln_ready"])
        give(V.tensor_copy(gt[:, :, :].rearrange("p a b -> p (a b)"), take(P, TT * 3 * NH)))
        n.tell(sem["gates_raw"])
        a = take(NDH, nw)
        for g in range(NG):
            rr = slice(g % 2 * NDH, g % 2 * NDH + NDH)
            ins = V.tensor_scalar(kc[rr, g // 2, 0:NCMP], a[:, g * NCMP:(g + 1) * NCMP],
                                  C("cb2", p=slice(0, NDH)), None, ALU.add)
            if g < NG - 1:
                did(ins)
            else:
                give(ins)
        did(V.memset(vc[:, :], 0.0))
        a = take(NCMP, NG * NDH)
        give(V.tensor_tensor(vc[0:NCMP, :].rearrange("p (g d) -> p g d", d=NDH),
                             a.rearrange("p (g d) -> p g d", d=NDH),
                             row[0:NCMP, ROW["cb2r"]:ROW["cb2r"] + NDH].unsqueeze(1)
                             .to_broadcast([NCMP, NG, NDH]), ALU.add))
        dve.wait_ge(sem["gates_ready"], 2)
        did(V.memset(s_2[:, :, S_CMP:SW], 0.0))
        dve.wait_ge(sem["in_toep"], 16)
        n.tell(sem["qkv_ready"])
        softmaxes(list(branch_waves()) + list(memory_waves(mq2, 1)), s_2)
        for k in range(KD):
            residual(k)
            if k:
                add_square(k == 1)
        stage("nffn2", squares=False, late=True)
        feed_forward("ffn2")
        for k in range(KD):
            residual(k)
            if k:
                add_square(k == 1)
        add_square(False)
        factor(rstd[:, :])
        for k in range(KD):
            n.did(V.scalar_tensor_tensor(h[:, k, :], h[:, k, :], C("final", k), rstd[:, :], ALU.mult,
                                         ALU.mult), sem["out_ready"])

    @block.scalar
    def _(act):
        n = Count(act)
        src = 0
        sqs = 0
        bc = 0
        waves_done = turned = valued = 0
        fed = 0
        A = nc.scalar

        def load(to, what, name):
            act.dma_start(to, what).then_inc(sem[name], 16)

        def did(ins):
            n.did(ins, sem["act_step"])

        def warm(func):
            did(A.activation(spare[:, :], C("eps"), func))

        def square(what):
            nonlocal sqs
            if sqs >= 2:
                act.wait_ge(sem["ss_added"], sqs - 1)
            n.did(A.activation(sq[:, sqs % 2, 0:what.shape[-1]], what, ACT.Square), sem["sq_ready"])
            sqs += 1

        def highs(gain, then_square=True):
            nonlocal src
            for k in range(KD):
                act.wait_ge(sem["src_ready"], src + 1)
                src += 1
                if gain is None:
                    ins = A.activation(xhi[:, k, :], h[:, k, :], ACT.Copy)
                else:
                    ins = A.activation(xhi[:, k, :], h[:, k, :], ACT.Identity, scale=C(gain, k))
                n.did(ins, sem["hi_ready"], False)
                if then_square:
                    square(h[:, k, :])

        def squares(tiles, arrived=None):
            nonlocal src
            for i, what in enumerate(tiles):
                if arrived:
                    arrived(i)
                else:
                    act.wait_ge(sem["src_ready"], src + 1)
                    src += 1
                square(what)

        def root(to, count):
            nonlocal bc
            warm(ACT.Sqrt)
            act.wait_ge(sem["bc_ready"], bc + 1)
            n.did(A.activation(to, pv[:, 0:to.shape[-1]], ACT.Sqrt, scale=1.0 / count, bias=C("eps")),
                  sem["rs_ready"])
            bc += 1

        def feed_forward(which, func):
            nonlocal fed
            c0 = COL[which]
            warm(func)
            per = {sem["a_ready"]: 4, sem["v_ready"]: 2}
            with act.Fori(0, KF_ // 2) as i:
                n.enter(i, per)
                for pair in range(2):
                    for half in range(2):
                        j = 2 * pair + half
                        w2, b = (col[:, bass.ds(i * 16 + (c0 + 8 * pair + 4 * half + x), 1)] for x in (2, 3))
                        act.wait_ge(sem["u_ready"], i * 4 + (4 * fed + j + 1))
                        n.did(A.activation(sq[:, half, :], u[:, half, 2:], ACT.Identity, scale=w2, bias=b),
                              sem["a_ready"])
                    act.wait_ge(sem["c_ready"], i * 4 + (4 * fed + 2 * pair + 1))
                    n.did(A.activation(sq[:, 0, :], sq[:, 0, :], func), sem["v_ready"])
            n.leave(KF_ // 2)
            fed += KF_ // 2

        def softmaxes(waves, s, pts):
            nonlocal waves_done, turned, valued
            warm(ACT.Exp)
            for i in range(len(waves) + 1):
                items = waves[i]["items"] if i < len(waves) else []
                turns = waves[i - 1]["turns"] if i else []
                if i >= 3 and i % 2:
                    valued += len(waves[i - 2]["turns"])
                if items:
                    act.wait_ge(sem["s_ready"], waves_done + i + 1)
                for k, x in enumerate(items):
                    st_ = stat[:, i % S_BUFS]
                    p_ = s[:, i % S_BUFS, x["off"]:x["off"] + x["n"]]
                    n.did(A.activation(p_, p_, ACT.Exp, scale=waves[i]["scale"], bias=st_[:, 1, k:k + 1],
                                       accum_out=st_[:, 2, k:k + 1]), sem["p_ready"], False)
                for k, x in enumerate(turns):
                    act.wait_ge(sem["t_ready"], turned + 1)
                    m, (c0, c1) = len(x["src"]) * P, place(waves[i - 1], k)
                    if i >= 3:
                        before = waves[(i - 1) // 2 * 2 - 1]
                        if last_on(waves[i - 1], k, before):
                            act.wait_ge(sem["pv_done"], valued - len(before["turns"])
                                        + last_on(waves[i - 1], k, before))
                    n.did(A.activation(pts[0:x["width"], (i - 1) % 2, c0:c1],
                                       sc[0:x["width"], turned % 2, 0:m], ACT.Copy), sem["t_copied"], False)
                    turned += 1
            waves_done += len(waves)
            valued += len(waves[-1]["turns"])

        def tiles(x, count=KD):
            return [x[:, k, :] for k in range(count)]

        load(relv[0:BUCKETS + 1, 0:NH], rel, "in_rel")
        load(bk[0:BUCKETS + 1, :], buckets, "in_bk")
        load(col[:, :], cols, "in_col")
        load(const[:, :], consts, "in_const")
        load(row[:, :], rws, "in_row")
        load(pos_i[NOPE:P, :], positions, "in_pos")
        load(chunkm[:, :], chunk, "in_chunk")
        act.wait_ge(sem["in_col"], 16)
        squares(tiles(h), lambda k: act.wait_ge(in_x[k // 2], 16))
        root(rstd[:, :], D)
        act.wait_ge(sem["angle_ready"], 1)
        n.did(A.activation(cs[NOPE:P, :], ang[NOPE:P, 0, :], ACT.Sin), sem["sine_ready"])
        act.wait_ge(sem["vr_ready"], 1)
        act.dma_start(distances.rearrange("h (r n) -> h r n", n=TW),
                      vr[0:NH, :].unsqueeze(1).to_broadcast([NH, P, TW])).then_inc(sem["dist_out"], 16)
        squares([lat[:, k, :] for k in range(3)])
        root(rstd2[:, :], Q_LORA)
        squares([lat[:, k, :] for k in range(3, 5)])
        root(rstd3[:, :], KV_LORA)
        warm(ACT.Sigmoid)
        for i in range(2 * KD):
            act.wait_ge(sem["gate_in"], i + 1)
            n.did(A.activation(sg[:, i, :], sg[:, i, :], ACT.Sigmoid), sem["sig_ready"])
        act.wait_ge(sem["kpe_ready"], 1)
        for i in range(HA):
            did(A.activation(kf[NOPE:QK, i, :], kpe[NOPE:QK, :], ACT.Copy))
        for i in range(HA):
            tile = mark["q"] + i
            act.wait_ge(sem["acc_ready"], tile + 1)
            n.did(A.activation(qf[0:NOPE, i, :], acc[0:NOPE, tile % 4, :], ACT.Copy), sem["q_copied"], False)
        for i in range(4):
            tile = mark["q"] + HA + i
            act.wait_ge(sem["acc_ready"], tile + 1)
            n.did(A.activation(kf[0:NOPE, 2 * i + 1, P:], acc[NOPE:P, tile % 4, P:], ACT.Copy),
                  sem["q_copied"], False)
        act.wait_ge(sem["q_copied"], HA + 4)
        n.tell(sem["qkv_ready"])
        softmaxes(list(latent_waves()), s_a, pt_a)
        act.wait_ge(sem["pv_done"], valued)
        load(mem[0][0][:, :, :], mem_t, "in_mem0")
        squares(tiles(mem[0][0]), lambda k: act.wait_ge(sem["in_mem0"], 16))
        root(rstd_m[:, :], D)
        root(rstd_mt[:, :], D)
        squares(tiles(y_o))
        root(rstd[:, :], D)
        highs("ffn_pre")
        root(rstd[:, :], D)
        feed_forward("ffn0", ACT.Gelu_apprx_tanh)
        act.wait_ge(sem["acc_ready"], mark["up0"])
        load(p_f[:, :, :], p_t, "in_p")
        squares(tiles(y_d))
        act.wait_ge(sem["acc_ready"], mark["down0"])
        load(mem[1][0][:, :, :], mem_t, "in_mem1")
        load(dm[:, :, :], sums, "in_sums")
        load(mk[:, :, :], masks, "in_masks")
        load(wg[0:GR, :], wgate, "in_wg")
        warm(ACT.Sqrt)
        for k in range(KD):
            if k == 2:
                root(rstd[:, :], D)
            tile = mark["down0"] + k
            act.wait_ge(sem["acc_ready"], tile + 1)
            n.did(A.activation(e[:, k, :], acc[:, tile % 4, :], ACT.Copy), sem["e_copied"], False)
        highs(None, False)
        warm(ACT.Sigmoid)
        for k in range(KD + 1):
            if k < KD:
                tile = mark["ple"] + k
                act.wait_ge(sem["acc_ready"], tile + 1)
                if k >= 2:
                    act.wait_ge(sem["acc_free"], tile - 1)
                n.did(A.activation(gs[:, k % 2, :], acc[:, tile % 4, :], ACT.Sigmoid), sem["ple_sig"])
            if k:
                squares([e[:, k - 1, :]])
        root(rstd[:, :], D)
        highs("nmix0")
        root(rstd[:, :], D)
        root(rstd_t[:, :], D)

        act.wait_ge(sem["gl_raw"], 1)
        flat = "p a b -> p (a b)"
        did(A.activation(glt[:, :, :].rearrange(flat), xg[:, :, :].rearrange(flat), ACT.Abs))
        did(A.activation(glt[:, :, :].rearrange(flat), glt[:, :, :].rearrange(flat), ACT.Exp, scale=-1.0))
        n.did(A.activation(glt[:, :, :].rearrange(flat), glt[:, :, :].rearrange(flat), ACT.Ln, bias=1.0),
              sem["gl_ln"])
        for lv in range(1, N_SUMS + 1):
            for hd in range(GH):
                act.wait_ge(sem["e_ready"], GH * (lv - 1) + hd + 1)
                if lv >= 3:
                    act.wait_ge(sem["acc_ready"], mark["pairs", lv - 2])
                n.did(A.activation(f[lv % 2][0:GDK, hd, :], ebank[hd][0:GDK, :], ACT.Exp), sem["f_ready"])
                n.tell(sem["e_free"])
        act.wait_ge(sem["gates_raw"], 1)
        n.did(A.activation(gg[:, :, :].rearrange(flat), gg[:, :, :].rearrange(flat), ACT.Silu),
              sem["gates_ready"])
        for i in range(TT):
            for hd in range(GH):
                act.wait_ge(sem["o_raw"], GH * i + hd + 1)
                did(A.activation(sq[:, 0, 0:GDV], o_g[:, i, hd * GDV:(hd + 1) * GDV], ACT.Square,
                                 accum_out=osum[:, GH * i + hd:GH * i + hd + 1]))
            part = slice(GH * i, GH * (i + 1))
            n.did(A.activation(oroot[:, part], osum[:, part], ACT.Sqrt, scale=1.0 / GDV, bias=C("eps")),
                  sem["oroot_ready"])
        for i in range(TT):
            for first, last in ((0, 4), (4, 6)):
                tile = mark["og"] + 2 * i + first // 4
                act.wait_ge(sem["acc_ready"], tile + 1)
                n.did(A.activation(xhi[:, first:last, i * P:(i + 1) * P],
                                   acc[:, tile % 4, 0:(last - first) * P].rearrange("p (c n) -> p c n", n=P),
                                   ACT.Copy), sem["hi_ready"], False)
        softmaxes(list(memory_waves(mq1, 0)), s_1, pt_1)
        squares(tiles(h))
        root(rstd[:, :], D)
        feed_forward("ffn1", ACT.Silu)
        squares(tiles(h))
        root(rstd[:, :], D)
        root(rstd_t[:, :], D)

        act.wait_ge(sem["z_done"], 1)
        act.wait_ge(sem["dist_out"], 16)
        width = TW - 1
        act.dma_start(toep[:, :, :], distances[:, P - 1:P - 1 + P * width]
                      .rearrange("h (p n) -> p h n", n=width)[:, :, 0:S]).then_inc(sem["in_toep"], 16)
        nw = NG * NCMP
        for j in range(2):
            act.wait_ge(sem["hid_raw"], j + 1)
            n.did(A.activation(hid[:, j, 0:nw], hid[:, j, 0:nw], ACT.Silu), sem["hid_ready"])
        act.wait_ge(sem["gates_raw"], 2)
        n.did(A.activation(gt[:, :, :].rearrange(flat), gt[:, :, :].rearrange(flat), ACT.Sigmoid),
              sem["gates_ready"])
        softmaxes(list(branch_waves()) + list(memory_waves(mq2, 1)), s_2, pt_2)
        squares(tiles(h))
        root(rstd[:, :], D)
        feed_forward("ffn2", ACT.Silu)
        squares(tiles(h))
        root(rstd[:, :], D)

    ctx.close()



def feature_major(x):
    x = np.asarray(x, np.float32)
    return np.ascontiguousarray(x.T.reshape(-1, P, x.shape[0]).transpose(1, 0, 2))


def kernel(**inputs):
    import concourse.bacc as bacc
    from concourse.bass_utils import run_bass_kernel_spmd as run

    a = {k: np.asarray(v) for k, v in inputs.items()}
    sums, masks = decay_tables()
    arrays = {
        "weights": weight_units(a),
        "x_t": feature_major(a["x"][0]),
        "p_t": feature_major(a["p"][0, 0]),
        "mem_t": feature_major(a["mem_2"][0]),
        "cols": columns(a),
        "rws": rows(a),
        "positions": np.ascontiguousarray(np.broadcast_to(a["positions"].astype(np.int32), (NOPE, S))),
        "rel": np.concatenate([a["rel_bias_2"], np.ones((1, NH), np.float32)]),
        "wgate": np.ascontiguousarray(a["gla_w_gate_up_2"][0]),
        "consts": fixed(),
        "chunk": chunk_mask(),
        "buckets": bucket_table(),
        "sums": sums.reshape(P, N_SUMS, P),
        "masks": masks.reshape(P, N_MASKS, P),
    }
    nc = bacc.Bacc("TRN2", target_bir_lowering=False, num_devices=1)
    args = [nc.dram_tensor(f"in_{k}", v.shape, mybir.dt.from_np(v.dtype), kind="ExternalInput").ap()
            for k, v in arrays.items()]
    args.append(nc.dram_tensor("out_t", (P, KD, S), F32, kind="ExternalOutput").ap())
    build_program(nc, *args)
    r = run(nc, [{f"in_{k}": v for k, v in arrays.items()}], core_ids=[0])
    y = r.results[0]["out_t"]
    return np.ascontiguousarray(y.transpose(2, 1, 0).reshape(1, S, D))
```
